# Optimizing a Trainium2 kernel written in Bass

```python
import jax
import jax.numpy as jnp
from jax import lax
import numpy as np

D_MODEL = 1024
BATCH = 1
SEQ = 512
DEPTH = 2

HEAD_DIM = 64
D_MIX = D_MODEL
N_MIX_HEADS = D_MIX // HEAD_DIM
NSA_HEADS = 8
NSA_GROUPS = 2
NSA_HPG = NSA_HEADS // NSA_GROUPS
NSA_WIDTH = NSA_HEADS * HEAD_DIM
NSA_KV_WIDTH = NSA_GROUPS * HEAD_DIM
CMP_BLOCK = 32
CMP_STRIDE = 16
CMP_HIDDEN = 256
SEL_BLOCK = 64
SEL_TOPK = 16
SEL_LOCAL = 2
SEL_Q_BLOCK = 64
WINDOW = 512
WIN_Q_BLOCK = 128
FORCE_BONUS = 1.0e4
LRU_BLOCKS = 4
LRU_WIDTH = LRU_BLOCKS * HEAD_DIM
LRU_BW = LRU_WIDTH // LRU_BLOCKS
CONV_WIDTH = 4
LRU_C = 8.0
ML_HEADS = 4
ML_WIDTH = ML_HEADS * HEAD_DIM
ML_CHUNK = 64
D_FF = 2816
EPS = 1e-6
NEG = -1e30

IN_SPLITS = (NSA_WIDTH,
             NSA_KV_WIDTH, NSA_KV_WIDTH,
             NSA_KV_WIDTH, NSA_KV_WIDTH,
             NSA_KV_WIDTH, NSA_KV_WIDTH,
             NSA_HEADS * 3,
             LRU_WIDTH, LRU_WIDTH,
             ML_WIDTH, ML_WIDTH, ML_WIDTH,
             ML_HEADS, ML_HEADS,
             ML_WIDTH)
D_IN = sum(IN_SPLITS)
IN_SPLIT_POINTS = tuple(int(c) for c in np.cumsum(IN_SPLITS)[:-1])

kernel_name = 'hymba_nsa_rglru_mlstm_macaron'

def rms_norm(x, g):
    xf = x.astype(jnp.float32)
    y = xf * lax.rsqrt(jnp.mean(xf * xf, axis=-1, keepdims=True) + EPS)
    return (y * g.astype(jnp.float32)).astype(x.dtype)

def swiglu(x, w1, w3, w2):
    return (jax.nn.silu(x @ w1) * (x @ w3)) @ w2

def masked_softmax(s, mask):
    s = jnp.where(mask, s.astype(jnp.float32), NEG)
    p = jax.nn.softmax(s, axis=-1)
    return jnp.where(mask, p, 0.0)

def alibi_slopes(n_heads):
    return jnp.asarray(2.0 ** (-8.0 * np.arange(1, n_heads + 1) / n_heads), dtype=jnp.float32)

def compress_blocks(z, blk_idx, pos, w1, w2):
    B = z.shape[0]
    n_cmp = blk_idx.shape[0]
    blocks = jnp.transpose(z[:, blk_idx], (0, 1, 3, 2, 4)) + pos
    flat = blocks.reshape(B, n_cmp, NSA_GROUPS, CMP_BLOCK * HEAD_DIM)
    return jax.nn.silu(flat @ w1) @ w2

def nsa_mixer(q, k_cmp, v_cmp, k_slc, v_slc, k_win, v_win, gate_logits,
              pos_k, w1_k, w2_k, pos_v, w1_v, w2_v):
    B, S = q.shape[0], q.shape[1]
    G, R, dh = NSA_GROUPS, NSA_HPG, HEAD_DIM
    slopes = alibi_slopes(NSA_HEADS).reshape(G, R)
    qg = (q * dh ** -0.5).reshape(B, S, G, R, dh)
    t = jnp.arange(S)

    n_cmp = (S - CMP_BLOCK) // CMP_STRIDE + 1
    cmp_start = np.arange(n_cmp) * CMP_STRIDE
    cmp_end = cmp_start + CMP_BLOCK - 1
    blk_idx = cmp_start[:, None] + np.arange(CMP_BLOCK)[None, :]
    kc = compress_blocks(k_cmp, blk_idx, pos_k, w1_k, w2_k)
    vc = compress_blocks(v_cmp, blk_idx, pos_v, w1_v, w2_v)
    dist_c = t[:, None] - cmp_end[None, :]
    s_c = jnp.einsum('bsgrd,bngd->bgrsn', qg, kc) - slopes[:, :, None, None] * dist_c
    p_c = masked_softmax(s_c, dist_c >= 0)
    o_c = jnp.einsum('bgrsn,bngd->bsgrd', p_c.astype(vc.dtype), vc).reshape(B, S, NSA_HEADS, dh)

    n_slc = S // SEL_BLOCK
    n_sel = min(SEL_TOPK, n_slc)
    slc_start = np.arange(n_slc) * SEL_BLOCK
    overlap = ((cmp_start[:, None] <= slc_start[None, :] + SEL_BLOCK - 1)
               & (cmp_end[:, None] >= slc_start[None, :])).astype(np.float32)
    imp = jnp.einsum('bgrsn,nj->bgsj', p_c, jnp.asarray(overlap))
    cur = t // SEL_BLOCK
    j = jnp.arange(n_slc)
    valid = j[None, :] <= cur[:, None]
    forced = valid & ((j[None, :] == 0) | (j[None, :] > cur[:, None] - SEL_LOCAL))
    score = jnp.where(valid, imp + jnp.where(forced, FORCE_BONUS, 0.0), NEG)
    _, sel_idx = lax.top_k(score, n_sel)

    kb = jnp.transpose(k_slc.reshape(B, n_slc, SEL_BLOCK, G, dh), (0, 3, 1, 2, 4))
    vb = jnp.transpose(v_slc.reshape(B, n_slc, SEL_BLOCK, G, dh), (0, 3, 1, 2, 4))
    nqc = S // SEL_Q_BLOCK
    n_keys = n_sel * SEL_BLOCK
    q_ch = jnp.transpose(qg.reshape(B, nqc, SEL_Q_BLOCK, G, R, dh), (1, 0, 2, 3, 4, 5))
    i_ch = jnp.transpose(sel_idx.reshape(B, G, nqc, SEL_Q_BLOCK, n_sel), (2, 0, 1, 3, 4))
    t_ch = t.reshape(nqc, SEL_Q_BLOCK)
    gather = jax.vmap(jax.vmap(lambda blocks, ids: blocks[ids]))

    def sel_chunk(args):
        qc, ic, tc = args
        kg = gather(kb, ic).reshape(B, G, SEL_Q_BLOCK, n_keys, dh)
        vg = gather(vb, ic).reshape(B, G, SEL_Q_BLOCK, n_keys, dh)
        kpos = (ic[..., None] * SEL_BLOCK + jnp.arange(SEL_BLOCK)).reshape(B, G, SEL_Q_BLOCK, n_keys)
        dist = tc[None, None, :, None] - kpos
        s = jnp.einsum('bqgrd,bgqkd->bgrqk', qc, kg) - slopes[None, :, :, None, None] * dist[:, :, None]
        p = masked_softmax(s, (dist >= 0)[:, :, None])
        return jnp.einsum('bgrqk,bgqkd->bqgrd', p.astype(vg.dtype), vg)

    o_s = lax.map(sel_chunk, (q_ch, i_ch, t_ch))
    o_s = jnp.transpose(o_s, (1, 0, 2, 3, 4, 5)).reshape(B, S, NSA_HEADS, dh)

    nqb = S // WIN_Q_BLOCK
    span = WINDOW + WIN_Q_BLOCK
    win_idx = np.arange(nqb)[:, None] * WIN_Q_BLOCK + np.arange(span)[None, :]
    pad = ((0, 0), (WINDOW, 0), (0, 0), (0, 0))
    kw = jnp.pad(k_win, pad)[:, win_idx]
    vw = jnp.pad(v_win, pad)[:, win_idx]
    kpos_w = win_idx - WINDOW
    dist_w = t.reshape(nqb, WIN_Q_BLOCK)[:, :, None] - kpos_w[:, None, :]
    mask_w = (dist_w >= 0) & (dist_w < WINDOW) & (kpos_w[:, None, :] >= 0)
    qw = qg.reshape(B, nqb, WIN_Q_BLOCK, G, R, dh)
    s_w = jnp.einsum('bcqgrd,bckgd->bgrcqk', qw, kw) - slopes[:, :, None, None, None] * dist_w
    p_w = masked_softmax(s_w, mask_w)
    o_w = jnp.einsum('bgrcqk,bckgd->bcqgrd', p_w.astype(vw.dtype), vw).reshape(B, S, NSA_HEADS, dh)

    g = jax.nn.sigmoid(gate_logits.astype(jnp.float32)).astype(q.dtype)
    return g[..., 0:1] * o_c + g[..., 1:2] * o_s + g[..., 2:3] * o_w

def rglru_mixer(x, gate, conv_w, conv_b, w_a, b_a, w_x, b_x, lam):
    B, S, C = x.shape
    xp = jnp.pad(x, ((0, 0), (CONV_WIDTH - 1, 0), (0, 0)))
    xc = conv_b + xp[:, 0:S] * conv_w[0]
    for tap in range(1, CONV_WIDTH):
        xc = xc + xp[:, tap:tap + S] * conv_w[tap]
    xb = xc.reshape(B, S, LRU_BLOCKS, LRU_BW)
    r = jax.nn.sigmoid(jnp.einsum('bsnc,ncd->bsnd', xb, w_a) + b_a).reshape(B, S, C)
    i = jax.nn.sigmoid(jnp.einsum('bsnc,ncd->bsnd', xb, w_x) + b_x).reshape(B, S, C)
    log_a = -LRU_C * r.astype(jnp.float32) * jax.nn.softplus(-lam.astype(jnp.float32))
    a = jnp.exp(log_a)
    u = jnp.sqrt(-jnp.expm1(2.0 * log_a)) * (i * xc).astype(jnp.float32)

    def combine(left, right):
        a1, b1 = left
        a2, b2 = right
        return a1 * a2, a2 * b1 + b2

    _, h = lax.associative_scan(combine, (a, u), axis=1)
    return h.astype(x.dtype) * jax.nn.gelu(gate)

def mlstm_mixer(q, k, v, i_pre, f_pre, o_pre):
    B, S, NH, dh = q.shape
    L = ML_CHUNK
    NC = S // L
    f32 = jnp.float32

    def to_chunks(z):
        z = z.astype(f32).reshape((B, NC, L) + z.shape[2:])
        return jnp.moveaxis(z, 3, 1)

    qc = to_chunks(q)
    kc = to_chunks(k) * dh ** -0.5
    vc = to_chunks(v)
    ig = to_chunks(i_pre)
    lf = jax.nn.log_sigmoid(to_chunks(f_pre))
    a = jnp.cumsum(lf, axis=-1)
    A = a[..., -1]
    causal = np.tril(np.ones((L, L), dtype=bool))
    D = jnp.where(causal, a[..., :, None] - a[..., None, :] + ig[..., None, :], NEG)
    w_end = A[..., None] - a + ig

    def step(carry, xs):
        C, n, m = carry
        A_c, w_c, k_c, v_c = xs
        m_new = jnp.maximum(A_c + m, jnp.max(w_c, axis=-1))
        decay = jnp.exp(A_c + m - m_new)
        wk = jnp.exp(w_c - m_new[..., None])
        C_new = decay[..., None, None] * C + jnp.einsum('bhs,bhsd,bhse->bhde', wk, k_c, v_c)
        n_new = decay[..., None] * n + jnp.einsum('bhs,bhsd->bhd', wk, k_c)
        return (C_new, n_new, m_new), (C, n, m)

    init = (jnp.zeros((B, NH, dh, dh), f32), jnp.zeros((B, NH, dh), f32), jnp.zeros((B, NH), f32))
    xs = (jnp.moveaxis(A, 2, 0), jnp.moveaxis(w_end, 2, 0), jnp.moveaxis(kc, 2, 0), jnp.moveaxis(vc, 2, 0))
    _, (C_prev, n_prev, m_prev) = lax.scan(step, init, xs)
    C_prev = jnp.moveaxis(C_prev, 0, 2)
    n_prev = jnp.moveaxis(n_prev, 0, 2)
    m_prev = jnp.moveaxis(m_prev, 0, 2)

    m_inter = a + m_prev[..., None]
    m = jnp.maximum(m_inter, jnp.max(D, axis=-1))
    inter = jnp.exp(m_inter - m)
    W = jnp.exp(D - m[..., None]) * jnp.einsum('bhcjd,bhcsd->bhcjs', qc, kc)
    num = inter[..., None] * jnp.einsum('bhcjd,bhcde->bhcje', qc, C_prev) + jnp.einsum('bhcjs,bhcse->bhcje', W, vc)
    den = inter * jnp.einsum('bhcjd,bhcd->bhcj', qc, n_prev) + jnp.sum(W, axis=-1)
    h = num / jnp.maximum(jnp.abs(den), jnp.exp(-m))[..., None]
    h = jnp.moveaxis(h, 1, 3).reshape(B, S, NH * dh)
    return (jax.nn.sigmoid(o_pre.astype(f32)) * h).astype(q.dtype)

def setup_inputs(seed: int = 0) -> dict:
    key = jax.random.key(seed)
    ks = jax.random.split(key, 32)

    def nrm(i, shape, scale):
        return jax.random.normal(ks[i], shape, jnp.float32) * scale

    def gain(i, shape):
        return 1.0 + 0.01 * jax.random.normal(ks[i], shape, jnp.float32)

    a0 = jax.random.uniform(ks[19], (DEPTH, LRU_WIDTH), jnp.float32, minval=0.9, maxval=0.999)
    b_f = jnp.linspace(3.0, 6.0, ML_HEADS, dtype=jnp.float32)[None, :] + nrm(21, (DEPTH, ML_HEADS), 0.01)
    return {
        'x': nrm(0, (BATCH, SEQ, D_MODEL), 1.0),
        'ffn1_norm': gain(1, (DEPTH, D_MODEL)),
        'ffn1_w1': nrm(2, (DEPTH, D_MODEL, D_FF), D_MODEL ** -0.5),
        'ffn1_w3': nrm(3, (DEPTH, D_MODEL, D_FF), D_MODEL ** -0.5),
        'ffn1_w2': nrm(4, (DEPTH, D_FF, D_MODEL), D_FF ** -0.5),
        'mix_norm': gain(5, (DEPTH, D_MODEL)),
        'w_in': nrm(6, (DEPTH, D_MODEL, D_IN), D_MODEL ** -0.5),
        'nsa_cmp_pos_k': nrm(7, (DEPTH, CMP_BLOCK, HEAD_DIM), 0.1),
        'nsa_cmp_w1_k': nrm(8, (DEPTH, CMP_BLOCK * HEAD_DIM, CMP_HIDDEN), (CMP_BLOCK * HEAD_DIM) ** -0.5),
        'nsa_cmp_w2_k': nrm(9, (DEPTH, CMP_HIDDEN, HEAD_DIM), CMP_HIDDEN ** -0.5),
        'nsa_cmp_pos_v': nrm(10, (DEPTH, CMP_BLOCK, HEAD_DIM), 0.1),
        'nsa_cmp_w1_v': nrm(11, (DEPTH, CMP_BLOCK * HEAD_DIM, CMP_HIDDEN), (CMP_BLOCK * HEAD_DIM) ** -0.5),
        'nsa_cmp_w2_v': nrm(12, (DEPTH, CMP_HIDDEN, HEAD_DIM), CMP_HIDDEN ** -0.5),
        'lru_conv_w': nrm(13, (DEPTH, CONV_WIDTH, LRU_WIDTH), CONV_WIDTH ** -0.5),
        'lru_conv_b': nrm(14, (DEPTH, LRU_WIDTH), 0.02),
        'lru_w_a': nrm(15, (DEPTH, LRU_BLOCKS, LRU_BW, LRU_BW), LRU_BW ** -0.5),
        'lru_b_a': nrm(16, (DEPTH, LRU_BLOCKS, LRU_BW), 0.02),
        'lru_w_x': nrm(17, (DEPTH, LRU_BLOCKS, LRU_BW, LRU_BW), LRU_BW ** -0.5),
        'lru_b_x': nrm(18, (DEPTH, LRU_BLOCKS, LRU_BW), 0.02),
        'lru_lambda': jnp.log(a0) - jnp.log1p(-a0),
        'ml_b_i': nrm(20, (DEPTH, ML_HEADS), 0.02),
        'ml_b_f': b_f,
        'head_norm': gain(22, (DEPTH, N_MIX_HEADS, HEAD_DIM)),
        'w_out': nrm(23, (DEPTH, D_MIX, D_MODEL), D_MIX ** -0.5),
        'ffn2_norm': gain(24, (DEPTH, D_MODEL)),
        'ffn2_w1': nrm(25, (DEPTH, D_MODEL, D_FF), D_MODEL ** -0.5),
        'ffn2_w3': nrm(26, (DEPTH, D_MODEL, D_FF), D_MODEL ** -0.5),
        'ffn2_w2': nrm(27, (DEPTH, D_FF, D_MODEL), D_FF ** -0.5),
        'final_norm': gain(28, (D_MODEL,)),
    }

def reference(x, ffn1_norm, ffn1_w1, ffn1_w3, ffn1_w2, mix_norm, w_in,
              nsa_cmp_pos_k, nsa_cmp_w1_k, nsa_cmp_w2_k, nsa_cmp_pos_v, nsa_cmp_w1_v, nsa_cmp_w2_v,
              lru_conv_w, lru_conv_b, lru_w_a, lru_b_a, lru_w_x, lru_b_x, lru_lambda,
              ml_b_i, ml_b_f, head_norm, w_out, ffn2_norm, ffn2_w1, ffn2_w3, ffn2_w2, final_norm):
    B, S = x.shape[0], x.shape[1]
    h = x
    for l in range(DEPTH):
        h = h + 0.5 * swiglu(rms_norm(h, ffn1_norm[l]), ffn1_w1[l], ffn1_w3[l], ffn1_w2[l])

        u = rms_norm(h, mix_norm[l]) @ w_in[l]
        (q_n, kc_n, vc_n, ks_n, vs_n, kw_n, vw_n, g_n,
         x_r, g_r, q_m, k_m, v_m, i_m, f_m, o_m) = jnp.split(u, IN_SPLIT_POINTS, axis=-1)
        kv = lambda z: z.reshape(B, S, NSA_GROUPS, HEAD_DIM)
        o_nsa = nsa_mixer(q_n.reshape(B, S, NSA_HEADS, HEAD_DIM), kv(kc_n), kv(vc_n), kv(ks_n), kv(vs_n),
                          kv(kw_n), kv(vw_n), g_n.reshape(B, S, NSA_HEADS, 3),
                          nsa_cmp_pos_k[l], nsa_cmp_w1_k[l], nsa_cmp_w2_k[l],
                          nsa_cmp_pos_v[l], nsa_cmp_w1_v[l], nsa_cmp_w2_v[l])
        o_lru = rglru_mixer(x_r, g_r, lru_conv_w[l], lru_conv_b[l], lru_w_a[l], lru_b_a[l],
                            lru_w_x[l], lru_b_x[l], lru_lambda[l])
        mh = lambda z: z.reshape(B, S, ML_HEADS, HEAD_DIM)
        o_ml = mlstm_mixer(mh(q_m), mh(k_m), mh(v_m), i_m + ml_b_i[l], f_m + ml_b_f[l], o_m)
        heads = jnp.concatenate([o_nsa, o_lru.reshape(B, S, LRU_BLOCKS, HEAD_DIM),
                                 o_ml.reshape(B, S, ML_HEADS, HEAD_DIM)], axis=2)
        heads = rms_norm(heads, head_norm[l]).reshape(B, S, D_MIX)
        h = h + heads @ w_out[l]

        h = h + 0.5 * swiglu(rms_norm(h, ffn2_norm[l]), ffn2_w1[l], ffn2_w3[l], ffn2_w2[l])
    return rms_norm(h, final_norm)


_drawn_inputs = setup_inputs


def setup_inputs(seed=0):
    import zlib

    import numpy as np

    out = dict(_drawn_inputs(seed))
    spreads = {}
    factors = {'ffn1_norm': 7.335,
     'mix_norm': 3.249,
     'nsa_cmp_pos_k': 6.787,
     'lru_b_a': 54.41,
     'lru_b_x': 51.246,
     'ml_b_i': 200.0,
     'head_norm': 129.905,
     'ffn2_norm': 25.673,
     'final_norm': 164.754,
     'nsa_cmp_pos_v': 8.0,
     'lru_conv_b': 8.0}
    for name, (base, spread) in spreads.items():
        noise = np.random.default_rng([zlib.crc32(name.encode()), seed]).standard_normal(out[name].shape)
        drawn = base * np.exp(spread * noise) if base else spread * noise
        out[name] = jnp.asarray(drawn.astype(out[name].dtype))
    for name, factor in factors.items():
        out[name] = (out[name] * factor).astype(out[name].dtype)
    return out
```

```python
from contextlib import ExitStack

import concourse.bass as bass
from concourse import mybir

F32 = mybir.dt.float32
F32R = mybir.dt.float32r
ALU = mybir.AluOpType
ACT = mybir.ActivationFunctionType
AX_X = mybir.AxisListType.X

P = 128
LAYERS = 2
S = 512
ST = S // P
DT = 1024 // P
FT = 2816 // P
FH = FT // 2
HD = 64
EPS = 1e-6
HEADS = 8
HPG = 4
NCMP = (S - 32) // 16 + 1
CP = 16
MASKED = 1e33
WIN_TILES = 16
U_Q, U_KC, U_VC, U_KS, U_XR, U_GR, U_QM, U_KM = 0, 4, 5, 6, 8, 10, 12, 14
TM_A, TM_B = 288, 512
UP_W, DOWN_W, TM_W = DT * P, FH * P, TM_A + TM_B
N_UP1, N_DN1, N_WIN, N_TM, N_OUT, N_UP2, N_DN2, N_CHUNKS = 0, 44, 60, 76, 84, 92, 136, 152


class Signal:

    def __init__(self, sem, before, per_layer):
        self.sem, self.before, self.per_layer = sem, before, per_layer

    def at(self, layer, count):
        return layer * self.per_layer + self.before + count


class Steps:

    def __init__(self, eng, sem):
        self.eng, self.sem, self.base, self.n = eng, sem, 0, 0

    def mark(self, ins):
        ins.then_inc(self.sem, 1)
        self.n += 1
        return self.base + self.n

    def done(self, ins):
        return self.eng.wait_ge(self.sem, self.mark(ins))


def build(nc, d, out):
    ctx = ExitStack()
    with ctx:
        enter = ctx.enter_context

        def sb(name, shape, dt=F32):
            return enter(nc.sbuf_tensor(name, shape, dt))

        resid = sb("resid", [P, DT, S])
        raw = [sb(f"raw{s}", [P, DOWN_W]) for s in range(2)]
        w_hi = [sb(f"w_hi{s}", [P, DOWN_W], F32R) for s in range(2)]
        w_lo = [sb(f"w_lo{s}", [P, DOWN_W], F32R) for s in range(2)]
        rstd = sb("rstd", [P, S])
        sumsq = sb("sumsq", [P, S])
        mean_sq = sumsq
        ones = sb("ones", [P, P])
        ident = sb("ident", [P, P])
        halves = sb("halves", [P, P])
        causal = sb("causal", [P, P])
        dist = sb("dist", [P, S])
        cmp_bias = sb("cmp_bias", [P, 2, ST, 4, 32])
        cmp_mask = sb("cmp_mask", [P, ST, 32])
        neg_slope = sb("neg_slope", [P, HEADS])
        pick = sb("pick", [4, 4, P])
        gains = sb("gains", [P, 7, DT])
        head_gain = sb("head_gain", [P, LAYERS, DT])
        lru_par = sb("lru_par", [P, LAYERS, 2, 8])
        gate_w = sb("gate_w", [P, LAYERS, 4, HD])
        gate_bd = sb("gate_bd", [P, 4, P])
        cmp_pos = sb("cmp_pos", [P, LAYERS, 2, CP])
        cmp_w2 = sb("cmp_w2", [P, LAYERS, 2, 2, HD])
        w2cur = sb("w2cur", [P, 2, 2, HD])
        ml_bias = sb("ml_bias", [4, LAYERS, 2])
        kcT = sb("kcT", [P, 2, 32])
        vc_bd = sb("vc_bd", [P, 256])

        top = [nc.sbuf_base]

        def region(size):
            at = (top[0] + 63) // 64 * 64
            top[0] = at + size
            return at

        def at(name, offset, shape, dt=F32):
            return nc.alloc_sbuf_tensor_at(name, shape, dt, offset=offset)

        x_area = region(2 * DT * S * 4)
        x_hi = at("x_hi", x_area, [P, DT, S], F32R)
        x_lo = at("x_lo", x_area + DT * S * 4, [P, DT, S], F32R)
        lru = [at(f"lru{i}", x_area + i * 4096, [P, 2, S]) for i in range(5)]
        rows = [at(f"row{i}", x_area + 20480 + i * 2048, [4, S]) for i in range(6)]

        mix = region(MIX_BYTES)
        hid_hi = at("hid_hi", mix, [P, FT, S], F32R)
        hid_lo = at("hid_lo", mix + FT * S * 4, [P, FT, S], F32R)
        tmp0 = mix + 2 * FT * S * 4
        g_scaled = at("g_scaled", tmp0, [P, S])
        g_silu = at("g_silu", tmp0 + 2048, [P, S])
        u_scaled = at("u_scaled", tmp0 + 4096, [P, S])
        sq = at("sq", tmp0 + 2048, [P, 2, S])
        hidden = at("hidden", tmp0 + 6144, [P, S])

        U = at("U", mix, [P, WIN_TILES, S])
        h_hi = at("h_hi", mix, [P, DT, S], F32R)
        h_lo = at("h_lo", mix + 16384, [P, DT, S], F32R)
        m1 = mix + 32768
        r1 = m1
        cmp_w1 = [at(f"cmp_w1_{i}", r1 + i * 16384, [P, CP, 256]) for i in range(2)]
        T = at("T", r1, [P, 2, S])
        PR = at("PR", r1 + 4096, [P, 2, S])
        PT = at("PT", r1 + 8192, [P, 2, S])
        q_head = [at(f"q_head{i}", r1 + 12288 + i * 2048, [HD, S]) for i in range(4)]
        ml_e = at("ml_e", r1 + 20480, [P, 2, S])
        ml_w = at("ml_w", r1 + 24576, [P, 2, S])
        att_o = at("att_o", r1 + 28672, [P, 2, S])
        o_sq = at("o_sq", r1, [P, ST * 12, HD])
        m2 = m1 + 32768
        k_all = at("k_all", m2, [HD, 4, S])
        v_all = at("v_all", m2 + 8192, [P, 4, ST, HD])
        v_aug = at("v_aug", m2 + 12288, [P, ST, 4, HD + 1])
        o_sig = at("o_sig", m2 + 16448, [P, ST, 256])
        o_all = at("o_all", m2 + 20544, [P, ST, 12, HD])
        zc = [at(f"zc{i}", m2 + 20544 + i * 4096, [P, CP, 64]) for i in range(2)]
        assert m2 + 20544 + 12288 <= mix + MIX_BYTES
        assert tmp0 + 8192 <= mix + MIX_BYTES
        small = region(SMALL_BYTES)

        def sm(name, shape, state=[0]):
            n = 4
            for k in shape[1:]:
                n *= k
            t = at(name, small + state[0], shape)
            state[0] += (n + 31) // 32 * 32
            assert state[0] <= SMALL_BYTES
            return t

        rcol = sm("rcol", [P, ST])
        gates = sm("gates", [P, ST, 24])
        ifcol = sm("ifcol", [P, ST, 8])
        cmp_hid = sm("cmp_hid", [P, 2, 2, 62])
        cmp_b = sm("cmp_b", [P, 4])
        cmp_max = sm("cmp_max", [P, 32])
        cmp_sum = sm("cmp_sum", [P, 32])
        n_max = sm("n_max", [P, 16])
        sums = sm("sums", [P, 4, 16])
        rec = sm("rec", [P, 16])
        coef = sm("coef", [P, 16])
        sp4 = sm("sp4", [P, 2])
        spt = sm("spt", [P, 6, 2])
        bcol = sm("bcol", [P, ST, 8])
        em = sm("em", [P, ST, 4])
        den = sm("den", [P, ST, 4])
        h_ss = sm("h_ss", [P, ST * 12])
        h_ms = sm("h_ms", [P, ST * 12])
        h_rs = sm("h_rs", [P, ST * 12])

        bank = [enter(nc.psum_tensor(f"bank{i}", [P, 512], F32)) for i in range(8)]

        def signal(name, per_layer, before=0):
            return Signal(enter(nc.semaphore(name)), before, per_layer)

        consts_loaded = signal("consts_loaded", 0)
        x_loaded = signal("x_loaded", 0)
        pool_consts = signal("pool_consts", 0)
        pool_zero = signal("pool_zero", 0)
        dve_consts = signal("dve_consts", 0)
        w_loaded = [signal(f"w_loaded{s}", 16 * N_CHUNKS // 2) for s in range(2)]
        w_hi_done = signal("w_hi_done", N_CHUNKS)
        w_lo_done = signal("w_lo_done", N_CHUNKS, 2)
        chunk_done = signal("chunk_done", N_CHUNKS, 2)
        resid_ready = signal("resid_ready", 24, 2)
        x_hi_done = signal("x_hi_done", 24, 8)
        x_lo_done = signal("x_lo_done", 24, 8)
        sq_ready = signal("sq_ready", 24, 8)
        sq_added = signal("sq_added", 24, 8 + 2)
        norm_sum = signal("norm_sum", 3)
        mean_ready = signal("mean_ready", 3)
        root_ready = signal("root_ready", 3)
        rstd_ready = signal("rstd_ready", 3)
        g_scaled_done = signal("g_scaled_done", 2 * FT, 1)
        silu_done = signal("silu_done", 2 * FT)
        u_scaled_done = signal("u_scaled_done", 2 * FT, 1)
        hidden_ready = signal("hidden_ready", 2 * FT)
        hidden_hi = signal("hidden_hi", 2 * FT)
        hidden_lo = signal("hidden_lo", 2 * FT)
        u_done = signal("u_done", WIN_TILES)
        rcol_ready = signal("rcol_ready", 1)
        rcol_done = signal("rcol_done", 1)
        tm_taken = signal("tm_taken", 1)
        cmp_w_loaded = [signal(f"cmp_w_loaded{i}", 16) for i in range(2)]
        layer_w_ready = signal("layer_w_ready", 1)
        k_all_ready = signal("k_all_ready", 4)
        zc_ready = [signal(f"zc_ready{i}", 1) for i in range(2)]
        cmp_h_ready = signal("cmp_h_ready", 1)
        cmp_b_done = signal("cmp_b_done", 1)
        cmp_hid_done = signal("cmp_hid_done", 1)
        cmp_kv_ready = signal("cmp_kv_ready", 1)
        cmp_kv_done = signal("cmp_kv_done", 1)
        cmp_s_ready = signal("cmp_s_ready", 2)
        cmp_t_done = signal("cmp_t_done", 1)
        cmp_p_done = signal("cmp_p_done", 1)
        cmp_pm_done = signal("cmp_pm_done", 1)
        cmp_tr_ready = signal("cmp_tr_ready", 1)
        cmp_pt_done = signal("cmp_pt_done", 1)
        cmp_o_ready = signal("cmp_o_ready", 1)
        cmp_o_done = signal("cmp_o_done", 1)
        conv_done = signal("conv_done", 2)
        lru_g_ready = signal("lru_g_ready", 2)
        lru_gates_done = signal("lru_gates_done", 2)
        sp_exp = signal("sp_exp", 1)
        sp_arg = signal("sp_arg", 2)
        sp_ln = signal("sp_ln", 1)
        sp_done = signal("sp_done", 1)
        lru_tanh = signal("lru_tanh", 1)
        lru_om = signal("lru_om", 1)
        lru_sqrt = signal("lru_sqrt", 1)
        lru_gelu = signal("lru_gelu", 1)
        lru_out = signal("lru_out", 1)
        lru_sq_done = signal("lru_sq_done", 1)
        lru_ms_ready = signal("lru_ms_ready", 1)
        lru_ms_done = signal("lru_ms_done", 1)
        lru_root = signal("lru_root", 1)
        lru_normed = signal("lru_normed", 1)
        lru_hi_done = signal("lru_hi_done", 2)
        lru_lo_done = signal("lru_lo_done", 2)
        q_loaded = [signal(f"q_loaded{i}", 64) for i in range(4)]
        att_s_ready = signal("att_s_ready", 64, 16)
        att_scored = signal("att_scored", 64, 4)
        att_exp_done = signal("att_exp_done", 64, 2)
        att_tr_ready = signal("att_tr_ready", 64, 2)
        att_copied = signal("att_copied", 64, 2)
        att_pv_ready = signal("att_pv_ready", 64, 2)
        acc_taken = signal("acc_taken", 4, 1)
        if_t_ready = signal("if_t_ready", 1)
        ml_abs = signal("ml_abs", 1)
        ml_exp = signal("ml_exp", 1)
        ml_arg = signal("ml_arg", 1)
        ml_ln = signal("ml_ln", 1)
        ml_rows = signal("ml_rows", 1)
        ml_cols_ready = signal("ml_cols_ready", 1)
        ml_cols_done = signal("ml_cols_done", 1)
        ml_em = signal("ml_em", 1)
        ml_m_ready = signal("ml_m_ready", 4)
        ml_d_done = signal("ml_d_done", 16, 0)
        ml_e_done = signal("ml_e_done", 16, 0)
        ml_s_ready = signal("ml_s_ready", 16)
        ml_w_done = signal("ml_w_done", 16, 2)
        ml_pv = signal("ml_pv", 16, 2)
        ml_o_done = signal("ml_o_done", 1)
        o_sq_done = signal("o_sq_done", 1)
        o_ms_done = signal("o_ms_done", 1)
        o_root = signal("o_root", 1)
        o_normed = signal("o_normed", 1)
        h_t_ready = signal("h_t_ready", 6)
        h_hi_done = signal("h_hi_done", 6)
        h_lo_done = signal("h_lo_done", 6, 0)
        dve_step = signal("dve_step", 0)
        waits_met = signal("waits_met", 0)
        out_ready = signal("out_ready", 0)
        out_stored = signal("out_stored", 0)

        def wait_alone(eng, sem, value):
            eng.wait_ge(sem, value).then_inc(waits_met.sem, 1)

        block = enter(nc.Block())

        @block.sync
        def _(sp):
            sp.dma_start(resid[:], d["x"]).then_inc(x_loaded.sem, 16)

            def stream(l, n, slot, src):
                sp.wait_ge(w_lo_done.sem, l * N_CHUNKS + n + 1)
                sp.dma_start(raw[slot][:, 0:src.shape[1]], src).then_inc(w_loaded[slot].sem, 16)

            with sp.Fori(0, LAYERS) as l:
                def ffn(up, down, n_up, n_down):
                    with sp.Fori(0, FT) as m:
                        for s in range(2):
                            stream(l, n_up + 2 * m + s, s, up[l, m, s])
                    with sp.Fori(0, DT) as m:
                        for s in range(2):
                            stream(l, n_down + 2 * m + s, s, down[l, m, s])

                ffn(d["up1"], d["down1"], N_UP1, N_DN1)
                with sp.Fori(0, WIN_TILES // 2) as j:
                    for s in range(2):
                        stream(l, N_WIN + 2 * j + s, s, d["w_in"][l, 2 * j + s])
                sp.wait_ge(chunk_done.sem, chunk_done.at(l, N_WIN))
                for i in range(2):
                    sp.dma_start(cmp_w1[i][:], d["cmp_w1"][l, i]).then_inc(cmp_w_loaded[i].sem, 16)
                with sp.Fori(0, DT // 2) as j:
                    for s in range(2):
                        stream(l, N_TM + 2 * j + s, s, d["w_tm"][l, 2 * j + s])
                for s in range(2):
                    stream(l, N_OUT + s, s, d["w_out"][l, s])
                sp.wait_ge(cmp_h_ready.sem, cmp_h_ready.at(l, 1))
                wait_alone(sp, u_done.sem, u_done.at(l, WIN_TILES))
                with sp.Fori(0, 2) as b:
                    with sp.Fori(0, 2) as g:
                        for h in range(HPG):
                            sp.wait_ge(att_s_ready.sem, l * 64 + (b * 2 + g) * 16 + 4 * h + 4)
                            sp.dma_start(q_head[h][:], U[HD * (h % 2):HD * (h % 2) + HD, g * 2 + (U_Q + h // 2), :])\
                              .then_inc(q_loaded[h].sem, 16)
                with sp.Fori(1, DT // 2) as j:
                    for s in range(2):
                        stream(l, N_OUT + 2 * j + s, s, d["w_out"][l, 2 * j + s])
                ffn(d["up2"], d["down2"], N_UP2, N_DN2)
            for m in range(DT):
                sp.wait_ge(out_ready.sem, m + 1)
                sp.dma_start(out[:, m, :], resid[:, m, :]).then_inc(out_stored.sem, 16)
            sp.wait_ge(out_stored.sem, 16 * DT)

        @block.gpsimd
        def _(pool):
            loads = [(gains, "gains"), (head_gain, "head_gain"), (lru_par, "lru_par"), (gate_w, "gate_w"),
                     (cmp_pos, "cmp_pos"), (cmp_w2, "cmp_w2"), (ml_bias, "ml_bias")]
            for t, name in loads:
                pool.dma_start(t[:], d[name]).then_inc(consts_loaded.sem, 16)
            zero = 0
            for t, v in [(ones, 1.0), (ident, 0.0), (halves, 0.0), (causal, 1.0), (cmp_mask, 1.0),
                         (pick, 1.0), (gate_bd, 0.0), (kcT, 0.0), (vc_bd, 0.0)]:
                nc.gpsimd.memset(t[:], v).then_inc(pool_zero.sem, 1)
                zero += 1
            nc.gpsimd.iota(dist[:], pattern=[[-1, S]], base=S - P, channel_multiplier=1,
                           allow_small_or_imprecise_dtypes=True).then_inc(pool_zero.sem, 1)
            nc.gpsimd.iota(cmp_bias[:], pattern=[[0, 2], [P, ST], [0, 4], [-16, 32]], base=-31, channel_multiplier=1,
                           allow_small_or_imprecise_dtypes=True).then_inc(pool_zero.sem, 1)
            for h in range(HEADS):
                nc.gpsimd.memset(neg_slope[:, h:h + 1], -(2.0 ** -(h + 1))).then_inc(pool_zero.sem, 1)
            zero += 2 + HEADS
            pool.wait_ge(pool_zero.sem, zero)
            sel = nc.gpsimd.affine_select
            sel(out=ident[:], in_=ident[:], compare_op=ALU.not_equal, fill=1.0, base=0, pattern=[[-1, P]],
                channel_multiplier=1).then_inc(pool_consts.sem, 1)
            sel(out=causal[:], in_=causal[:], compare_op=ALU.is_ge, fill=0.0, base=0, pattern=[[1, P]],
                channel_multiplier=-1).then_inc(pool_consts.sem, 1)
            sel(out=dist[:], in_=dist[:], compare_op=ALU.is_ge, fill=MASKED, base=S - P, pattern=[[-1, S]],
                channel_multiplier=1).then_inc(pool_consts.sem, 1)
            sel(out=cmp_bias[:], in_=cmp_bias[:], compare_op=ALU.is_ge, fill=MASKED, base=-31,
                pattern=[[0, 2], [P, ST], [0, 4], [-16, 32]], channel_multiplier=1).then_inc(pool_consts.sem, 1)
            sel(out=cmp_mask[:], in_=cmp_mask[:], compare_op=ALU.is_ge, fill=0.0, base=-31,
                pattern=[[P, ST], [-16, 32]], channel_multiplier=1).then_inc(pool_consts.sem, 1)
            sel(out=pick[:], in_=pick[:], compare_op=ALU.is_equal, fill=0.0, base=0, pattern=[[-1, 4], [0, P]],
                channel_multiplier=1).then_inc(pool_consts.sem, 1)

        POOL_CONSTS = 6

        @block.tensor
        def _(pe):
            mm = nc.tensor.matmul
            pe.sem_inc(chunk_done.sem, 2)
            pe.sem_inc(att_s_ready.sem, 16)
            pe.sem_inc(att_tr_ready.sem, 2)
            pe.sem_inc(att_pv_ready.sem, 2)
            pe.sem_inc(ml_pv.sem, 2)
            pe.wait_ge(pool_consts.sem, POOL_CONSTS)
            pe.wait_ge(dve_consts.sem, 1)

            def product(slot, tiles, a_hi, a_lo, k0, dst, first, last, tile_wait=None):
                for k in range(tiles):
                    if tile_wait is not None:
                        tile_wait(k)
                    wh = w_hi[slot][:, k * P:(k + 1) * P]
                    wl = w_lo[slot][:, k * P:(k + 1) * P]
                    mm(dst, wh, a_hi[:, k0 + k, :], start=first and k == 0, stop=False)
                    mm(dst, wh, a_lo[:, k0 + k, :], start=False, stop=False)
                    ins = mm(dst, wl, a_hi[:, k0 + k, :], start=False, stop=last and k == tiles - 1)
                return ins

            with pe.Fori(0, LAYERS) as l:
                def chunk_split(n):
                    pe.wait_ge(w_lo_done.sem, w_lo_done.at(l, n + 1))

                def norm(q):
                    pe.wait_ge(sq_added.sem, sq_added.at(l, 8 * q))
                    mm(bank[6][:, :], ones[:], sumsq[:], start=True, stop=True).then_inc(norm_sum.sem, 1)

                def up(f, n_up, m, first):
                    n = n_up + 2 * m
                    chunk_split(n)
                    pe.wait_ge(g_scaled_done.sem, g_scaled_done.at(l, f * FT + m))
                    wait = (lambda k: pe.wait_ge(x_lo_done.sem, x_lo_done.at(l, (16 * f - 8) + k + 1))) if first else None
                    product(0, DT, x_hi, x_lo, 0, bank[0][:], True, True, wait).then_inc(chunk_done.sem, 1)
                    if first:
                        norm(2 * f)
                    chunk_split(n + 1)
                    pe.wait_ge(u_scaled_done.sem, u_scaled_done.at(l, f * FT + m))
                    product(1, DT, x_hi, x_lo, 0, bank[1][:], True, True).then_inc(chunk_done.sem, 1)

                def down(f, n_down, j):
                    for i in range(2):
                        m = 2 * j + i
                        n = n_down + 2 * m
                        pe.wait_ge(resid_ready.sem, resid_ready.at(l, 16 * f + m - 1))
                        for s in range(2):
                            chunk_split(n + s)
                            pe.wait_ge(hidden_lo.sem, hidden_lo.at(l, f * FT + FH * (s + 1)))
                            product(s, FH, hid_hi, hid_lo, FH * s, bank[4 + i][:], s == 0, s == 1)\
                                .then_inc(chunk_done.sem, 1)

                for f, n_up, n_down in ((0, N_UP1, N_DN1),):
                    up(f, n_up, 0, True)
                    with pe.Fori(1, FT) as m:
                        up(f, n_up, m, False)
                    with pe.Fori(0, DT // 2) as j:
                        down(f, n_down, j)

                def w_in(j, first):
                    for i in range(2):
                        chunk_split(N_WIN + 2 * j + i)
                        if not first:
                            pe.wait_ge(u_done.sem, u_done.at(l, 2 * j + i - 1))
                        wait = (lambda k: pe.wait_ge(x_lo_done.sem, x_lo_done.at(l, k + 1))) if first and i == 0 else None
                        product(i, DT, x_hi, x_lo, 0, bank[2 + i][:], True, True, wait).then_inc(chunk_done.sem, 1)
                        if first and i == 0:
                            norm(1)

                w_in(0, True)
                with pe.Fori(1, WIN_TILES // 2) as j:
                    w_in(j, False)
                pe.wait_ge(rstd_ready.sem, rstd_ready.at(l, 2))
                for t in range(ST):
                    ins = mm(bank[6][:, t:t + 1], rstd[0:1, t * P:(t + 1) * P], ones[0:1, 0:1], start=True, stop=True)
                ins.then_inc(rcol_ready.sem, 1)
                pe.wait_ge(u_done.sem, u_done.at(l, WIN_TILES))
                pe.wait_ge(rcol_done.sem, rcol_done.at(l, 1))
                for k in range(DT):
                    chunk_split(N_TM + k)
                    wh, wl = w_hi[k % 2], w_lo[k % 2]
                    for t in range(ST):
                        xh, xl = (a[:, k, t * P:(t + 1) * P] for a in (x_hi, x_lo))
                        for x, w, part in ((xh, wh, 0), (xh, wl, 1), (xl, wh, 2)):
                            for half, (c0, c1) in enumerate(((0, TM_A), (TM_A, TM_W))):
                                ins = mm(bank[2 * t + half][:, 0:c1 - c0], x, w[:, c0:c1],
                                         start=k == 0 and part == 0, stop=k == DT - 1 and part == 2)
                    ins.then_inc(chunk_done.sem, 1)
                pe.wait_ge(tm_taken.sem, tm_taken.at(l, 1))

                for kv in range(2):
                    pe.wait_ge(cmp_w_loaded[kv].sem, cmp_w_loaded[kv].at(l, 16))
                    pe.wait_ge(zc_ready[kv].sem, zc_ready[kv].at(l, 1))
                    for m in range(2):
                        o = (2 * kv + m) * 64
                        for c in range(CP):
                            ins = mm(bank[2][:, o:o + 63], cmp_w1[kv][:, c, m * P:(m + 1) * P], zc[kv][:, c, 0:63],
                                     start=c == 0, stop=c == CP - 1)
                ins.then_inc(cmp_h_ready.sem, 1)
                pe.wait_ge(cmp_hid_done.sem, cmp_hid_done.at(l, 1))
                pe.wait_ge(layer_w_ready.sem, layer_w_ready.at(l, 1))
                for par in range(2):
                    for g in range(2):
                        for m in range(2):
                            mm(bank[3][HD * par:HD * par + HD, g * 32:g * 32 + NCMP], w2cur[:, 0, m, :],
                               cmp_hid[:, 0, m, g * NCMP:(g + 1) * NCMP], start=m == 0, stop=m == 1)
                for j in range(4):
                    g = j // 2
                    for m in range(2):
                        ins = mm(bank[5][32 * j:32 * j + NCMP, HD * j:HD * (j + 1)],
                                 cmp_hid[:, 1, m, g * NCMP:(g + 1) * NCMP], w2cur[:, 1, m, :],
                                 start=m == 0, stop=m == 1)
                ins.then_inc(cmp_kv_ready.sem, 1)
                pe.wait_ge(cmp_kv_done.sem, cmp_kv_done.at(l, 1))
                for t in range(ST):
                    for h in range(HEADS):
                        par = h % 2
                        hp = HD * par
                        o = (t * 4 + h // 2) * 32
                        ins = mm(bank[2 + par][:, o:o + 32], U[hp:hp + HD, U_Q + h // 2, t * P:(t + 1) * P],
                                 kcT[hp:hp + HD, h // HPG, :], start=True, stop=True)
                        if t == ST - 1 and h >= HEADS - 2:
                            ins.then_inc(cmp_s_ready.sem, 1)
                for c in range(2):
                    pe.wait_ge(conv_done.sem, conv_done.at(l, c + 1))
                    if c:
                        pe.wait_ge(lru_gates_done.sem, lru_gates_done.at(l, c))
                    mm(bank[0][:], gate_bd[:, c, :], lru[0][:, c, :], start=True, stop=True)
                    mm(bank[1][:], gate_bd[:, 2 + c, :], lru[0][:, c, :], start=True, stop=True)\
                        .then_inc(lru_g_ready.sem, 1)
                for t in range(ST):
                    nc.tensor.transpose(bank[6][0:4, t * P:(t + 1) * P], ifcol[:, t, 0:4], ident[:])
                for t in range(ST):
                    ins = nc.tensor.transpose(bank[7][0:4, t * P:(t + 1) * P], ifcol[:, t, 4:8], ident[:])
                ins.then_inc(if_t_ready.sem, 1)
                pe.wait_ge(cmp_pm_done.sem, cmp_pm_done.at(l, 1))
                for n in range(8):
                    ins = nc.tensor.transpose(bank[4 + n // 4][:, (n % 4) * P:(n % 4 + 1) * P],
                                              PR[:, n // 4, (n % 4) * P:(n % 4 + 1) * P], ident[:])
                ins.then_inc(cmp_tr_ready.sem, 1)
                pe.wait_ge(cmp_pt_done.sem, cmp_pt_done.at(l, 1))
                for t in range(ST):
                    for par in range(2):
                        ins = mm(bank[2 + t][:, par * 256:(par + 1) * 256], PT[:, par, t * P:(t + 1) * P], vc_bd[:],
                                 start=True, stop=True)
                ins.then_inc(cmp_o_ready.sem, 1)
                pe.wait_ge(lru_sq_done.sem, lru_sq_done.at(l, 1))
                for c in range(2):
                    ins = mm(bank[c][:], halves[:], lru[1][:, c, :], start=True, stop=True)
                ins.then_inc(lru_ms_ready.sem, 1)
                wait_alone(pe, ml_rows.sem, ml_rows.at(l, 1))
                for t in range(ST):
                    nc.tensor.transpose(bank[6][:, t * 8:t * 8 + 4], rows[3][:, t * P:(t + 1) * P], ident[0:4, 0:4])
                    ins = nc.tensor.transpose(bank[6][:, t * 8 + 4:t * 8 + 8], rows[5][:, t * P:(t + 1) * P],
                                              ident[0:4, 0:4])
                ins.then_inc(ml_cols_ready.sem, 1)
                pe.wait_ge(cmp_o_done.sem, cmp_o_done.at(l, 1))
                pe.wait_ge(ml_cols_done.sem, ml_cols_done.at(l, 1))
                pe.wait_ge(lru_ms_done.sem, lru_ms_done.at(l, 1))

                def ml_scores(n):
                    h, j = n // ST, n % ST
                    hp = HD * (h % 2)
                    if j == 0:
                        if h:
                            pe.wait_ge(ml_d_done.sem, ml_d_done.at(l, ST * h))
                        mm(bank[6][:], pick[:, h, :], rows[4][:], start=True, stop=True).then_inc(ml_m_ready.sem, 1)
                    pe.wait_ge(ml_w_done.sem, ml_w_done.at(l, n - 1))
                    mm(bank[n % 2][:, 0:S - j * P], U[hp:hp + HD, U_KM + h // 2, j * P:(j + 1) * P],
                       U[hp:hp + HD, U_QM + h // 2, j * P:S], start=True, stop=True).then_inc(ml_s_ready.sem, 1)

                ml_scores(0)
                for n in range(16):
                    if n + 1 < 16:
                        ml_scores(n + 1)
                    h, j = n // ST, n % ST
                    pe.wait_ge(ml_w_done.sem, ml_w_done.at(l, n + 1))
                    for i in range(j, ST):
                        ins = mm(bank[(2, 3, 4, 5)[i]][:, h * (HD + 1):(h + 1) * (HD + 1)],
                                 ml_w[:, n % 2, (i - j) * P:(i - j + 1) * P], v_aug[:, j, h, :],
                                 start=j == 0, stop=j == i)
                    ins.then_inc(ml_pv.sem, 1)

                pe.wait_ge(ml_o_done.sem, ml_o_done.at(l, 1))
                wait_alone(pe, k_all_ready.sem, k_all_ready.at(l, 4))
                with pe.Fori(0, 2) as b:
                    with pe.Fori(0, 2) as g:
                        kv = b * 2 + g

                        def scores(u):
                            h, i = u // ST, u % ST
                            if i == 0:
                                pe.wait_ge(q_loaded[h].sem, l * 64 + kv * 16 + 16)
                            wait_alone(pe, att_scored.sem, l * 64 + kv * 16 + u + 1)
                            w = (i + 1) * P
                            ins = mm(bank[u % 4][:, 0:w], q_head[h][:, i * P:(i + 1) * P], k_all[:, kv, 0:w],
                                     start=True, stop=True)
                            ins.then_inc(att_s_ready.sem, 1)

                        def flip(u):
                            pe.wait_ge(att_exp_done.sem, l * 64 + kv * 16 + u + 3)
                            pe.wait_ge(att_copied.sem, l * 64 + kv * 16 + u + 1)
                            for j in range(u % ST + 1):
                                ins = nc.tensor.transpose(bank[4 + u % 2][:, j * P:(j + 1) * P],
                                                          PR[:, u % 2, j * P:(j + 1) * P], ident[:])
                            ins.then_inc(att_tr_ready.sem, 1)

                        def values(u):
                            pe.wait_ge(att_copied.sem, l * 64 + kv * 16 + u + 3)
                            i = u % ST
                            if u == 0:
                                pe.wait_ge(acc_taken.sem, l * 4 + kv + 1)
                            for j in range(i + 1):
                                ins = mm(bank[6 + u // 8][:, (u % 8) * HD:(u % 8 + 1) * HD],
                                         PT[:, u % 2, j * P:(j + 1) * P], v_all[:, kv, j, :],
                                         start=j == 0, stop=j == i)
                            ins.then_inc(att_pv_ready.sem, 1)

                        for u in range(3):
                            scores(u)
                        for u in range(16):
                            if u + 3 < 16:
                                scores(u + 3)
                            flip(u)
                            if u:
                                values(u - 1)
                        values(15)

                pe.wait_ge(o_normed.sem, o_normed.at(l, 1))
                for n in range(6):
                    if n >= 4:
                        pe.wait_ge(h_lo_done.sem, h_lo_done.at(l, n - 3))
                    for t in range(ST):
                        ins = nc.tensor.transpose(bank[n % 4][:, t * P:(t + 1) * P], o_all[:, t, 2 * n:2 * n + 2, :],
                                                  ident[:])
                    ins.then_inc(h_t_ready.sem, 1)

                wait_alone(pe, h_lo_done.sem, h_lo_done.at(l, 6))
                wait_alone(pe, lru_lo_done.sem, lru_lo_done.at(l, 2))

                def w_out(j):
                    for i in range(2):
                        chunk_split(N_OUT + 2 * j + i)
                        pe.wait_ge(resid_ready.sem, resid_ready.at(l, DT + 2 * j + i - 1))
                        product(i, DT, h_hi, h_lo, 0, bank[4 + i][:], True, True).then_inc(chunk_done.sem, 1)

                with pe.Fori(0, DT // 2) as j:
                    w_out(j)

                up(1, N_UP2, 0, True)
                with pe.Fori(1, FT) as m:
                    up(1, N_UP2, m, False)
                with pe.Fori(0, DT // 2) as j:
                    down(1, N_DN2, j)
            pe.wait_ge(sq_added.sem, sq_added.at(LAYERS, 0))
            mm(bank[6][:, :], ones[:], sumsq[:], start=True, stop=True).then_inc(norm_sum.sem, 1)

        @block.scalar
        def _(act):
            fn = nc.scalar.activation
            act.sem_inc(att_exp_done.sem, 2)
            act.sem_inc(att_copied.sem, 2)
            act.wait_ge(consts_loaded.sem, 16 * CONST_LOADS)
            act.wait_ge(x_loaded.sem, 16)

            def split_hi(l, n, half, slot, width):
                act.wait_ge(w_loaded[slot].sem, w_loaded[slot].at(l, 16 * half + 16))
                act.wait_ge(chunk_done.sem, chunk_done.at(l, n - 1))
                fn(w_hi[slot][:, 0:width], raw[slot][:, 0:width], ACT.Copy).then_inc(w_hi_done.sem, 1)

            def next_hi(l, n, half, s, width):
                split_hi(l, n + 2 + s, half + 1, s, width)

            def norm_input(l, r, m, q):
                g = gains[:, q, bass.ds(m, 1)]
                tile = resid[:, bass.ds(m, 1), :].rearrange("p a s -> p (a s)")
                fn(x_hi[:, bass.ds(m, 1), :].rearrange("p a s -> p (a s)"), tile, ACT.Copy, scale=g)\
                    .then_inc(x_hi_done.sem, 1)

            def square(l, r, m, slot):
                wait_alone(act, sq_added.sem, sq_added.at(l, r + m - 1))
                fn(sq[:, slot, :], resid[:, bass.ds(m, 1), :].rearrange("p a s -> p (a s)"), ACT.Square)\
                    .then_inc(sq_ready.sem, 1)

            def root(l, q):
                act.wait_ge(mean_ready.sem, mean_ready.at(l, q + 1))
                fn(mean_sq[:], mean_sq[:], ACT.Sqrt).then_inc(root_ready.sem, 1)

            for m in range(DT):
                norm_input(0, -DT, m, 0)
                square(0, -DT, m, m % 2)

            with act.Fori(0, LAYERS) as l:
                def up(f, n_up, m, width, first=False):
                    n, half = n_up + 2 * m, n_up // 2 + m
                    next_hi(l, n, half, 0, width)
                    if first:
                        root(l, 2 * f)
                    act.wait_ge(g_scaled_done.sem, g_scaled_done.at(l, f * FT + m + 1))
                    fn(g_silu[:], g_scaled[:], ACT.Silu).then_inc(silu_done.sem, 1)
                    next_hi(l, n, half, 1, width)
                    act.wait_ge(hidden_ready.sem, hidden_ready.at(l, f * FT + m + 1))
                    fn(hid_hi[:, bass.ds(m, 1), :].rearrange("p a s -> p (a s)"), hidden[:], ACT.Copy)\
                        .then_inc(hidden_hi.sem, 1)

                def project(n0, r, q, j, chunks, width):
                    for i in range(2):
                        m = 2 * j + i
                        for c in range(chunks):
                            s = (i * chunks + c) % 2
                            n = n0 + chunks * m + c
                            half = n0 // 2 + (chunks * j + (i * chunks + c) // 2)
                            if width[i]:
                                next_hi(l, n0 + 2 * chunks * j + (i * chunks + c) - s, half, s, width[i])
                        act.wait_ge(resid_ready.sem, resid_ready.at(l, r + m + 1))
                        norm_input(l, r, m, q)
                        square(l, r, m, i)

                def ffn(f, n_up, n_down, r, q, next_width):
                    up(f, n_up, 0, UP_W, True)
                    nc.scalar.preload_act_table(ACT.Silu)
                    with act.Fori(1, FT - 1) as m:
                        up(f, n_up, m, UP_W)
                    up(f, n_up, FT - 1, DOWN_W)
                    with act.Fori(0, DT // 2 - 1) as j:
                        project(n_down, r, q, j, 2, (DOWN_W, DOWN_W))
                    project(n_down, r, q, DT // 2 - 1, 2, (DOWN_W, next_width))

                for s in range(2):
                    split_hi(l, s, 0, s, UP_W)
                ffn(0, N_UP1, N_DN1, 0, 3 * l + 1, UP_W)

                next_hi(l, N_WIN, N_WIN // 2, 0, UP_W)
                root(l, 1)
                next_hi(l, N_WIN, N_WIN // 2, 1, UP_W)
                with act.Fori(1, WIN_TILES // 2 - 1) as j:
                    for s in range(2):
                        next_hi(l, N_WIN + 2 * j, N_WIN // 2 + j, s, UP_W)
                for s in range(2):
                    next_hi(l, N_TM - 2, N_TM // 2 - 1, s, TM_W)
                act.wait_ge(rcol_ready.sem, rcol_ready.at(l, 1))
                fn(rcol[:], bank[6][:, 0:ST], ACT.Copy).then_inc(rcol_done.sem, 1)
                for j in range(DT // 2):
                    for s in range(2):
                        next_hi(l, N_TM + 2 * j, N_TM // 2 + j, s, TM_W if j < DT // 2 - 1 else UP_W)
                act.wait_ge(chunk_done.sem, chunk_done.at(l, N_OUT))
                act.wait_ge(rcol_done.sem, rcol_done.at(l, 1))
                for t in range(ST):
                    r, a, c = rcol[:, t:t + 1], bank[2 * t], bank[2 * t + 1]
                    fn(v_all[:, :, t, :], a[:, 0:256].rearrange("p (k d) -> p k d", k=4), ACT.Copy, scale=r)
                    fn(ifcol[:, t, :], a[:, 280:288], ACT.Copy, scale=r)
                    fn(v_aug[:, t, :, 0:HD], c[:, 0:256].rearrange("p (h d) -> p h d", h=4), ACT.Copy, scale=r)
                    fn(gates[:, t, :], a[:, 256:280], ACT.Sigmoid, scale=r)
                    ins = fn(o_sig[:, t, :], c[:, 256:512], ACT.Sigmoid, scale=r)
                ins.then_inc(tm_taken.sem, 1)
                act.wait_ge(u_done.sem, u_done.at(l, WIN_TILES))
                for kv in range(4):
                    g = HD * (kv % 2)
                    fn(k_all[:, kv, :], U[g:g + HD, U_KS + kv // 2, :], ACT.Copy, scale=HD ** -0.5)\
                        .then_inc(k_all_ready.sem, 1)

                for par in range(2):
                    for g in range(2):
                        src = U[HD * g:HD * g + HD, U_KC, :]
                        for pairs, view in block_halves(src, par):
                            fn(zc[0][HD * par:HD * par + HD, pairs, g * NCMP:(g + 1) * NCMP], view, ACT.Copy)
                fn(zc[0][:, :, 62], cmp_pos[:, l, 0, :], ACT.Copy).then_inc(zc_ready[0].sem, 1)
                act.wait_ge(cmp_h_ready.sem, cmp_h_ready.at(l, 1))
                fn(cmp_b[:], bank[2][:, 0:256].rearrange("p (a n) -> p a n", a=4)[:, :, 62], ACT.Copy)\
                    .then_inc(cmp_b_done.sem, 1)
                act.wait_ge(cmp_b_done.sem, cmp_b_done.at(l, 1))
                for n in range(4):
                    ins = fn(cmp_hid[:, n // 2, n % 2, :], bank[2][:, n * 64:n * 64 + 62], ACT.Silu,
                             bias=cmp_b[:, n:n + 1])
                ins.then_inc(cmp_hid_done.sem, 1)
                for c in range(2):
                    act.wait_ge(lru_g_ready.sem, lru_g_ready.at(l, c + 1))
                    fn(lru[1][:, c, :], bank[0][:], ACT.Sigmoid, bias=lru_par[:, l, c, 5:6])
                    fn(lru[2][:, c, :], bank[1][:], ACT.Sigmoid, bias=lru_par[:, l, c, 6:7])\
                        .then_inc(lru_gates_done.sem, 1)
                act.wait_ge(sp_arg.sem, sp_arg.at(l, 1))
                fn(spt[:, 1, :], spt[:, 0, :], ACT.Exp, scale=-1.0).then_inc(sp_exp.sem, 1)
                act.wait_ge(cmp_t_done.sem, cmp_t_done.at(l, 1))
                fn(PR[:], T[:], ACT.Exp).then_inc(cmp_p_done.sem, 1)
                act.wait_ge(ml_abs.sem, ml_abs.at(l, 1))
                fn(rows[2][:], rows[2][:], ACT.Exp, scale=-1.0).then_inc(ml_exp.sem, 1)
                act.wait_ge(sp_arg.sem, sp_arg.at(l, 2))
                fn(spt[:, 3, :], spt[:, 2, :], ACT.Ln).then_inc(sp_ln.sem, 1)
                act.wait_ge(ml_arg.sem, ml_arg.at(l, 1))
                fn(rows[4][:], rows[3][:], ACT.Ln).then_inc(ml_ln.sem, 1)
                act.wait_ge(cmp_tr_ready.sem, cmp_tr_ready.at(l, 1))
                for n in range(2):
                    ins = fn(PT[:, n, :], bank[4 + n][:], ACT.Copy)
                ins.then_inc(cmp_pt_done.sem, 1)
                act.wait_ge(sp_done.sem, sp_done.at(l, 1))
                act.wait_ge(lru_gates_done.sem, lru_gates_done.at(l, 2))
                for c in range(2):
                    ins = fn(lru[1][:, c, :], lru[1][:, c, :], ACT.Tanh, scale=sp4[:, c:c + 1])
                ins.then_inc(lru_tanh.sem, 1)
                fn(U[:, U_GR:U_GR + 2, :], U[:, U_GR:U_GR + 2, :], ACT.Gelu_apprx_tanh).then_inc(lru_gelu.sem, 1)
                act.wait_ge(lru_om.sem, lru_om.at(l, 1))
                fn(lru[1][:], lru[1][:], ACT.Sqrt).then_inc(lru_sqrt.sem, 1)
                act.wait_ge(lru_out.sem, lru_out.at(l, 1))
                fn(lru[1][:], lru[0][:], ACT.Square).then_inc(lru_sq_done.sem, 1)
                act.wait_ge(lru_ms_done.sem, lru_ms_done.at(l, 1))
                fn(lru[3][:], lru[3][:], ACT.Sqrt).then_inc(lru_root.sem, 1)
                act.wait_ge(ml_cols_done.sem, ml_cols_done.at(l, 1))
                fn(em[:], bcol[:, :, 4:8], ACT.Exp, scale=-1.0).then_inc(ml_em.sem, 1)
                for n in range(16):
                    act.wait_ge(ml_d_done.sem, ml_d_done.at(l, n + 1))
                    e = ml_e[:, n % 2, 0:S - (n % ST) * P]
                    fn(e, e, ACT.Exp).then_inc(ml_e_done.sem, 1)

                with act.Fori(0, 2) as b:
                    with act.Fori(0, 2) as g:
                        pas = l * 64 + (b * 2 + g) * 16

                        def exps(u):
                            act.wait_ge(att_scored.sem, pas + u + 5)
                            act.wait_ge(att_tr_ready.sem, pas + u + 1)
                            w = (u % ST + 1) * P
                            fn(PR[:, u % 2, 0:w], T[:, u % 2, 0:w], ACT.Exp, bias=n_max[:, u:u + 1],
                               accum_out=sums[:, b * 2 + g, u:u + 1]).then_inc(att_exp_done.sem, 1)

                        exps(0)
                        for u in range(16):
                            if u + 1 < 16:
                                exps(u + 1)
                            act.wait_ge(att_tr_ready.sem, pas + u + 3)
                            act.wait_ge(att_pv_ready.sem, pas + u + 1)
                            w = (u % ST + 1) * P
                            fn(PT[:, u % 2, 0:w], bank[4 + u % 2][:, 0:w], ACT.Copy).then_inc(att_copied.sem, 1)

                act.wait_ge(acc_taken.sem, acc_taken.at(l, 4))
                fn(o_sq[:], o_all[:].rearrange("p t h d -> p (t h) d"), ACT.Square).then_inc(o_sq_done.sem, 1)
                act.wait_ge(o_ms_done.sem, o_ms_done.at(l, 1))
                fn(h_ms[:], h_ms[:], ACT.Sqrt).then_inc(o_root.sem, 1)
                act.wait_ge(lru_normed.sem, lru_normed.at(l, 1))
                for c in range(2):
                    fn(h_hi[:, 4 + c, :], lru[2][:, c, :], ACT.Copy).then_inc(lru_hi_done.sem, 1)
                for n in range(6):
                    k = n if n < 4 else n + 2
                    act.wait_ge(h_t_ready.sem, h_t_ready.at(l, n + 1))
                    fn(h_hi[:, k, :], bank[n % 4][:], ACT.Copy, scale=head_gain[:, l, k:k + 1])\
                        .then_inc(h_hi_done.sem, 1)

                with act.Fori(0, DT // 2) as j:
                    project(N_OUT, DT, 3 * l + 2, j, 1, (UP_W, UP_W))
                ffn(1, N_UP2, N_DN2, 2 * DT, 3 * l + 3, 0)
            root(LAYERS, 0)

        @block.vector
        def _(dve):
            tt, ts, stt = nc.vector.tensor_tensor, nc.vector.tensor_scalar, nc.vector.scalar_tensor_tensor
            steps = Steps(dve, dve_step.sem)
            dve.sem_inc(w_lo_done.sem, 2)
            dve.sem_inc(sq_added.sem, 2)
            dve.sem_inc(resid_ready.sem, 2)
            dve.sem_inc(att_scored.sem, 4)
            dve.sem_inc(ml_w_done.sem, 2)
            dve.sem_inc(g_scaled_done.sem, 1)
            dve.sem_inc(u_scaled_done.sem, 1)
            dve.sem_inc(acc_taken.sem, 1)
            dve.wait_ge(consts_loaded.sem, 16 * CONST_LOADS)
            dve.wait_ge(pool_consts.sem, POOL_CONSTS)
            dve.wait_ge(x_loaded.sem, 16)
            nc.vector.memset(halves[0:HD, 0:HD], 1.0)
            nc.vector.memset(halves[HD:P, HD:P], 1.0).then_inc(dve_consts.sem, 1)
            for h in range(HEADS):
                ts(cmp_bias[:, h % 2, :, h // 2, :], cmp_bias[:, h % 2, :, h // 2, :], neg_slope[:, h:h + 1], None, ALU.mult)

            def flat(t, m):
                return t[:, bass.ds(m, 1), :].rearrange("p a s -> p (a s)")

            def split_lo(l, n, slot, width):
                dve.wait_ge(w_hi_done.sem, w_hi_done.at(l, n + 1))
                tt(w_lo[slot][:, 0:width], raw[slot][:, 0:width], w_hi[slot][:, 0:width].bitcast(F32), ALU.subtract)\
                    .then_inc(w_lo_done.sem, 1)

            def norm_low(l, r, m, q):
                dve.wait_ge(x_hi_done.sem, x_hi_done.at(l, r + m + 1))
                stt(flat(x_lo, m), flat(resid, m), gains[:, q, bass.ds(m, 1)], flat(x_hi, m).bitcast(F32),
                    ALU.mult, ALU.subtract).then_inc(x_lo_done.sem, 1)

            def norm_add(l, r, m, slot):
                dve.wait_ge(sq_ready.sem, sq_ready.at(l, r + m + 1))
                dve.wait_ge(sq_added.sem, sq_added.at(l, r + m))
                tt(sumsq[:], sumsq[:], sq[:, slot, :], ALU.add).then_inc(sq_added.sem, 1)

            def norm_finish(l, q):
                dve.wait_ge(norm_sum.sem, norm_sum.at(l, q + 1))
                ts(mean_sq[:], bank[6][:], 1.0 / (DT * P), EPS, ALU.mult, ALU.add).then_inc(mean_ready.sem, 1)
                dve.wait_ge(root_ready.sem, root_ready.at(l, q + 1))
                nc.vector.reciprocal(rstd[:], mean_sq[:]).then_inc(rstd_ready.sem, 1)
                dve.wait_ge(rstd_ready.sem, rstd_ready.at(l, q + 1))

            steps.done(nc.vector.memset(sumsq[:], 0.0)).then_inc(waits_met.sem, 1)
            for m in range(DT):
                norm_low(0, -DT, m, 0)
                norm_add(0, -DT, m, m % 2)
            before = steps.n

            with dve.Fori(0, LAYERS) as l:
                steps.base, steps.n = l * DVE_STEPS + before, 0

                def up(f, n_up, m, width, first=False):
                    n = n_up + 2 * m
                    if first:
                        split_lo(l, n + 2, 0, width)
                        norm_finish(l, 2 * f)
                    dve.wait_ge(chunk_done.sem, chunk_done.at(l, n + 1))
                    tt(g_scaled[:], bank[0][:], rstd[:], ALU.mult).then_inc(g_scaled_done.sem, 1)
                    if not first:
                        split_lo(l, n + 2, 0, width)
                    dve.wait_ge(chunk_done.sem, chunk_done.at(l, n + 2))
                    tt(u_scaled[:], bank[1][:], rstd[:], ALU.mult).then_inc(u_scaled_done.sem, 1)
                    split_lo(l, n + 3, 1, width)
                    dve.wait_ge(silu_done.sem, silu_done.at(l, f * FT + m + 1))
                    dve.wait_ge(u_scaled_done.sem, u_scaled_done.at(l, f * FT + m + 1))
                    tt(hidden[:], g_silu[:], u_scaled[:], ALU.mult).then_inc(hidden_ready.sem, 1)
                    dve.wait_ge(hidden_hi.sem, hidden_hi.at(l, f * FT + m + 1))
                    tt(flat(hid_lo, m), hidden[:], flat(hid_hi, m).bitcast(F32), ALU.subtract)\
                        .then_inc(hidden_lo.sem, 1)

                def project(n0, r, q, j, chunks, factor, width):
                    for i in range(2):
                        m = 2 * j + i
                        first_n = n0 + 2 * chunks * j + i * chunks
                        if chunks == 2 and width[i]:
                            split_lo(l, first_n + 2, 0, width[i])
                        dve.wait_ge(chunk_done.sem, chunk_done.at(l, first_n + chunks))
                        stt(flat(resid, m), bank[4 + i][:], factor, flat(resid, m), ALU.mult, ALU.add)\
                            .then_inc(resid_ready.sem, 1)
                        if chunks == 1:
                            split_lo(l, first_n + 2, i, width[i])
                        elif width[i]:
                            split_lo(l, first_n + 3, 1, width[i])
                        norm_low(l, r, m, q)
                        norm_add(l, r, m, i)

                def ffn(f, n_up, n_down, r, q, next_width):
                    up(f, n_up, 0, UP_W, True)
                    with dve.Fori(1, FT - 1) as m:
                        up(f, n_up, m, UP_W)
                    up(f, n_up, FT - 1, DOWN_W)
                    steps.done(nc.vector.memset(sumsq[:], 0.0)).then_inc(waits_met.sem, 1)
                    with dve.Fori(0, DT // 2 - 1) as j:
                        project(n_down, r, q, j, 2, 0.5, (DOWN_W, DOWN_W))
                    project(n_down, r, q, DT // 2 - 1, 2, 0.5, (DOWN_W, next_width))

                for s in range(2):
                    split_lo(l, s, s, UP_W)
                ffn(0, N_UP1, N_DN1, 0, 3 * l + 1, UP_W)

                def take_u(m, i, n):
                    dve.wait_ge(chunk_done.sem, chunk_done.at(l, n + 1))
                    tt(flat(U, m), bank[2 + i][:], rstd[:], ALU.mult).then_inc(u_done.sem, 1)

                split_lo(l, N_WIN + 2, 0, UP_W)
                norm_finish(l, 1)
                take_u(0, 0, N_WIN)
                take_u(1, 1, N_WIN + 1)
                split_lo(l, N_WIN + 3, 1, UP_W)
                with dve.Fori(1, WIN_TILES // 2 - 1) as j:
                    for i in range(2):
                        take_u(2 * j + i, i, N_WIN + 2 * j + i)
                        split_lo(l, N_WIN + 2 * j + i + 2, i, UP_W)
                for i in range(2):
                    take_u(WIN_TILES - 2 + i, i, N_TM - 2 + i)
                    split_lo(l, N_TM + i, i, TM_W)
                for k in range(DT):
                    split_lo(l, N_TM + k + 2, k % 2, TM_W if k < DT - 2 else UP_W)

                dve.wait_ge(u_done.sem, u_done.at(l, WIN_TILES))
                for par in range(2):
                    h = slice(HD * par, HD * par + HD)
                    nc.vector.tensor_copy(gate_bd[h, :, h], gate_w[h, l, :, :])
                nc.vector.tensor_copy(w2cur[:], cmp_w2[:, l, :, :, :]).then_inc(layer_w_ready.sem, 1)
                for par in range(2):
                    for g in range(2):
                        src = U[HD * g:HD * g + HD, U_VC, :]
                        for pairs, view in block_halves(src, par):
                            nc.vector.tensor_copy(zc[1][HD * par:HD * par + HD, pairs, g * NCMP:(g + 1) * NCMP], view)
                nc.vector.tensor_copy(zc[1][:, :, 62], cmp_pos[:, l, 1, :]).then_inc(zc_ready[1].sem, 1)
                nc.vector.memset(v_aug[:, :, :, HD:HD + 1], 1.0)
                dve.wait_ge(chunk_done.sem, chunk_done.at(l, N_OUT))
                for c in range(2):
                    par = lru_par[:, l, c, :]
                    steps.done(ts(lru[0][:, c, :], U[:, U_XR + c, :], par[:, 3:4], par[:, 4:5], ALU.mult, ALU.add))
                    for tap in (2, 1, 0):
                        lag = 3 - tap
                        ins = stt(lru[0][:, c, lag:S], U[:, U_XR + c, 0:S - lag], par[:, tap:tap + 1],
                                  lru[0][:, c, lag:S], ALU.mult, ALU.add)
                        if tap:
                            steps.done(ins)
                    ins.then_inc(conv_done.sem, 1)
                    dve.wait_ge(conv_done.sem, conv_done.at(l, c + 1))
                stt(spt[:, 0, :], lru_par[:, l, :, 7], -1.0, lru_par[:, l, :, 7], ALU.mult, ALU.max).then_inc(sp_arg.sem, 1)
                dve.wait_ge(cmp_kv_ready.sem, cmp_kv_ready.at(l, 1))
                nc.vector.tensor_copy(kcT[:, :, 0:NCMP], bank[3][:, 0:64].rearrange("p (g n) -> p g n", g=2)[:, :, 0:NCMP])
                for j in range(4):
                    h = slice(32 * j, 32 * j + NCMP)
                    ins = nc.vector.tensor_copy(vc_bd[h, HD * j:HD * (j + 1)], bank[5][h, HD * j:HD * (j + 1)])
                ins.then_inc(cmp_kv_done.sem, 1)
                for half in range(2):
                    dve.wait_ge(cmp_s_ready.sem, cmp_s_ready.at(l, half + 1))
                    ins = stt(T[:, half, :], bank[2 + half][:], HD ** -0.5,
                              cmp_bias[:, half, :, :, :].rearrange("p t h n -> p (t h n)"),
                              ALU.mult, ALU.add)
                steps.done(ins)
                t4 = T[:].rearrange("p a (b n) -> p (a b) n", n=32)
                steps.done(nc.vector.tensor_reduce(cmp_max[:], t4, AX_X, ALU.max))
                tt(t4, t4, wide(cmp_max[:], 32), ALU.subtract).then_inc(cmp_t_done.sem, 1)
                dve.wait_ge(if_t_ready.sem, if_t_ready.at(l, 1))
                ts(rows[0][:], bank[6][0:4, :], ml_bias[:, l, 0:1], None, ALU.add)
                steps.done(ts(rows[1][:], bank[7][0:4, :], ml_bias[:, l, 1:2], None, ALU.add))
                stt(rows[2][:], rows[1][:], -1.0, rows[1][:], ALU.mult, ALU.max).then_inc(ml_abs.sem, 1)
                dve.wait_ge(sp_exp.sem, sp_exp.at(l, 1))
                ts(spt[:, 2, :], spt[:, 1, :], 1.0, None, ALU.add).then_inc(sp_arg.sem, 1)
                dve.wait_ge(ml_exp.sem, ml_exp.at(l, 1))
                ts(rows[3][:], rows[2][:], 1.0, None, ALU.add).then_inc(ml_arg.sem, 1)
                dve.wait_ge(cmp_p_done.sem, cmp_p_done.at(l, 1))
                p4 = PR[:].rearrange("p a (b n) -> p (a b) n", n=32)
                steps.done(nc.vector.tensor_reduce(cmp_sum[:], p4, AX_X, ALU.add))
                for par in range(2):
                    pt4 = PR[:, par, :].rearrange("p (t h n) -> p t h n", t=ST, n=32)
                    ins = tt(pt4, pt4, cmp_mask[:].unsqueeze(2).to_broadcast([P, ST, 4, 32]), ALU.mult)
                ins.then_inc(cmp_pm_done.sem, 1)

                def log1p(e, u, ln, a, b, arg_sem, arg_count, ln_sem, ln_count):
                    dve.wait_ge(arg_sem, arg_count)
                    steps.done(ts(a, u, -1.0, None, ALU.add))
                    steps.done(tt(a, e, a, ALU.subtract))
                    steps.done(nc.vector.reciprocal(b, u))
                    steps.done(tt(a, a, b, ALU.mult))
                    dve.wait_ge(ln_sem, ln_count)
                    steps.done(tt(ln, ln, a, ALU.add))

                log1p(spt[:, 1, :], spt[:, 2, :], spt[:, 3, :], spt[:, 4, :], spt[:, 5, :],
                      sp_arg.sem, sp_arg.at(l, 2), sp_ln.sem, sp_ln.at(l, 1))
                steps.done(ts(spt[:, 4, :], lru_par[:, l, :, 7], -1.0, 0.0, ALU.mult, ALU.max))
                steps.done(tt(spt[:, 4, :], spt[:, 4, :], spt[:, 3, :], ALU.add))
                ts(sp4[:], spt[:, 4, :], 4.0, None, ALU.mult).then_inc(sp_done.sem, 1)
                log1p(rows[2][:], rows[3][:], rows[4][:], rows[5][:], rows[2][:],
                      ml_arg.sem, ml_arg.at(l, 1), ml_ln.sem, ml_ln.at(l, 1))
                steps.done(ts(rows[1][:], rows[1][:], 0.0, None, ALU.min))
                steps.done(tt(rows[1][:], rows[1][:], rows[4][:], ALU.subtract))
                steps.done(nc.vector.memset(rows[5][:], 1.0))
                steps.done(nc.vector.tensor_tensor_scan(rows[2][:], rows[5][:], rows[1][:], 0.0, ALU.mult, ALU.add))
                steps.done(tt(rows[3][:], rows[0][:], rows[2][:], ALU.subtract))
                steps.done(nc.vector.tensor_tensor_scan(rows[4][:], rows[3][:], rows[3][:], 0.0, ALU.max, ALU.max))
                steps.done(tt(rows[5][:], rows[2][:], rows[4][:], ALU.add))
                ts(rows[4][:], rows[4][:], -1.0, None, ALU.mult).then_inc(ml_rows.sem, 1)

                steps.done(nc.vector.reciprocal(cmp_sum[:], cmp_sum[:]))
                c3 = cmp_sum[:].rearrange("p (a t h) -> p a t h", a=2, t=ST)
                g4 = gates[:].rearrange("p t (h a c) -> p a t h c", a=2, c=3)
                dve.wait_ge(tm_taken.sem, tm_taken.at(l, 1))
                steps.done(tt(c3, c3, g4[:, :, :, :, 0], ALU.mult))
                dve.wait_ge(cmp_o_ready.sem, cmp_o_ready.at(l, 1))
                for t in range(ST):
                    ins = tt(o_all[:, t, 0:HEADS, :].rearrange("p (h a) d -> p a h d", a=2),
                             bank[2 + t][:].rearrange("p (a h d) -> p a h d", a=2, h=4), wide(c3[:, :, t, :], HD),
                             ALU.mult)
                ins.then_inc(cmp_o_done.sem, 1)

                dve.wait_ge(lru_tanh.sem, lru_tanh.at(l, 1))
                tt(lru[2][:], lru[2][:], lru[0][:], ALU.mult)
                steps.done(ts(lru[3][:], lru[1][:], 1.0, None, ALU.add))
                steps.done(nc.vector.reciprocal(lru[3][:], lru[3][:]))
                ts(lru[4][:], lru[1][:], -1.0, 1.0, ALU.mult, ALU.add).then_inc(lru_om.sem, 1)
                dve.wait_ge(lru_om.sem, lru_om.at(l, 1))
                steps.done(tt(lru[4][:], lru[4][:], lru[3][:], ALU.mult))
                dve.wait_ge(lru_sqrt.sem, lru_sqrt.at(l, 1))
                for c in range(2):
                    ins = stt(lru[1][:, c, :], lru[1][:, c, :], 2.0, lru[3][:, c, :], ALU.mult, ALU.mult)
                steps.done(ins)
                steps.done(tt(lru[1][:], lru[1][:], lru[2][:], ALU.mult))
                for c in range(2):
                    ins = nc.vector.tensor_tensor_scan(lru[3][:, c, :], lru[4][:, c, :], lru[1][:, c, :], 0.0,
                                                       ALU.mult, ALU.add)
                steps.done(ins)
                dve.wait_ge(lru_gelu.sem, lru_gelu.at(l, 1))
                tt(lru[0][:], lru[3][:], U[:, U_GR:U_GR + 2, :], ALU.mult).then_inc(lru_out.sem, 1)
                dve.wait_ge(lru_ms_ready.sem, lru_ms_ready.at(l, 1))
                for c in range(2):
                    ins = ts(lru[3][:, c, :], bank[c][:], 1.0 / HD, EPS, ALU.mult, ALU.add)
                ins.then_inc(lru_ms_done.sem, 1)
                dve.wait_ge(lru_root.sem, lru_root.at(l, 1))
                steps.done(nc.vector.reciprocal(lru[3][:], lru[3][:]))
                for c in range(2):
                    ins = stt(lru[2][:, c, :], lru[0][:, c, :], head_gain[:, l, 4 + c:5 + c], lru[3][:, c, :],
                              ALU.mult, ALU.mult)
                ins.then_inc(lru_normed.sem, 1)

                dve.wait_ge(ml_cols_ready.sem, ml_cols_ready.at(l, 1))
                nc.vector.tensor_copy(bcol[:], bank[6][:, 0:32].rearrange("p (t c) -> p t c", t=ST))\
                    .then_inc(ml_cols_done.sem, 1)
                dve.wait_ge(ml_cols_done.sem, ml_cols_done.at(l, 1))

                def exponent(n):
                    h, j = n // ST, n % ST
                    if j == 0:
                        dve.wait_ge(ml_m_ready.sem, ml_m_ready.at(l, h + 1))
                    ts(ml_e[:, n % 2, 0:S - j * P], bank[6][:, j * P:S], bcol[:, j, h:h + 1], 0.0, ALU.add, ALU.min)\
                        .then_inc(ml_d_done.sem, 1)

                exponent(0)
                for n in range(16):
                    if n + 1 < 16:
                        exponent(n + 1)
                    w = S - (n % ST) * P
                    dve.wait_ge(ml_e_done.sem, ml_e_done.at(l, n + 1))
                    dve.wait_ge(ml_s_ready.sem, ml_s_ready.at(l, n + 1))
                    dve.wait_ge(ml_pv.sem, ml_pv.at(l, n - 1))
                    steps.done(stt(ml_w[:, n % 2, 0:w], ml_e[:, n % 2, 0:w], HD ** -0.5, bank[n % 2][:, 0:w],
                                   ALU.mult, ALU.mult))
                    tt(ml_w[:, n % 2, 0:P], ml_w[:, n % 2, 0:P], causal[:], ALU.mult).then_inc(ml_w_done.sem, 1)
                dve.wait_ge(ml_pv.sem, ml_pv.at(l, 16))
                dve.wait_ge(ml_em.sem, ml_em.at(l, 1))
                acc = [bank[2 + t][:, 0:4 * (HD + 1)].rearrange("p (h d) -> p h d", h=4) for t in range(ST)]
                for t in range(ST):
                    ins = nc.vector.tensor_copy(den[:, t, :], acc[t][:, :, HD])
                steps.done(ins)
                steps.done(stt(den[:], den[:], -1.0, den[:], ALU.mult, ALU.max))
                steps.done(tt(den[:], den[:], em[:], ALU.max))
                steps.done(nc.vector.reciprocal(den[:], den[:]))
                for t in range(ST):
                    ins = tt(o_all[:, t, HEADS:12, :], acc[t][:, :, 0:HD], wide(den[:, t, :], HD), ALU.mult)
                ins.then_inc(ml_o_done.sem, 1)
                dve.wait_ge(ml_o_done.sem, ml_o_done.at(l, 1))
                steps.done(tt(o_all[:, :, HEADS:12, :], o_all[:, :, HEADS:12, :],
                              o_sig[:].rearrange("p t (h d) -> p t h d", h=4), ALU.mult)).then_inc(waits_met.sem, 1)

                done_before = steps.n
                PASS_STEPS = 16 + 4
                with dve.Fori(0, 2) as b:
                    with dve.Fori(0, 2) as g:
                        kv = b * 2 + g
                        pas = l * 64 + kv * 16
                        steps.base, steps.n = l * DVE_STEPS + before + kv * PASS_STEPS, done_before
                        for u in range(16):
                            h, i = u // ST, u % ST
                            w = (i + 1) * P
                            dve.wait_ge(att_s_ready.sem, pas + u + 17)
                            dve.wait_ge(att_exp_done.sem, pas + u + 1)
                            steps.done(stt(T[:, u % 2, 0:w], dist[:, S - w:S], neg_slope[:, bass.ds(g * HPG + h, 1)],
                                           bank[u % 4][:, 0:w], ALU.mult, ALU.add))
                            nc.vector.tensor_reduce(n_max[:, u:u + 1], T[:, u % 2, 0:w], AX_X, ALU.max, negate=True)\
                                .then_inc(att_scored.sem, 1)
                        dve.wait_ge(att_exp_done.sem, pas + 18)
                        steps.done(nc.vector.reciprocal(rec[:], sums[:, kv, :]))
                        gv = gates[:].rearrange("p t (h c) -> p c h t", c=3)
                        gv = gv[:, bass.ds(b + 1, 1), bass.ds(g * HPG, HPG), :].rearrange("p a h t -> p (a h) t")
                        steps.done(tt(coef[:].rearrange("p (h t) -> p h t", h=HPG), rec[:].rearrange("p (h t) -> p h t", h=HPG),
                                      gv, ALU.mult))
                        dve.wait_ge(att_pv_ready.sem, pas + 18)
                        for n in range(2):
                            ins = tt(att_o[:, n, :].rearrange("p (u d) -> p u d", u=8),
                                     bank[6 + n][:].rearrange("p (u d) -> p u d", u=8), wide(coef[:, 8 * n:8 * n + 8], HD),
                                     ALU.mult)
                        steps.done(ins)
                        for n in range(2):
                            o = o_all[:].rearrange("p t h d -> p h t d")[:, bass.ds(g * HPG + 2 * n, 2), :, :]
                            ins = tt(o, o, att_o[:, n, :].rearrange("p (h t d) -> p h t d", h=2, t=ST), ALU.add)
                            if n == 0:
                                steps.done(ins)
                        ins.then_inc(acc_taken.sem, 1)
                        dve.wait_ge(acc_taken.sem, l * 4 + kv + 2)
                        assert steps.n == done_before + PASS_STEPS
                steps.base, steps.n = l * DVE_STEPS + before, done_before + 4 * PASS_STEPS

                dve.wait_ge(o_sq_done.sem, o_sq_done.at(l, 1))
                steps.done(nc.vector.tensor_reduce(h_ss[:], o_sq[:], AX_X, ALU.add))
                ts(h_ms[:], h_ss[:], 1.0 / HD, EPS, ALU.mult, ALU.add).then_inc(o_ms_done.sem, 1)
                dve.wait_ge(o_root.sem, o_root.at(l, 1))
                steps.done(nc.vector.reciprocal(h_rs[:], h_ms[:]))
                o3 = o_all[:].rearrange("p t h d -> p (t h) d")
                tt(o3, o3, wide(h_rs[:], HD), ALU.mult).then_inc(o_normed.sem, 1)
                for c in range(2):
                    dve.wait_ge(lru_hi_done.sem, lru_hi_done.at(l, c + 1))
                    tt(h_lo[:, 4 + c, :], lru[2][:, c, :], h_hi[:, 4 + c, :].bitcast(F32), ALU.subtract)\
                        .then_inc(lru_lo_done.sem, 1)
                for n in range(6):
                    k = n if n < 4 else n + 2
                    dve.wait_ge(h_hi_done.sem, h_hi_done.at(l, n + 1))
                    stt(h_lo[:, k, :], bank[n % 4][:], head_gain[:, l, k:k + 1], h_hi[:, k, :].bitcast(F32),
                        ALU.mult, ALU.subtract).then_inc(h_lo_done.sem, 1)
                steps.done(nc.vector.memset(sumsq[:], 0.0)).then_inc(waits_met.sem, 1)
                with dve.Fori(0, DT // 2) as j:
                    project(N_OUT, DT, 3 * l + 2, j, 1, 1.0, (UP_W, UP_W))
                ffn(1, N_UP2, N_DN2, 2 * DT, 3 * l + 3, 0)
                assert steps.n == DVE_STEPS, steps.n
            norm_finish(LAYERS, 0)
            for m in range(DT):
                stt(resid[:, m, :], resid[:, m, :], gains[:, 3 * LAYERS, m:m + 1], rstd[:], ALU.mult, ALU.mult)\
                    .then_inc(out_ready.sem, 1)


MIX_BYTES, SMALL_BYTES = 98368, 5120
DVE_STEPS = 144
CONST_LOADS = 7


def wide(ap, n):
    return ap.unsqueeze(len(ap.shape)).to_broadcast([*ap.shape, n])


def block_halves(src, par):
    v = src.rearrange("p (n c two) -> p two c n", two=2, c=8)[:, par, :, :]
    return (slice(0, 8), v[:, :, 0:NCMP]), (slice(8, 16), v[:, :, 1:NCMP + 1])


def kernel(**inputs):
    import numpy as np
    import concourse.bacc as bacc
    from concourse.bass_utils import run_bass_kernel_spmd

    a = {k: np.asarray(v) for k, v in inputs.items()}
    L = LAYERS

    def tiles(w, kt, mt):
        return w.reshape(L, kt, P, mt, P).transpose(0, 3, 2, 1, 4).reshape(L, mt, P, kt * P)

    def down(w):
        w = w.reshape(L, 2, FH, P, DT, P).transpose(0, 4, 1, 3, 2, 5)
        return w.reshape(L, DT, 2, P, FH * P)

    def up(w1, w3):
        return np.stack([tiles(w1, DT, FT), tiles(w3, DT, FT)], axis=2)

    w = a["w_in"]
    fm = np.concatenate([w[:, :, 0:768], w[:, :, 768:896], w[:, :, 1024:1152], w[:, :, 1304:2328]], axis=2)
    tm = np.concatenate([w[:, :, 896:1024], w[:, :, 1152:1280], w[:, :, 1280:1304], w[:, :, 2584:2592],
                         w[:, :, 2328:2584], w[:, :, 2592:2848]], axis=2)

    def cols(v, n):
        return v.reshape(*v.shape[:-1], n, P)

    gains = np.stack([a["ffn1_norm"], a["mix_norm"], a["ffn2_norm"]], axis=1).reshape(3 * L, 1024)
    gains = cols(np.concatenate([gains, a["final_norm"][None]], axis=0), DT).transpose(2, 0, 1)
    lru = [cols(a["lru_conv_w"], 2)[:, t] for t in range(4)] +           [cols(a[k].reshape(L, 256), 2) for k in ("lru_conv_b", "lru_b_a", "lru_b_x", "lru_lambda")]
    gate = np.stack([a["lru_w_a"], a["lru_w_x"]], axis=1).reshape(L, 2, 2, 2, HD, HD)
    arrays = {
        "x": a["x"][0].T.reshape(DT, P, S).transpose(1, 0, 2),
        "up1": up(a["ffn1_w1"], a["ffn1_w3"]), "down1": down(a["ffn1_w2"]),
        "up2": up(a["ffn2_w1"], a["ffn2_w3"]), "down2": down(a["ffn2_w2"]),
        "w_in": tiles(fm, DT, WIN_TILES), "w_tm": tm.reshape(L, DT, P, TM_W),
        "w_out": tiles(a["w_out"], DT, DT),
        "cmp_w1": np.stack([a["nsa_cmp_w1_k"], a["nsa_cmp_w1_v"]], axis=1).reshape(L, 2, CP, P, 256)
                    .transpose(0, 1, 3, 2, 4),
        "gains": gains,
        "head_gain": cols(a["head_norm"].reshape(L, 1024), DT).transpose(2, 0, 1),
        "lru_par": np.stack(lru, axis=-1).transpose(2, 0, 1, 3),
        "gate_w": gate.transpose(3, 4, 0, 1, 2, 5).reshape(P, L, 4, HD),
        "cmp_pos": np.stack([a["nsa_cmp_pos_k"], a["nsa_cmp_pos_v"]], axis=1).reshape(L, 2, CP, P)
                     .transpose(3, 0, 1, 2),
        "cmp_w2": np.stack([a["nsa_cmp_w2_k"], a["nsa_cmp_w2_v"]], axis=1).reshape(L, 2, 2, P, HD)
                    .transpose(3, 0, 1, 2, 4),
        "ml_bias": np.stack([a["ml_b_i"], a["ml_b_f"]], axis=-1).transpose(1, 0, 2),
    }
    arrays = {k: np.ascontiguousarray(v) for k, v in arrays.items()}
    nc = bacc.Bacc("TRN2", target_bir_lowering=False, num_devices=1)
    d = {k: nc.dram_tensor(f"{k}_dram", v.shape, F32, kind="ExternalInput").ap() for k, v in arrays.items()}
    out = nc.dram_tensor("out_dram", (P, DT, S), F32, kind="ExternalOutput").ap()
    build(nc, d, out)
    got = run_bass_kernel_spmd(nc, [{f"{k}_dram": v for k, v in arrays.items()}], core_ids=[0]).results[0]["out_dram"]
    return np.ascontiguousarray(got.transpose(2, 1, 0)).reshape(1, S, 1024)
```

```python
from contextlib import ExitStack

import concourse.bass as bass
from concourse import mybir

F32 = mybir.dt.float32
F32R = mybir.dt.float32r
ALU = mybir.AluOpType
ACT = mybir.ActivationFunctionType
AX_X = mybir.AxisListType.X

P = 128
LAYERS = 2
S = 512
ST = S // P
DT = 1024 // P
FT = 2816 // P
FH = FT // 2
HD = 64
EPS = 1e-6
HEADS = 8
HPG = 4
NCMP = (S - 32) // 16 + 1
CP = 16
MASKED = 1e33
WIN_TILES = 16
U_XR, U_GR, U_Q, U_KC, U_VC, U_KS, U_QM, U_KM = 0, 2, 4, 8, 9, 10, 12, 14
TM_A, TM_B = 288, 512
UP_W, DOWN_W, TM_W = DT * P, FH * P, TM_A + TM_B
N_UP1, N_DN1, N_WIN, N_TM, N_OUT, N_UP2, N_DN2, N_CHUNKS = 0, 44, 60, 76, 84, 92, 136, 152


class Signal:

    def __init__(self, sem, before, per_layer):
        self.sem, self.before, self.per_layer = sem, before, per_layer

    def at(self, layer, count):
        return layer * self.per_layer + self.before + count


class Steps:

    def __init__(self, eng, sem):
        self.eng, self.sem, self.base, self.n = eng, sem, 0, 0

    def mark(self, ins):
        ins.then_inc(self.sem, 1)
        self.n += 1
        return self.base + self.n

    def done(self, ins):
        return self.eng.wait_ge(self.sem, self.mark(ins))


def build(nc, d, out):
    ctx = ExitStack()
    with ctx:
        enter = ctx.enter_context

        def sb(name, shape, dt=F32):
            return enter(nc.sbuf_tensor(name, shape, dt))

        resid = sb("resid", [P, DT, S])
        raw = [sb(f"raw{s}", [P, DOWN_W]) for s in range(2)]
        w_hi = [sb(f"w_hi{s}", [P, DOWN_W], F32R) for s in range(2)]
        w_lo = [sb(f"w_lo{s}", [P, DOWN_W], F32R) for s in range(2)]
        rstd = sb("rstd", [P, S])
        sumsq = sb("sumsq", [P, S])
        mean_sq = sumsq
        ones = sb("ones", [P, P])
        ident = sb("ident", [P, P])
        halves = sb("halves", [P, P])
        causal = sb("causal", [P, P])
        dist = sb("dist", [P, S])
        cmp_bias = sb("cmp_bias", [P, 2, ST, 4, 32])
        cmp_mask = sb("cmp_mask", [P, ST, 32])
        neg_slope = sb("neg_slope", [P, HEADS])
        pick = sb("pick", [4, 4, P])
        gains = sb("gains", [P, 7, DT])
        head_gain = sb("head_gain", [P, LAYERS, DT])
        lru_par = sb("lru_par", [P, LAYERS, 2, 8])
        gate_w = sb("gate_w", [P, LAYERS, 4, HD])
        gate_bd = sb("gate_bd", [P, 4, P])
        cmp_pos = sb("cmp_pos", [P, LAYERS, 2, 2, CP])
        cmp_w2 = sb("cmp_w2", [P, LAYERS, 2, 2, HD])
        w2cur = sb("w2cur", [P, 2, 2, HD])
        ml_bias = sb("ml_bias", [4, LAYERS, 2])
        kcT = sb("kcT", [P, 2, 32])
        vc_bd = sb("vc_bd", [P, 256])

        top = [nc.sbuf_base]

        def region(size):
            at = (top[0] + 63) // 64 * 64
            top[0] = at + size
            return at

        def at(name, offset, shape, dt=F32):
            return nc.alloc_sbuf_tensor_at(name, shape, dt, offset=offset)

        x_area = region(2 * DT * S * 4)
        x_hi = at("x_hi", x_area, [P, DT, S], F32R)
        x_lo = at("x_lo", x_area + DT * S * 4, [P, DT, S], F32R)
        rows = [at(f"row{i}", x_area + i * 2048, [4, S]) for i in range(6)]
        k_hi = at("k_hi", x_area + 12288, [P, 4, S], F32R)
        k_lo = at("k_lo", x_area + 20480, [P, 4, S], F32R)

        mix = region(MIX_BYTES)
        hid_hi = at("hid_hi", mix, [P, FT, S], F32R)
        hid_lo = at("hid_lo", mix + FT * S * 4, [P, FT, S], F32R)
        tmp0 = mix + 2 * FT * S * 4
        g_scaled = at("g_scaled", tmp0, [P, S])
        g_silu = at("g_silu", tmp0 + 2048, [P, S])
        u_scaled = at("u_scaled", tmp0 + 4096, [P, S])
        sq = at("sq", tmp0 + 2048, [P, 2, S])
        hidden = at("hidden", tmp0 + 6144, [P, S])

        U = at("U", mix, [P, WIN_TILES, S])
        h_hi = at("h_hi", mix, [P, DT, S], F32R)
        h_lo = at("h_lo", mix + 16384, [P, DT, S], F32R)
        m1 = mix + 32768
        r1 = m1
        lru = [at(f"lru{i}", r1 + i * 4096, [P, 2, S]) for i in range(5)]
        cmp_w1 = [at(f"cmp_w1_{i}", r1 + i * 16384, [P, CP, 256]) for i in range(2)]
        T = at("T", r1, [P, 2, S])
        PR = at("PR", r1 + 4096, [P, 2, S])
        PT = at("PT", r1 + 8192, [P, 2, S])
        q_head = [at(f"q_head{i}", r1 + 12288 + i * 2048, [P, S], F32R) for i in range(4)]
        ml_e = at("ml_e", r1 + 20480, [P, 2, S])
        ml_w = at("ml_w", r1 + 24576, [P, 2, S])
        att_o = at("att_o", r1 + 28672, [P, 2, S])
        cmp_act = at("cmp_act", r1 + 28672, [2 * NCMP, 2, 256])
        o_sq = at("o_sq", r1, [P, ST * 12, HD])
        m2 = m1 + 32768
        q_hi = at("q_hi", m2, [P, HEADS // 2, S], F32R)
        q_lo = at("q_lo", mix + U_Q * S * 4, [P, HEADS // 2, S], F32R)
        v_all = at("v_all", m2 + 8192, [P, 4, ST, HD])
        v_aug = at("v_aug", m2 + 12288, [P, ST, 4, HD + 1])
        o_sig = at("o_sig", m2 + 16448, [P, ST, 256])
        o_all = at("o_all", m2 + 20544, [P, ST, 12, HD])
        zc = [at(f"zc{i}", m2 + 20544 + i * 4096, [P, CP, 2 * NCMP]) for i in range(2)]
        assert m2 + 20544 + 12288 <= mix + MIX_BYTES
        assert tmp0 + 8192 <= mix + MIX_BYTES
        small = region(SMALL_BYTES)

        def sm(name, shape, state=[0]):
            n = 4
            for k in shape[1:]:
                n *= k
            t = at(name, small + state[0], shape)
            state[0] += (n + 31) // 32 * 32
            assert state[0] <= SMALL_BYTES
            return t

        rcol = sm("rcol", [P, ST])
        gates = sm("gates", [P, ST, 24])
        ifcol = sm("ifcol", [P, ST, 8])
        cmp_hid = sm("cmp_hid", [P, 2, 2, 62])
        cmp_max = sm("cmp_max", [P, 32])
        cmp_sum = sm("cmp_sum", [P, 32])
        n_max = sm("n_max", [P, 16])
        sums = sm("sums", [P, 4, 16])
        rec = sm("rec", [P, 16])
        coef = sm("coef", [P, 16])
        sp4 = sm("sp4", [P, 2])
        spt = sm("spt", [P, 6, 2])
        bcol = sm("bcol", [P, ST, 8])
        em = sm("em", [P, ST, 4])
        den = sm("den", [P, ST, 4])
        h_ss = sm("h_ss", [P, ST * 12])
        h_ms = sm("h_ms", [P, ST * 12])
        h_rs = sm("h_rs", [P, ST * 12])

        bank = [enter(nc.psum_tensor(f"bank{i}", [P, 512], F32)) for i in range(8)]

        def signal(name, per_layer, before=0):
            return Signal(enter(nc.semaphore(name)), before, per_layer)

        consts_loaded = signal("consts_loaded", 0)
        gains_loaded = signal("gains_loaded", 0)
        x_loaded = signal("x_loaded", 0)
        pool_consts = signal("pool_consts", 0)
        pool_zero = signal("pool_zero", 0)
        dve_consts = signal("dve_consts", 0)
        w_loaded = [signal(f"w_loaded{s}", 16 * N_CHUNKS // 2) for s in range(2)]
        w_hi_done = signal("w_hi_done", N_CHUNKS)
        w_lo_done = signal("w_lo_done", N_CHUNKS, 2)
        chunk_done = signal("chunk_done", N_CHUNKS, 2)
        resid_ready = signal("resid_ready", 24, 2)
        x_hi_done = signal("x_hi_done", 24, 8)
        x_lo_done = signal("x_lo_done", 24, 8)
        sq_ready = signal("sq_ready", 24, 8)
        sq_added = signal("sq_added", 24, 8 + 2)
        norm_sum = signal("norm_sum", 3)
        mean_ready = signal("mean_ready", 3)
        root_ready = signal("root_ready", 3)
        rstd_ready = signal("rstd_ready", 3)
        g_scaled_done = signal("g_scaled_done", 2 * FT, 1)
        silu_done = signal("silu_done", 2 * FT)
        u_scaled_done = signal("u_scaled_done", 2 * FT, 1)
        hidden_ready = signal("hidden_ready", 2 * FT)
        hidden_hi = signal("hidden_hi", 2 * FT)
        hidden_lo = signal("hidden_lo", 2 * FT)
        u_done = signal("u_done", WIN_TILES)
        rcol_ready = signal("rcol_ready", 1)
        rcol_done = signal("rcol_done", 1)
        tm_taken = signal("tm_taken", 1)
        tm_values_taken = signal("tm_values_taken", 1)
        o_sig_done = signal("o_sig_done", 1)
        cmp_w_loaded = [signal(f"cmp_w_loaded{i}", 4 * 16) for i in range(2)]
        layer_w_ready = signal("layer_w_ready", 1)
        k_hi_done = signal("k_hi_done", 4)
        k_lo_done = signal("k_lo_done", 4)
        q_hi_done = signal("q_hi_done", 1)
        q_lo_done = signal("q_lo_done", 1)
        zc_ready = [signal(f"zc_ready{i}", 1) for i in range(2)]
        cmp_h_ready = signal("cmp_h_ready", 1)
        cmp_act_done = signal("cmp_act_done", 1)
        cmp_t_ready = signal("cmp_t_ready", 1)
        cmp_hid_done = signal("cmp_hid_done", 1)
        cmp_kv_ready = signal("cmp_kv_ready", 1)
        cmp_kv_done = signal("cmp_kv_done", 1)
        cmp_s_ready = signal("cmp_s_ready", 2)
        cmp_t_done = signal("cmp_t_done", 1)
        cmp_p_done = signal("cmp_p_done", 1)
        cmp_pm_done = signal("cmp_pm_done", 1)
        cmp_tr_ready = signal("cmp_tr_ready", 1)
        cmp_pt_done = signal("cmp_pt_done", 1)
        cmp_o_ready = signal("cmp_o_ready", 1)
        cmp_o_done = signal("cmp_o_done", 1)
        conv_done = signal("conv_done", 2)
        lru_g_ready = signal("lru_g_ready", 2)
        lru_gates_done = signal("lru_gates_done", 2)
        sp_exp = signal("sp_exp", 1)
        sp_arg = signal("sp_arg", 2)
        sp_ln = signal("sp_ln", 1)
        sp_done = signal("sp_done", 1)
        lru_tanh = signal("lru_tanh", 1)
        lru_om = signal("lru_om", 1)
        lru_sqrt = signal("lru_sqrt", 1)
        lru_gelu = signal("lru_gelu", 1)
        lru_out = signal("lru_out", 1)
        lru_sq_done = signal("lru_sq_done", 1)
        lru_ms_ready = signal("lru_ms_ready", 1)
        lru_ms_done = signal("lru_ms_done", 1)
        lru_root = signal("lru_root", 1)
        lru_normed = signal("lru_normed", 1)
        lru_hi_done = signal("lru_hi_done", 2)
        lru_lo_done = signal("lru_lo_done", 2)
        q_loaded = [signal(f"q_loaded{i}", 4 * 32) for i in range(4)]
        att_s_ready = signal("att_s_ready", 64, 16)
        att_scored = signal("att_scored", 64, 4)
        att_exp_done = signal("att_exp_done", 64, 2)
        att_tr_ready = signal("att_tr_ready", 64, 2)
        att_copied = signal("att_copied", 64, 2)
        att_pv_ready = signal("att_pv_ready", 64, 2)
        acc_taken = signal("acc_taken", 4, 1)
        if_t_ready = signal("if_t_ready", 1)
        ml_abs = signal("ml_abs", 1)
        ml_exp = signal("ml_exp", 1)
        ml_arg = signal("ml_arg", 1)
        ml_ln = signal("ml_ln", 1)
        ml_rows = signal("ml_rows", 1)
        ml_cols_ready = signal("ml_cols_ready", 1)
        ml_cols_done = signal("ml_cols_done", 1)
        ml_em = signal("ml_em", 1)
        ml_m_ready = signal("ml_m_ready", 4)
        ml_d_done = signal("ml_d_done", 16, 0)
        ml_e_done = signal("ml_e_done", 16, 0)
        ml_s_ready = signal("ml_s_ready", 16)
        ml_w_done = signal("ml_w_done", 16, 2)
        ml_pv = signal("ml_pv", 16, 2)
        ml_o_done = signal("ml_o_done", 1)
        o_sq_done = signal("o_sq_done", 1)
        o_ms_done = signal("o_ms_done", 1)
        o_root = signal("o_root", 1)
        o_normed = signal("o_normed", 1)
        h_t_ready = signal("h_t_ready", 6)
        h_hi_done = signal("h_hi_done", 6)
        h_lo_done = signal("h_lo_done", 6, 0)
        dve_step = signal("dve_step", 0)
        waits_met = signal("waits_met", 0)
        out_ready = signal("out_ready", 0)
        out_stored = signal("out_stored", 0)

        def wait_alone(eng, sem, value):
            eng.wait_ge(sem, value).then_inc(waits_met.sem, 1)

        block = enter(nc.Block())

        @block.sync
        def _(sp):
            sp.dma_start(resid[:], d["x"]).then_inc(x_loaded.sem, 16)

            def stream(l, n, slot, src):
                sp.wait_ge(w_lo_done.sem, l * N_CHUNKS + n + 1)
                sp.dma_start(raw[slot][:, 0:src.shape[1]], src).then_inc(w_loaded[slot].sem, 16)

            with sp.Fori(0, LAYERS) as l:
                def ffn(up, down, n_up, n_down):
                    with sp.Fori(0, FT) as m:
                        for s in range(2):
                            stream(l, n_up + 2 * m + s, s, up[l, m, s])
                    with sp.Fori(0, DT) as m:
                        for s in range(2):
                            stream(l, n_down + 2 * m + s, s, down[l, m, s])

                ffn(d["up1"], d["down1"], N_UP1, N_DN1)
                with sp.Fori(0, WIN_TILES // 2) as j:
                    for s in range(2):
                        stream(l, N_WIN + 2 * j + s, s, d["w_in"][l, 2 * j + s])
                for k in range(DT):
                    stream(l, N_TM + k, k % 2, d["w_tm"][l, k])
                    if k == 0:
                        sp.wait_ge(lru_normed.sem, lru_normed.at(l, 1))
                    piece = slice(k % 4 * 4, k % 4 * 4 + 4)
                    sp.dma_start(cmp_w1[k // 4][:, piece, :], d["cmp_w1"][l, k // 4, :, piece, :])\
                        .then_inc(cmp_w_loaded[k // 4].sem, 16)
                for s in range(2):
                    stream(l, N_OUT + s, s, d["w_out"][l, s])
                with sp.Fori(1, DT // 2) as j:
                    for s in range(2):
                        stream(l, N_OUT + 2 * j + s, s, d["w_out"][l, 2 * j + s])
                ffn(d["up2"], d["down2"], N_UP2, N_DN2)
            for m in range(DT):
                sp.wait_ge(out_ready.sem, m + 1)
                sp.dma_start(out[:, m, :], resid[:, m, :]).then_inc(out_stored.sem, 16)
            sp.wait_ge(out_stored.sem, 16 * DT)

        @block.gpsimd
        def _(pool):
            pool.dma_start(gains[:], d["gains"]).then_inc(gains_loaded.sem, 16)
            loads = [(head_gain, "head_gain"), (lru_par, "lru_par"), (gate_w, "gate_w"),
                     (cmp_pos, "cmp_pos"), (cmp_w2, "cmp_w2"), (ml_bias, "ml_bias")]
            for t, name in loads:
                pool.dma_start(t[:], d[name]).then_inc(consts_loaded.sem, 16)
            zero = 0
            for t, v in [(ones, 1.0), (ident, 0.0), (halves, 0.0), (causal, 1.0), (cmp_mask, 1.0),
                         (pick, 1.0), (gate_bd, 0.0), (kcT, 0.0), (vc_bd, 0.0)]:
                nc.gpsimd.memset(t[:], v).then_inc(pool_zero.sem, 1)
                zero += 1
            nc.gpsimd.iota(dist[:], pattern=[[-1, S]], base=S - P, channel_multiplier=1,
                           allow_small_or_imprecise_dtypes=True).then_inc(pool_zero.sem, 1)
            nc.gpsimd.iota(cmp_bias[:], pattern=[[0, 2], [P, ST], [0, 4], [-16, 32]], base=-31, channel_multiplier=1,
                           allow_small_or_imprecise_dtypes=True).then_inc(pool_zero.sem, 1)
            for h in range(HEADS):
                nc.gpsimd.memset(neg_slope[:, h:h + 1], -(2.0 ** -(h + 1))).then_inc(pool_zero.sem, 1)
            zero += 2 + HEADS
            pool.wait_ge(pool_zero.sem, zero)
            sel = nc.gpsimd.affine_select
            sel(out=ident[:], in_=ident[:], compare_op=ALU.not_equal, fill=1.0, base=0, pattern=[[-1, P]],
                channel_multiplier=1).then_inc(pool_consts.sem, 1)
            sel(out=causal[:], in_=causal[:], compare_op=ALU.is_ge, fill=0.0, base=0, pattern=[[1, P]],
                channel_multiplier=-1).then_inc(pool_consts.sem, 1)
            sel(out=dist[:], in_=dist[:], compare_op=ALU.is_ge, fill=MASKED, base=S - P, pattern=[[-1, S]],
                channel_multiplier=1).then_inc(pool_consts.sem, 1)
            sel(out=cmp_bias[:], in_=cmp_bias[:], compare_op=ALU.is_ge, fill=MASKED, base=-31,
                pattern=[[0, 2], [P, ST], [0, 4], [-16, 32]], channel_multiplier=1).then_inc(pool_consts.sem, 1)
            sel(out=cmp_mask[:], in_=cmp_mask[:], compare_op=ALU.is_ge, fill=0.0, base=-31,
                pattern=[[P, ST], [-16, 32]], channel_multiplier=1).then_inc(pool_consts.sem, 1)
            sel(out=pick[:], in_=pick[:], compare_op=ALU.is_equal, fill=0.0, base=0, pattern=[[-1, 4], [0, P]],
                channel_multiplier=1).then_inc(pool_consts.sem, 1)

            with pool.Fori(0, LAYERS) as l:
                pool.wait_ge(q_hi_done.sem, q_hi_done.at(l, 1))
                wait_alone(pool, q_lo_done.sem, q_lo_done.at(l, 1))
                with pool.Fori(0, 2) as b:
                    with pool.Fori(0, 2) as g:
                        for h in range(HPG):
                            pool.wait_ge(att_s_ready.sem, l * 64 + (b * 2 + g) * 16 + 4 * h + 4)
                            for part, q in enumerate((q_hi, q_lo)):
                                pool.dma_start(q_head[h][HD * part:HD * part + HD, :],
                                             q[HD * (h % 2):HD * (h % 2) + HD, g * 2 + h // 2, :])\
                                  .then_inc(q_loaded[h].sem, 16)

        POOL_CONSTS = 6

        @block.tensor
        def _(pe):
            mm = nc.tensor.matmul
            pe.sem_inc(chunk_done.sem, 2)
            pe.sem_inc(att_s_ready.sem, 16)
            pe.sem_inc(att_tr_ready.sem, 2)
            pe.sem_inc(att_pv_ready.sem, 2)
            pe.sem_inc(ml_pv.sem, 2)
            pe.wait_ge(pool_consts.sem, POOL_CONSTS)
            pe.wait_ge(dve_consts.sem, 1)

            def product(slot, tiles, a_hi, a_lo, k0, dst, first, last, tile_wait=None):
                for k in range(tiles):
                    if tile_wait is not None:
                        tile_wait(k)
                    wh = w_hi[slot][:, k * P:(k + 1) * P]
                    wl = w_lo[slot][:, k * P:(k + 1) * P]
                    mm(dst, wh, a_hi[:, k0 + k, :], start=first and k == 0, stop=False)
                    mm(dst, wh, a_lo[:, k0 + k, :], start=False, stop=False)
                    ins = mm(dst, wl, a_hi[:, k0 + k, :], start=False, stop=last and k == tiles - 1)
                return ins

            with pe.Fori(0, LAYERS) as l:
                def chunk_split(n):
                    pe.wait_ge(w_lo_done.sem, w_lo_done.at(l, n + 1))

                def norm(q):
                    pe.wait_ge(sq_added.sem, sq_added.at(l, 8 * q))
                    mm(bank[6][:, :], ones[:], sumsq[:], start=True, stop=True).then_inc(norm_sum.sem, 1)

                def up(f, n_up, m, first):
                    n = n_up + 2 * m
                    chunk_split(n)
                    pe.wait_ge(g_scaled_done.sem, g_scaled_done.at(l, f * FT + m))
                    wait = (lambda k: pe.wait_ge(x_lo_done.sem, x_lo_done.at(l, (16 * f - 8) + k + 1))) if first else None
                    product(0, DT, x_hi, x_lo, 0, bank[0][:], True, True, wait).then_inc(chunk_done.sem, 1)
                    if first:
                        norm(2 * f)
                    chunk_split(n + 1)
                    pe.wait_ge(u_scaled_done.sem, u_scaled_done.at(l, f * FT + m))
                    product(1, DT, x_hi, x_lo, 0, bank[1][:], True, True).then_inc(chunk_done.sem, 1)

                def down(f, n_down, j):
                    for i in range(2):
                        m = 2 * j + i
                        n = n_down + 2 * m
                        pe.wait_ge(resid_ready.sem, resid_ready.at(l, 16 * f + m - 1))
                        for s in range(2):
                            chunk_split(n + s)
                            pe.wait_ge(hidden_lo.sem, hidden_lo.at(l, f * FT + FH * (s + 1)))
                            product(s, FH, hid_hi, hid_lo, FH * s, bank[4 + i][:], s == 0, s == 1)\
                                .then_inc(chunk_done.sem, 1)

                for f, n_up, n_down in ((0, N_UP1, N_DN1),):
                    up(f, n_up, 0, True)
                    with pe.Fori(1, FT) as m:
                        up(f, n_up, m, False)
                    with pe.Fori(0, DT // 2) as j:
                        down(f, n_down, j)

                def w_in(j, first):
                    for i in range(2):
                        chunk_split(N_WIN + 2 * j + i)
                        if not first:
                            pe.wait_ge(u_done.sem, u_done.at(l, 2 * j + i - 1))
                        wait = (lambda k: pe.wait_ge(x_lo_done.sem, x_lo_done.at(l, k + 1))) if first and i == 0 else None
                        product(i, DT, x_hi, x_lo, 0, bank[2 + i][:], True, True, wait).then_inc(chunk_done.sem, 1)
                        if first and i == 0:
                            norm(1)

                w_in(0, True)
                with pe.Fori(1, 5) as j:
                    w_in(j, False)
                pe.wait_ge(layer_w_ready.sem, layer_w_ready.at(l, 1))
                for c in range(2):
                    pe.wait_ge(conv_done.sem, conv_done.at(l, c + 1))
                    mm(bank[4 * c][:], gate_bd[:, c, :], lru[0][:, c, :], start=True, stop=True)
                    mm(bank[4 * c + 1][:], gate_bd[:, 2 + c, :], lru[0][:, c, :], start=True, stop=True)\
                        .then_inc(lru_g_ready.sem, 1)
                with pe.Fori(5, 7) as j:
                    w_in(j, False)
                pe.wait_ge(lru_sq_done.sem, lru_sq_done.at(l, 1))
                for c in range(2):
                    ins = mm(bank[c][:], halves[:], lru[1][:, c, :], start=True, stop=True)
                ins.then_inc(lru_ms_ready.sem, 1)
                w_in(WIN_TILES // 2 - 1, False)
                pe.wait_ge(rstd_ready.sem, rstd_ready.at(l, 2))
                for t in range(ST):
                    ins = mm(bank[6][:, t:t + 1], rstd[0:1, t * P:(t + 1) * P], ones[0:1, 0:1], start=True, stop=True)
                ins.then_inc(rcol_ready.sem, 1)
                pe.wait_ge(u_done.sem, u_done.at(l, WIN_TILES))
                pe.wait_ge(rcol_done.sem, rcol_done.at(l, 1))
                for k in range(DT):
                    chunk_split(N_TM + k)
                    wh, wl = w_hi[k % 2], w_lo[k % 2]
                    for t in range(ST):
                        xh, xl = (a[:, k, t * P:(t + 1) * P] for a in (x_hi, x_lo))
                        for x, w, part in ((xh, wh, 0), (xh, wl, 1), (xl, wh, 2)):
                            for half, (c0, c1) in enumerate(((0, TM_A), (TM_A, TM_W))):
                                ins = mm(bank[2 * t + half][:, 0:c1 - c0], x, w[:, c0:c1],
                                         start=k == 0 and part == 0, stop=k == DT - 1 and part == 2)
                    ins.then_inc(chunk_done.sem, 1)
                pe.wait_ge(tm_taken.sem, tm_taken.at(l, 1))

                pe.wait_ge(tm_values_taken.sem, tm_values_taken.at(l, 1))
                for t in range(ST):
                    nc.tensor.transpose(bank[6][0:4, t * P:(t + 1) * P], ifcol[:, t, 0:4], ident[:])
                for t in range(ST):
                    ins = nc.tensor.transpose(bank[7][0:4, t * P:(t + 1) * P], ifcol[:, t, 4:8], ident[:])
                ins.then_inc(if_t_ready.sem, 1)
                for kv in range(2):
                    pe.wait_ge(cmp_w_loaded[kv].sem, cmp_w_loaded[kv].at(l, 4 * 16))
                    pe.wait_ge(zc_ready[kv].sem, zc_ready[kv].at(l, 1))
                    for c in range(CP):
                        ins = mm(bank[2 + kv][0:2 * NCMP, 0:256], zc[kv][:, c, :], cmp_w1[kv][:, c, :],
                                 start=c == 0, stop=c == CP - 1)
                ins.then_inc(cmp_h_ready.sem, 1)
                wait_alone(pe, cmp_act_done.sem, cmp_act_done.at(l, 1))
                for n in range(4):
                    ins = nc.tensor.transpose(bank[4][:, n * 64:n * 64 + 2 * NCMP],
                                              cmp_act[:, n // 2, (n % 2) * P:(n % 2 + 1) * P],
                                              ident[0:2 * NCMP, 0:2 * NCMP])
                ins.then_inc(cmp_t_ready.sem, 1)
                wait_alone(pe, ml_rows.sem, ml_rows.at(l, 1))
                for t in range(ST):
                    nc.tensor.transpose(bank[6][:, t * 8:t * 8 + 4], rows[3][:, t * P:(t + 1) * P], ident[0:4, 0:4])
                    ins = nc.tensor.transpose(bank[6][:, t * 8 + 4:t * 8 + 8], rows[5][:, t * P:(t + 1) * P],
                                              ident[0:4, 0:4])
                ins.then_inc(ml_cols_ready.sem, 1)
                pe.wait_ge(cmp_hid_done.sem, cmp_hid_done.at(l, 1))
                for par in range(2):
                    for g in range(2):
                        for m in range(2):
                            mm(bank[3][HD * par:HD * par + HD, g * 32:g * 32 + NCMP], w2cur[:, 0, m, :],
                               cmp_hid[:, 0, m, g * NCMP:(g + 1) * NCMP], start=m == 0, stop=m == 1)
                for j in range(4):
                    g = j // 2
                    for m in range(2):
                        ins = mm(bank[5][32 * j:32 * j + NCMP, HD * j:HD * (j + 1)],
                                 cmp_hid[:, 1, m, g * NCMP:(g + 1) * NCMP], w2cur[:, 1, m, :],
                                 start=m == 0, stop=m == 1)
                ins.then_inc(cmp_kv_ready.sem, 1)
                pe.wait_ge(cmp_kv_done.sem, cmp_kv_done.at(l, 1))
                for t in range(ST):
                    for h in range(HEADS):
                        par = h % 2
                        hp = HD * par
                        o = (t * 4 + h // 2) * 32
                        ins = mm(bank[2 + par][:, o:o + 32], U[hp:hp + HD, U_Q + h // 2, t * P:(t + 1) * P],
                                 kcT[hp:hp + HD, h // HPG, :], start=True, stop=True)
                        if t == ST - 1 and h >= HEADS - 2:
                            ins.then_inc(cmp_s_ready.sem, 1)
                pe.wait_ge(cmp_pm_done.sem, cmp_pm_done.at(l, 1))
                for n in range(8):
                    ins = nc.tensor.transpose(bank[4 + n // 4][:, (n % 4) * P:(n % 4 + 1) * P],
                                              PR[:, n // 4, (n % 4) * P:(n % 4 + 1) * P], ident[:])
                ins.then_inc(cmp_tr_ready.sem, 1)
                pe.wait_ge(cmp_pt_done.sem, cmp_pt_done.at(l, 1))
                for t in range(ST):
                    for par in range(2):
                        ins = mm(bank[2 + t][:, par * 256:(par + 1) * 256], PT[:, par, t * P:(t + 1) * P], vc_bd[:],
                                 start=True, stop=True)
                ins.then_inc(cmp_o_ready.sem, 1)
                pe.wait_ge(cmp_o_done.sem, cmp_o_done.at(l, 1))
                pe.wait_ge(ml_cols_done.sem, ml_cols_done.at(l, 1))

                def ml_scores(n):
                    h, j = n // ST, n % ST
                    hp = HD * (h % 2)
                    if j == 0:
                        if h:
                            pe.wait_ge(ml_d_done.sem, ml_d_done.at(l, ST * h))
                        mm(bank[6][:], pick[:, h, :], rows[4][:], start=True, stop=True).then_inc(ml_m_ready.sem, 1)
                    pe.wait_ge(ml_w_done.sem, ml_w_done.at(l, n - 1))
                    mm(bank[n % 2][:, 0:S - j * P], U[hp:hp + HD, U_KM + h // 2, j * P:(j + 1) * P],
                       U[hp:hp + HD, U_QM + h // 2, j * P:S], start=True, stop=True).then_inc(ml_s_ready.sem, 1)

                ml_scores(0)
                for n in range(16):
                    if n + 1 < 16:
                        ml_scores(n + 1)
                    h, j = n // ST, n % ST
                    pe.wait_ge(ml_w_done.sem, ml_w_done.at(l, n + 1))
                    for i in range(j, ST):
                        ins = mm(bank[(2, 3, 4, 5)[i]][:, h * (HD + 1):(h + 1) * (HD + 1)],
                                 ml_w[:, n % 2, (i - j) * P:(i - j + 1) * P], v_aug[:, j, h, :],
                                 start=j == 0, stop=j == i)
                    ins.then_inc(ml_pv.sem, 1)

                pe.wait_ge(ml_o_done.sem, ml_o_done.at(l, 1))
                wait_alone(pe, k_lo_done.sem, k_lo_done.at(l, 4))
                with pe.Fori(0, 2) as b:
                    with pe.Fori(0, 2) as g:
                        kv = b * 2 + g

                        def scores(u):
                            h, i = u // ST, u % ST
                            if i == 0:
                                pe.wait_ge(q_loaded[h].sem, l * 128 + kv * 32 + 32)
                            wait_alone(pe, att_scored.sem, l * 64 + kv * 16 + u + 1)
                            w = (i + 1) * P
                            q = q_head[h][:, i * P:(i + 1) * P]
                            mm(bank[u % 4][:, 0:w], q, k_hi[:, kv, 0:w], start=True, stop=False)
                            ins = mm(bank[u % 4][:, 0:w], q, k_lo[:, kv, 0:w], start=False, stop=True)
                            ins.then_inc(att_s_ready.sem, 1)

                        def flip(u):
                            pe.wait_ge(att_exp_done.sem, l * 64 + kv * 16 + u + 3)
                            pe.wait_ge(att_copied.sem, l * 64 + kv * 16 + u + 1)
                            for j in range(u % ST + 1):
                                ins = nc.tensor.transpose(bank[4 + u % 2][:, j * P:(j + 1) * P],
                                                          PR[:, u % 2, j * P:(j + 1) * P], ident[:])
                            ins.then_inc(att_tr_ready.sem, 1)

                        def values(u):
                            pe.wait_ge(att_copied.sem, l * 64 + kv * 16 + u + 3)
                            i = u % ST
                            if u == 0:
                                pe.wait_ge(acc_taken.sem, l * 4 + kv + 1)
                            for j in range(i + 1):
                                ins = mm(bank[6 + u // 8][:, (u % 8) * HD:(u % 8 + 1) * HD],
                                         PT[:, u % 2, j * P:(j + 1) * P], v_all[:, kv, j, :],
                                         start=j == 0, stop=j == i)
                            ins.then_inc(att_pv_ready.sem, 1)

                        for u in range(3):
                            scores(u)
                        for u in range(16):
                            if u + 3 < 16:
                                scores(u + 3)
                            flip(u)
                            if u:
                                values(u - 1)
                        values(15)

                pe.wait_ge(o_normed.sem, o_normed.at(l, 1))
                for n in range(6):
                    if n >= 4:
                        pe.wait_ge(h_lo_done.sem, h_lo_done.at(l, n - 3))
                    for t in range(ST):
                        ins = nc.tensor.transpose(bank[n % 4][:, t * P:(t + 1) * P], o_all[:, t, 2 * n:2 * n + 2, :],
                                                  ident[:])
                    ins.then_inc(h_t_ready.sem, 1)

                wait_alone(pe, h_lo_done.sem, h_lo_done.at(l, 6))
                wait_alone(pe, lru_lo_done.sem, lru_lo_done.at(l, 2))

                def w_out(j):
                    for i in range(2):
                        chunk_split(N_OUT + 2 * j + i)
                        pe.wait_ge(resid_ready.sem, resid_ready.at(l, DT + 2 * j + i - 1))
                        product(i, DT, h_hi, h_lo, 0, bank[4 + i][:], True, True).then_inc(chunk_done.sem, 1)

                with pe.Fori(0, DT // 2) as j:
                    w_out(j)

                up(1, N_UP2, 0, True)
                with pe.Fori(1, FT) as m:
                    up(1, N_UP2, m, False)
                with pe.Fori(0, DT // 2) as j:
                    down(1, N_DN2, j)
            pe.wait_ge(sq_added.sem, sq_added.at(LAYERS, 0))
            mm(bank[6][:, :], ones[:], sumsq[:], start=True, stop=True).then_inc(norm_sum.sem, 1)

        @block.scalar
        def _(act):
            fn = nc.scalar.activation
            act.sem_inc(att_exp_done.sem, 2)
            act.sem_inc(att_copied.sem, 2)
            act.wait_ge(gains_loaded.sem, 16)
            act.wait_ge(x_loaded.sem, 16)

            def split_hi(l, n, half, slot, width):
                act.wait_ge(w_loaded[slot].sem, w_loaded[slot].at(l, 16 * half + 16))
                act.wait_ge(chunk_done.sem, chunk_done.at(l, n - 1))
                fn(w_hi[slot][:, 0:width], raw[slot][:, 0:width], ACT.Copy).then_inc(w_hi_done.sem, 1)

            def next_hi(l, n, half, s, width):
                split_hi(l, n + 2 + s, half + 1, s, width)

            def norm_input(l, r, m, q):
                g = gains[:, q, bass.ds(m, 1)]
                tile = resid[:, bass.ds(m, 1), :].rearrange("p a s -> p (a s)")
                fn(x_hi[:, bass.ds(m, 1), :].rearrange("p a s -> p (a s)"), tile, ACT.Copy, scale=g)\
                    .then_inc(x_hi_done.sem, 1)

            def square(l, r, m, slot):
                wait_alone(act, sq_added.sem, sq_added.at(l, r + m - 1))
                fn(sq[:, slot, :], resid[:, bass.ds(m, 1), :].rearrange("p a s -> p (a s)"), ACT.Square)\
                    .then_inc(sq_ready.sem, 1)

            def root(l, q):
                act.wait_ge(mean_ready.sem, mean_ready.at(l, q + 1))
                fn(mean_sq[:], mean_sq[:], ACT.Sqrt).then_inc(root_ready.sem, 1)

            for m in range(DT):
                norm_input(0, -DT, m, 0)
                square(0, -DT, m, m % 2)
            act.wait_ge(consts_loaded.sem, 16 * CONST_LOADS)

            with act.Fori(0, LAYERS) as l:
                def up(f, n_up, m, width, first=False):
                    n, half = n_up + 2 * m, n_up // 2 + m
                    next_hi(l, n, half, 0, width)
                    if first:
                        root(l, 2 * f)
                    act.wait_ge(g_scaled_done.sem, g_scaled_done.at(l, f * FT + m + 1))
                    fn(g_silu[:], g_scaled[:], ACT.Silu).then_inc(silu_done.sem, 1)
                    next_hi(l, n, half, 1, width)
                    act.wait_ge(hidden_ready.sem, hidden_ready.at(l, f * FT + m + 1))
                    fn(hid_hi[:, bass.ds(m, 1), :].rearrange("p a s -> p (a s)"), hidden[:], ACT.Copy)\
                        .then_inc(hidden_hi.sem, 1)

                def project(n0, r, q, j, chunks, width):
                    for i in range(2):
                        m = 2 * j + i
                        for c in range(chunks):
                            s = (i * chunks + c) % 2
                            n = n0 + chunks * m + c
                            half = n0 // 2 + (chunks * j + (i * chunks + c) // 2)
                            if width[i]:
                                next_hi(l, n0 + 2 * chunks * j + (i * chunks + c) - s, half, s, width[i])
                        act.wait_ge(resid_ready.sem, resid_ready.at(l, r + m + 1))
                        norm_input(l, r, m, q)
                        square(l, r, m, i)

                def ffn(f, n_up, n_down, r, q, next_width):
                    up(f, n_up, 0, UP_W, True)
                    nc.scalar.preload_act_table(ACT.Silu)
                    with act.Fori(1, FT - 1) as m:
                        up(f, n_up, m, UP_W)
                    up(f, n_up, FT - 1, DOWN_W)
                    with act.Fori(0, DT // 2 - 1) as j:
                        project(n_down, r, q, j, 2, (DOWN_W, DOWN_W))
                    project(n_down, r, q, DT // 2 - 1, 2, (DOWN_W, next_width))

                for s in range(2):
                    split_hi(l, s, 0, s, UP_W)
                ffn(0, N_UP1, N_DN1, 0, 3 * l + 1, UP_W)

                next_hi(l, N_WIN, N_WIN // 2, 0, UP_W)
                root(l, 1)
                next_hi(l, N_WIN, N_WIN // 2, 1, UP_W)

                def next_tile(m):
                    next_hi(l, N_WIN + m - m % 2, (N_WIN + m) // 2, m % 2, UP_W)

                next_tile(2)
                act.wait_ge(sp_arg.sem, sp_arg.at(l, 1))
                fn(spt[:, 1, :], spt[:, 0, :], ACT.Exp, scale=-1.0).then_inc(sp_exp.sem, 1)
                next_tile(3)
                act.wait_ge(sp_arg.sem, sp_arg.at(l, 2))
                fn(spt[:, 3, :], spt[:, 2, :], ACT.Ln).then_inc(sp_ln.sem, 1)
                next_tile(4)
                next_tile(5)
                next_tile(6)
                next_tile(7)
                next_tile(8)
                next_tile(9)
                for c in range(2):
                    act.wait_ge(lru_g_ready.sem, lru_g_ready.at(l, c + 1))
                    fn(lru[1][:, c, :], bank[4 * c][:], ACT.Sigmoid, bias=lru_par[:, l, c, 5:6])
                    fn(lru[2][:, c, :], bank[4 * c + 1][:], ACT.Sigmoid, bias=lru_par[:, l, c, 6:7])\
                        .then_inc(lru_gates_done.sem, 1)
                act.wait_ge(sp_done.sem, sp_done.at(l, 1))
                act.wait_ge(lru_gates_done.sem, lru_gates_done.at(l, 2))
                for c in range(2):
                    ins = fn(lru[1][:, c, :], lru[1][:, c, :], ACT.Tanh, scale=sp4[:, c:c + 1])
                ins.then_inc(lru_tanh.sem, 1)
                next_tile(10)
                act.wait_ge(u_done.sem, u_done.at(l, U_GR + 2))
                fn(U[:, U_GR:U_GR + 2, :], U[:, U_GR:U_GR + 2, :], ACT.Gelu_apprx_tanh).then_inc(lru_gelu.sem, 1)
                act.wait_ge(lru_om.sem, lru_om.at(l, 1))
                fn(lru[1][:], lru[1][:], ACT.Sqrt).then_inc(lru_sqrt.sem, 1)
                next_tile(11)
                next_tile(12)
                act.wait_ge(lru_out.sem, lru_out.at(l, 1))
                fn(lru[1][:], lru[0][:], ACT.Square).then_inc(lru_sq_done.sem, 1)
                next_tile(13)
                next_hi(l, N_TM - 2, N_TM // 2 - 1, 0, TM_W)
                act.wait_ge(lru_ms_done.sem, lru_ms_done.at(l, 1))
                fn(lru[3][:], lru[3][:], ACT.Sqrt).then_inc(lru_root.sem, 1)
                next_hi(l, N_TM - 2, N_TM // 2 - 1, 1, TM_W)
                act.wait_ge(rcol_ready.sem, rcol_ready.at(l, 1))
                fn(rcol[:], bank[6][:, 0:ST], ACT.Copy).then_inc(rcol_done.sem, 1)
                for j in range(DT // 2):
                    for s in range(2):
                        next_hi(l, N_TM + 2 * j, N_TM // 2 + j, s, TM_W if j < DT // 2 - 1 else UP_W)
                act.wait_ge(chunk_done.sem, chunk_done.at(l, N_OUT))
                act.wait_ge(rcol_done.sem, rcol_done.at(l, 1))
                for t in range(ST):
                    fn(ifcol[:, t, :], bank[2 * t][:, 280:288], ACT.Copy, scale=rcol[:, t:t + 1])
                    fn(v_all[:, :, t, :], bank[2 * t][:, 0:256].rearrange("p (k d) -> p k d", k=4), ACT.Copy,
                       scale=rcol[:, t:t + 1])
                for t in range(ST):
                    ins = fn(gates[:, t, :], bank[2 * t][:, 256:280], ACT.Sigmoid, scale=rcol[:, t:t + 1])
                ins.then_inc(tm_taken.sem, 1)
                act.wait_ge(tm_values_taken.sem, tm_values_taken.at(l, 1))
                fn(o_sig[:], o_sig[:], ACT.Sigmoid).then_inc(o_sig_done.sem, 1)
                act.wait_ge(ml_abs.sem, ml_abs.at(l, 1))
                fn(rows[2][:], rows[2][:], ACT.Exp, scale=-1.0).then_inc(ml_exp.sem, 1)
                act.wait_ge(ml_arg.sem, ml_arg.at(l, 1))
                fn(rows[4][:], rows[3][:], ACT.Ln).then_inc(ml_ln.sem, 1)
                act.wait_ge(cmp_h_ready.sem, cmp_h_ready.at(l, 1))
                for kv in range(2):
                    ins = fn(cmp_act[:, kv, :], bank[2 + kv][0:2 * NCMP, 0:256], ACT.Silu)
                ins.then_inc(cmp_act_done.sem, 1)
                act.wait_ge(cmp_t_ready.sem, cmp_t_ready.at(l, 1))
                fn(cmp_hid[:].rearrange("p a b n -> p (a b) n"),
                   bank[4][:, 0:256].rearrange("p (a n) -> p a n", n=64)[:, :, 0:2 * NCMP], ACT.Copy)\
                    .then_inc(cmp_hid_done.sem, 1)
                for kv in range(4):
                    src = slice(HD * (kv % 2), HD * (kv % 2) + HD)
                    for half in range(2):
                        ins = fn(k_hi[HD * half:HD * half + HD, kv, :], U[src, U_KS + kv // 2, :], ACT.Copy,
                                 scale=HD ** -0.5)
                    ins.then_inc(k_hi_done.sem, 1)
                fn(q_hi[:], U[:, U_Q:U_Q + HEADS // 2, :], ACT.Copy).then_inc(q_hi_done.sem, 1)
                act.wait_ge(cmp_t_done.sem, cmp_t_done.at(l, 1))
                fn(PR[:], T[:], ACT.Exp).then_inc(cmp_p_done.sem, 1)
                act.wait_ge(cmp_tr_ready.sem, cmp_tr_ready.at(l, 1))
                for n in range(2):
                    ins = fn(PT[:, n, :], bank[4 + n][:], ACT.Copy)
                ins.then_inc(cmp_pt_done.sem, 1)
                act.wait_ge(ml_cols_done.sem, ml_cols_done.at(l, 1))
                fn(em[:], bcol[:, :, 4:8], ACT.Exp, scale=-1.0).then_inc(ml_em.sem, 1)
                for n in range(16):
                    act.wait_ge(ml_d_done.sem, ml_d_done.at(l, n + 1))
                    e = ml_e[:, n % 2, 0:S - (n % ST) * P]
                    fn(e, e, ACT.Exp).then_inc(ml_e_done.sem, 1)

                with act.Fori(0, 2) as b:
                    with act.Fori(0, 2) as g:
                        pas = l * 64 + (b * 2 + g) * 16

                        def exps(u):
                            act.wait_ge(att_scored.sem, pas + u + 5)
                            act.wait_ge(att_tr_ready.sem, pas + u + 1)
                            w = (u % ST + 1) * P
                            fn(PR[:, u % 2, 0:w], T[:, u % 2, 0:w], ACT.Exp, bias=n_max[:, u:u + 1],
                               accum_out=sums[:, b * 2 + g, u:u + 1]).then_inc(att_exp_done.sem, 1)

                        exps(0)
                        for u in range(16):
                            if u + 1 < 16:
                                exps(u + 1)
                            act.wait_ge(att_tr_ready.sem, pas + u + 3)
                            act.wait_ge(att_pv_ready.sem, pas + u + 1)
                            w = (u % ST + 1) * P
                            fn(PT[:, u % 2, 0:w], bank[4 + u % 2][:, 0:w], ACT.Copy).then_inc(att_copied.sem, 1)

                act.wait_ge(acc_taken.sem, acc_taken.at(l, 4))
                fn(o_sq[:], o_all[:].rearrange("p t h d -> p (t h) d"), ACT.Square).then_inc(o_sq_done.sem, 1)
                act.wait_ge(o_ms_done.sem, o_ms_done.at(l, 1))
                fn(h_ms[:], h_ms[:], ACT.Sqrt).then_inc(o_root.sem, 1)
                act.wait_ge(lru_normed.sem, lru_normed.at(l, 1))
                for c in range(2):
                    fn(h_hi[:, 4 + c, :], U[:, U_GR + c, :], ACT.Copy).then_inc(lru_hi_done.sem, 1)
                for n in range(6):
                    k = n if n < 4 else n + 2
                    act.wait_ge(h_t_ready.sem, h_t_ready.at(l, n + 1))
                    if k == U_GR:
                        act.wait_ge(lru_lo_done.sem, lru_lo_done.at(l, 2))
                    fn(h_hi[:, k, :], bank[n % 4][:], ACT.Copy, scale=head_gain[:, l, k:k + 1])\
                        .then_inc(h_hi_done.sem, 1)

                with act.Fori(0, DT // 2) as j:
                    project(N_OUT, DT, 3 * l + 2, j, 1, (UP_W, UP_W))
                ffn(1, N_UP2, N_DN2, 2 * DT, 3 * l + 3, 0)
            root(LAYERS, 0)

        @block.vector
        def _(dve):
            tt, ts, stt = nc.vector.tensor_tensor, nc.vector.tensor_scalar, nc.vector.scalar_tensor_tensor
            steps = Steps(dve, dve_step.sem)
            dve.sem_inc(w_lo_done.sem, 2)
            dve.sem_inc(sq_added.sem, 2)
            dve.sem_inc(resid_ready.sem, 2)
            dve.sem_inc(att_scored.sem, 4)
            dve.sem_inc(ml_w_done.sem, 2)
            dve.sem_inc(g_scaled_done.sem, 1)
            dve.sem_inc(u_scaled_done.sem, 1)
            dve.sem_inc(acc_taken.sem, 1)
            dve.wait_ge(gains_loaded.sem, 16)
            dve.wait_ge(x_loaded.sem, 16)

            def flat(t, m):
                return t[:, bass.ds(m, 1), :].rearrange("p a s -> p (a s)")

            def split_lo(l, n, slot, width):
                dve.wait_ge(w_hi_done.sem, w_hi_done.at(l, n + 1))
                tt(w_lo[slot][:, 0:width], raw[slot][:, 0:width], w_hi[slot][:, 0:width].bitcast(F32), ALU.subtract)\
                    .then_inc(w_lo_done.sem, 1)

            def norm_low(l, r, m, q):
                dve.wait_ge(x_hi_done.sem, x_hi_done.at(l, r + m + 1))
                stt(flat(x_lo, m), flat(resid, m), gains[:, q, bass.ds(m, 1)], flat(x_hi, m).bitcast(F32),
                    ALU.mult, ALU.subtract).then_inc(x_lo_done.sem, 1)

            def norm_add(l, r, m, slot):
                dve.wait_ge(sq_ready.sem, sq_ready.at(l, r + m + 1))
                dve.wait_ge(sq_added.sem, sq_added.at(l, r + m))
                tt(sumsq[:], sumsq[:], sq[:, slot, :], ALU.add).then_inc(sq_added.sem, 1)

            def norm_finish(l, q):
                dve.wait_ge(norm_sum.sem, norm_sum.at(l, q + 1))
                ts(mean_sq[:], bank[6][:], 1.0 / (DT * P), EPS, ALU.mult, ALU.add).then_inc(mean_ready.sem, 1)
                dve.wait_ge(root_ready.sem, root_ready.at(l, q + 1))
                nc.vector.reciprocal(rstd[:], mean_sq[:]).then_inc(rstd_ready.sem, 1)
                dve.wait_ge(rstd_ready.sem, rstd_ready.at(l, q + 1))

            steps.done(nc.vector.memset(sumsq[:], 0.0)).then_inc(waits_met.sem, 1)
            for m in range(DT):
                norm_low(0, -DT, m, 0)
                norm_add(0, -DT, m, m % 2)
            dve.wait_ge(consts_loaded.sem, 16 * CONST_LOADS)
            dve.wait_ge(pool_consts.sem, POOL_CONSTS)
            nc.vector.memset(halves[0:HD, 0:HD], 1.0)
            nc.vector.memset(halves[HD:P, HD:P], 1.0).then_inc(dve_consts.sem, 1)
            for h in range(HEADS):
                ts(cmp_bias[:, h % 2, :, h // 2, :], cmp_bias[:, h % 2, :, h // 2, :], neg_slope[:, h:h + 1], None, ALU.mult)
            before = steps.n

            with dve.Fori(0, LAYERS) as l:
                steps.base, steps.n = l * DVE_STEPS + before, 0

                def up(f, n_up, m, width, first=False):
                    n = n_up + 2 * m
                    if first:
                        split_lo(l, n + 2, 0, width)
                        norm_finish(l, 2 * f)
                    dve.wait_ge(chunk_done.sem, chunk_done.at(l, n + 1))
                    tt(g_scaled[:], bank[0][:], rstd[:], ALU.mult).then_inc(g_scaled_done.sem, 1)
                    if not first:
                        split_lo(l, n + 2, 0, width)
                    dve.wait_ge(chunk_done.sem, chunk_done.at(l, n + 2))
                    tt(u_scaled[:], bank[1][:], rstd[:], ALU.mult).then_inc(u_scaled_done.sem, 1)
                    split_lo(l, n + 3, 1, width)
                    dve.wait_ge(silu_done.sem, silu_done.at(l, f * FT + m + 1))
                    dve.wait_ge(u_scaled_done.sem, u_scaled_done.at(l, f * FT + m + 1))
                    tt(hidden[:], g_silu[:], u_scaled[:], ALU.mult).then_inc(hidden_ready.sem, 1)
                    dve.wait_ge(hidden_hi.sem, hidden_hi.at(l, f * FT + m + 1))
                    tt(flat(hid_lo, m), hidden[:], flat(hid_hi, m).bitcast(F32), ALU.subtract)\
                        .then_inc(hidden_lo.sem, 1)

                def project(n0, r, q, j, chunks, factor, width):
                    for i in range(2):
                        m = 2 * j + i
                        first_n = n0 + 2 * chunks * j + i * chunks
                        if chunks == 2 and width[i]:
                            split_lo(l, first_n + 2, 0, width[i])
                        dve.wait_ge(chunk_done.sem, chunk_done.at(l, first_n + chunks))
                        stt(flat(resid, m), bank[4 + i][:], factor, flat(resid, m), ALU.mult, ALU.add)\
                            .then_inc(resid_ready.sem, 1)
                        if chunks == 1:
                            split_lo(l, first_n + 2, i, width[i])
                        elif width[i]:
                            split_lo(l, first_n + 3, 1, width[i])
                        norm_low(l, r, m, q)
                        norm_add(l, r, m, i)

                def ffn(f, n_up, n_down, r, q, next_width):
                    up(f, n_up, 0, UP_W, True)
                    with dve.Fori(1, FT - 1) as m:
                        up(f, n_up, m, UP_W)
                    up(f, n_up, FT - 1, DOWN_W)
                    steps.done(nc.vector.memset(sumsq[:], 0.0)).then_inc(waits_met.sem, 1)
                    with dve.Fori(0, DT // 2 - 1) as j:
                        project(n_down, r, q, j, 2, 0.5, (DOWN_W, DOWN_W))
                    project(n_down, r, q, DT // 2 - 1, 2, 0.5, (DOWN_W, next_width))

                for s in range(2):
                    split_lo(l, s, s, UP_W)
                ffn(0, N_UP1, N_DN1, 0, 3 * l + 1, UP_W)

                def take_u(m, i, n):
                    dve.wait_ge(chunk_done.sem, chunk_done.at(l, n + 1))
                    tt(flat(U, m), bank[2 + i][:], rstd[:], ALU.mult).then_inc(u_done.sem, 1)

                split_lo(l, N_WIN + 2, 0, UP_W)
                norm_finish(l, 1)
                def log1p(e, u, ln, a, b, arg_sem, arg_count, ln_sem, ln_count):
                    dve.wait_ge(arg_sem, arg_count)
                    steps.done(ts(a, u, -1.0, None, ALU.add))
                    steps.done(tt(a, e, a, ALU.subtract))
                    steps.done(nc.vector.reciprocal(b, u))
                    steps.done(tt(a, a, b, ALU.mult))
                    dve.wait_ge(ln_sem, ln_count)
                    steps.done(tt(ln, ln, a, ALU.add))


                def tile(m):
                    take_u(m, m % 2, N_WIN + m)
                    split_lo(l, N_WIN + m + 2, m % 2, UP_W)

                take_u(0, 0, N_WIN)
                take_u(1, 1, N_WIN + 1)
                split_lo(l, N_WIN + 3, 1, UP_W)
                for par in range(2):
                    h = slice(HD * par, HD * par + HD)
                    nc.vector.tensor_copy(gate_bd[h, :, h], gate_w[h, l, :, :])
                nc.vector.tensor_copy(w2cur[:], cmp_w2[:, l, :, :, :]).then_inc(layer_w_ready.sem, 1)
                stt(spt[:, 0, :], lru_par[:, l, :, 7], -1.0, lru_par[:, l, :, 7], ALU.mult, ALU.max).then_inc(sp_arg.sem, 1)
                tile(2)
                dve.wait_ge(sp_exp.sem, sp_exp.at(l, 1))
                ts(spt[:, 2, :], spt[:, 1, :], 1.0, None, ALU.add).then_inc(sp_arg.sem, 1)
                tile(3)
                tile(4)

                def conv(c):
                    dve.wait_ge(u_done.sem, u_done.at(l, U_XR + c + 1))
                    par = lru_par[:, l, c, :]
                    steps.done(ts(lru[0][:, c, :], U[:, U_XR + c, :], par[:, 3:4], par[:, 4:5], ALU.mult, ALU.add))
                    for tap in (2, 1, 0):
                        lag = 3 - tap
                        ins = stt(lru[0][:, c, lag:S], U[:, U_XR + c, 0:S - lag], par[:, tap:tap + 1],
                                  lru[0][:, c, lag:S], ALU.mult, ALU.add)
                        if tap:
                            steps.done(ins)
                    ins.then_inc(conv_done.sem, 1)
                    dve.wait_ge(conv_done.sem, conv_done.at(l, c + 1))

                conv(0)
                tile(5)
                conv(1)
                tile(6)
                log1p(spt[:, 1, :], spt[:, 2, :], spt[:, 3, :], spt[:, 4, :], spt[:, 5, :],
                      sp_arg.sem, sp_arg.at(l, 2), sp_ln.sem, sp_ln.at(l, 1))
                steps.done(ts(spt[:, 4, :], lru_par[:, l, :, 7], -1.0, 0.0, ALU.mult, ALU.max))
                steps.done(tt(spt[:, 4, :], spt[:, 4, :], spt[:, 3, :], ALU.add))
                ts(sp4[:], spt[:, 4, :], 4.0, None, ALU.mult).then_inc(sp_done.sem, 1)
                tile(7)
                tile(8)
                tile(9)
                dve.wait_ge(lru_tanh.sem, lru_tanh.at(l, 1))
                tt(lru[2][:], lru[2][:], lru[0][:], ALU.mult)
                steps.done(ts(lru[3][:], lru[1][:], 1.0, None, ALU.add))
                steps.done(nc.vector.reciprocal(lru[3][:], lru[3][:]))
                ts(lru[4][:], lru[1][:], -1.0, 1.0, ALU.mult, ALU.add).then_inc(lru_om.sem, 1)
                dve.wait_ge(lru_om.sem, lru_om.at(l, 1))
                steps.done(tt(lru[4][:], lru[4][:], lru[3][:], ALU.mult))
                tile(10)
                dve.wait_ge(lru_sqrt.sem, lru_sqrt.at(l, 1))
                for c in range(2):
                    ins = stt(lru[1][:, c, :], lru[1][:, c, :], 2.0, lru[3][:, c, :], ALU.mult, ALU.mult)
                steps.done(ins)
                steps.done(tt(lru[1][:], lru[1][:], lru[2][:], ALU.mult))
                for c in range(2):
                    ins = nc.vector.tensor_tensor_scan(lru[3][:, c, :], lru[4][:, c, :], lru[1][:, c, :], 0.0,
                                                       ALU.mult, ALU.add)
                steps.done(ins)
                dve.wait_ge(lru_gelu.sem, lru_gelu.at(l, 1))
                tt(lru[0][:], lru[3][:], U[:, U_GR:U_GR + 2, :], ALU.mult).then_inc(lru_out.sem, 1)
                tile(11)
                tile(12)
                tile(13)
                dve.wait_ge(lru_ms_ready.sem, lru_ms_ready.at(l, 1))
                for c in range(2):
                    ins = ts(lru[3][:, c, :], bank[c][:], 1.0 / HD, EPS, ALU.mult, ALU.add)
                ins.then_inc(lru_ms_done.sem, 1)
                take_u(WIN_TILES - 2, 0, N_TM - 2)
                split_lo(l, N_TM, 0, TM_W)
                dve.wait_ge(lru_root.sem, lru_root.at(l, 1))
                steps.done(nc.vector.reciprocal(lru[3][:], lru[3][:]))
                for c in range(2):
                    ins = stt(U[:, U_GR + c, :], lru[0][:, c, :], head_gain[:, l, 4 + c:5 + c], lru[3][:, c, :],
                              ALU.mult, ALU.mult)
                ins.then_inc(lru_normed.sem, 1)

                take_u(WIN_TILES - 1, 1, N_TM - 1)
                split_lo(l, N_TM + 1, 1, TM_W)
                nc.vector.memset(v_aug[:, :, :, HD:HD + 1], 1.0)
                for k in range(DT):
                    split_lo(l, N_TM + k + 2, k % 2, TM_W if k < DT - 2 else UP_W)
                    if k < 4:
                        kv, par = k // 2, k % 2
                        if k == 0:
                            dve.wait_ge(u_done.sem, u_done.at(l, WIN_TILES))
                        for g in range(2):
                            src = slice(HD * g, HD * g + HD)
                            for pairs, view in block_halves(U[src, U_KC + kv, :], par):
                                ins = tt(zc[kv][HD * par:HD * par + HD, pairs, g * NCMP:(g + 1) * NCMP], view,
                                         wide(cmp_pos[src, l, kv, par, pairs], NCMP), ALU.add)
                        if par:
                            ins.then_inc(zc_ready[kv].sem, 1)
                dve.wait_ge(rcol_done.sem, rcol_done.at(l, 1))
                dve.wait_ge(chunk_done.sem, chunk_done.at(l, N_OUT))
                for t in range(ST):
                    ts(o_sig[:, t, :], bank[2 * t + 1][:, 256:512], rcol[:, t:t + 1], None, ALU.mult)
                    ins = ts(v_aug[:, t, :, 0:HD], bank[2 * t + 1][:, 0:256].rearrange("p (h d) -> p h d", h=4),
                             rcol[:, t:t + 1], None, ALU.mult)
                ins.then_inc(tm_values_taken.sem, 1)
                dve.wait_ge(if_t_ready.sem, if_t_ready.at(l, 1))
                ts(rows[0][:], bank[6][0:4, :], ml_bias[:, l, 0:1], None, ALU.add)
                steps.done(ts(rows[1][:], bank[7][0:4, :], ml_bias[:, l, 1:2], None, ALU.add))
                stt(rows[2][:], rows[1][:], -1.0, rows[1][:], ALU.mult, ALU.max).then_inc(ml_abs.sem, 1)
                dve.wait_ge(ml_exp.sem, ml_exp.at(l, 1))
                ts(rows[3][:], rows[2][:], 1.0, None, ALU.add).then_inc(ml_arg.sem, 1)
                log1p(rows[2][:], rows[3][:], rows[4][:], rows[5][:], rows[2][:],
                      ml_arg.sem, ml_arg.at(l, 1), ml_ln.sem, ml_ln.at(l, 1))
                steps.done(ts(rows[1][:], rows[1][:], 0.0, None, ALU.min))
                steps.done(tt(rows[1][:], rows[1][:], rows[4][:], ALU.subtract))
                steps.done(nc.vector.memset(rows[5][:], 1.0))
                steps.done(nc.vector.tensor_tensor_scan(rows[2][:], rows[5][:], rows[1][:], 0.0, ALU.mult, ALU.add))
                steps.done(tt(rows[3][:], rows[0][:], rows[2][:], ALU.subtract))
                steps.done(nc.vector.tensor_tensor_scan(rows[4][:], rows[3][:], rows[3][:], 0.0, ALU.max, ALU.max))
                steps.done(tt(rows[5][:], rows[2][:], rows[4][:], ALU.add))
                ts(rows[4][:], rows[4][:], -1.0, None, ALU.mult).then_inc(ml_rows.sem, 1)

                dve.wait_ge(ml_cols_ready.sem, ml_cols_ready.at(l, 1))
                nc.vector.tensor_copy(bcol[:], bank[6][:, 0:32].rearrange("p (t c) -> p t c", t=ST))\
                    .then_inc(ml_cols_done.sem, 1)
                dve.wait_ge(ml_cols_done.sem, ml_cols_done.at(l, 1))


                dve.wait_ge(cmp_kv_ready.sem, cmp_kv_ready.at(l, 1))
                nc.vector.tensor_copy(kcT[:, :, 0:NCMP], bank[3][:, 0:64].rearrange("p (g n) -> p g n", g=2)[:, :, 0:NCMP])
                for j in range(4):
                    h = slice(32 * j, 32 * j + NCMP)
                    ins = nc.vector.tensor_copy(vc_bd[h, HD * j:HD * (j + 1)], bank[5][h, HD * j:HD * (j + 1)])
                ins.then_inc(cmp_kv_done.sem, 1)
                for kv in range(4):
                    dve.wait_ge(k_hi_done.sem, k_hi_done.at(l, kv + 1))
                    src = slice(HD * (kv % 2), HD * (kv % 2) + HD)
                    for half in range(2):
                        ins = stt(k_lo[HD * half:HD * half + HD, kv, :], U[src, U_KS + kv // 2, :], HD ** -0.5,
                                  k_hi[src, kv, :].bitcast(F32), ALU.mult, ALU.subtract)
                    ins.then_inc(k_lo_done.sem, 1)
                for half in range(2):
                    dve.wait_ge(cmp_s_ready.sem, cmp_s_ready.at(l, half + 1))
                    ins = stt(T[:, half, :], bank[2 + half][:], HD ** -0.5,
                              cmp_bias[:, half, :, :, :].rearrange("p t h n -> p (t h n)"),
                              ALU.mult, ALU.add)
                steps.done(ins)
                t4 = T[:].rearrange("p a (b n) -> p (a b) n", n=32)
                steps.done(nc.vector.tensor_reduce(cmp_max[:], t4, AX_X, ALU.max))
                tt(t4, t4, wide(cmp_max[:], 32), ALU.subtract).then_inc(cmp_t_done.sem, 1)
                dve.wait_ge(q_hi_done.sem, q_hi_done.at(l, 1))
                tt(q_lo[:], U[:, U_Q:U_Q + HEADS // 2, :], q_hi[:].bitcast(F32), ALU.subtract).then_inc(q_lo_done.sem, 1)
                dve.wait_ge(cmp_p_done.sem, cmp_p_done.at(l, 1))
                p4 = PR[:].rearrange("p a (b n) -> p (a b) n", n=32)
                steps.done(nc.vector.tensor_reduce(cmp_sum[:], p4, AX_X, ALU.add))
                for par in range(2):
                    pt4 = PR[:, par, :].rearrange("p (t h n) -> p t h n", t=ST, n=32)
                    ins = tt(pt4, pt4, cmp_mask[:].unsqueeze(2).to_broadcast([P, ST, 4, 32]), ALU.mult)
                ins.then_inc(cmp_pm_done.sem, 1)

                steps.done(nc.vector.reciprocal(cmp_sum[:], cmp_sum[:]))
                c3 = cmp_sum[:].rearrange("p (a t h) -> p a t h", a=2, t=ST)
                g4 = gates[:].rearrange("p t (h a c) -> p a t h c", a=2, c=3)
                dve.wait_ge(tm_taken.sem, tm_taken.at(l, 1))
                steps.done(tt(c3, c3, g4[:, :, :, :, 0], ALU.mult))
                dve.wait_ge(cmp_o_ready.sem, cmp_o_ready.at(l, 1))
                for t in range(ST):
                    ins = tt(o_all[:, t, 0:HEADS, :].rearrange("p (h a) d -> p a h d", a=2),
                             bank[2 + t][:].rearrange("p (a h d) -> p a h d", a=2, h=4), wide(c3[:, :, t, :], HD),
                             ALU.mult)
                ins.then_inc(cmp_o_done.sem, 1)

                def exponent(n):
                    h, j = n // ST, n % ST
                    if j == 0:
                        dve.wait_ge(ml_m_ready.sem, ml_m_ready.at(l, h + 1))
                    ts(ml_e[:, n % 2, 0:S - j * P], bank[6][:, j * P:S], bcol[:, j, h:h + 1], 0.0, ALU.add, ALU.min)\
                        .then_inc(ml_d_done.sem, 1)

                exponent(0)
                for n in range(16):
                    if n + 1 < 16:
                        exponent(n + 1)
                    w = S - (n % ST) * P
                    dve.wait_ge(ml_e_done.sem, ml_e_done.at(l, n + 1))
                    dve.wait_ge(ml_s_ready.sem, ml_s_ready.at(l, n + 1))
                    dve.wait_ge(ml_pv.sem, ml_pv.at(l, n - 1))
                    steps.done(stt(ml_w[:, n % 2, 0:w], ml_e[:, n % 2, 0:w], HD ** -0.5, bank[n % 2][:, 0:w],
                                   ALU.mult, ALU.mult))
                    tt(ml_w[:, n % 2, 0:P], ml_w[:, n % 2, 0:P], causal[:], ALU.mult).then_inc(ml_w_done.sem, 1)
                dve.wait_ge(ml_pv.sem, ml_pv.at(l, 16))
                dve.wait_ge(ml_em.sem, ml_em.at(l, 1))
                acc = [bank[2 + t][:, 0:4 * (HD + 1)].rearrange("p (h d) -> p h d", h=4) for t in range(ST)]
                for t in range(ST):
                    ins = nc.vector.tensor_copy(den[:, t, :], acc[t][:, :, HD])
                steps.done(ins)
                steps.done(stt(den[:], den[:], -1.0, den[:], ALU.mult, ALU.max))
                steps.done(tt(den[:], den[:], em[:], ALU.max))
                steps.done(nc.vector.reciprocal(den[:], den[:]))
                for t in range(ST):
                    ins = tt(o_all[:, t, HEADS:12, :], acc[t][:, :, 0:HD], wide(den[:, t, :], HD), ALU.mult)
                ins.then_inc(ml_o_done.sem, 1)
                dve.wait_ge(ml_o_done.sem, ml_o_done.at(l, 1))
                dve.wait_ge(o_sig_done.sem, o_sig_done.at(l, 1))
                steps.done(tt(o_all[:, :, HEADS:12, :], o_all[:, :, HEADS:12, :],
                              o_sig[:].rearrange("p t (h d) -> p t h d", h=4), ALU.mult)).then_inc(waits_met.sem, 1)

                done_before = steps.n
                PASS_STEPS = 16 + 4
                with dve.Fori(0, 2) as b:
                    with dve.Fori(0, 2) as g:
                        kv = b * 2 + g
                        pas = l * 64 + kv * 16
                        steps.base, steps.n = l * DVE_STEPS + before + kv * PASS_STEPS, done_before
                        for u in range(16):
                            h, i = u // ST, u % ST
                            w = (i + 1) * P
                            dve.wait_ge(att_s_ready.sem, pas + u + 17)
                            dve.wait_ge(att_exp_done.sem, pas + u + 1)
                            steps.done(stt(T[:, u % 2, 0:w], dist[:, S - w:S], neg_slope[:, bass.ds(g * HPG + h, 1)],
                                           bank[u % 4][:, 0:w], ALU.mult, ALU.add))
                            nc.vector.tensor_reduce(n_max[:, u:u + 1], T[:, u % 2, 0:w], AX_X, ALU.max, negate=True)\
                                .then_inc(att_scored.sem, 1)
                        dve.wait_ge(att_exp_done.sem, pas + 18)
                        steps.done(nc.vector.reciprocal(rec[:], sums[:, kv, :]))
                        gv = gates[:].rearrange("p t (h c) -> p c h t", c=3)
                        gv = gv[:, bass.ds(b + 1, 1), bass.ds(g * HPG, HPG), :].rearrange("p a h t -> p (a h) t")
                        steps.done(tt(coef[:].rearrange("p (h t) -> p h t", h=HPG), rec[:].rearrange("p (h t) -> p h t", h=HPG),
                                      gv, ALU.mult))
                        dve.wait_ge(att_pv_ready.sem, pas + 18)
                        for n in range(2):
                            ins = tt(att_o[:, n, :].rearrange("p (u d) -> p u d", u=8),
                                     bank[6 + n][:].rearrange("p (u d) -> p u d", u=8), wide(coef[:, 8 * n:8 * n + 8], HD),
                                     ALU.mult)
                        steps.done(ins)
                        for n in range(2):
                            o = o_all[:].rearrange("p t h d -> p h t d")[:, bass.ds(g * HPG + 2 * n, 2), :, :]
                            ins = tt(o, o, att_o[:, n, :].rearrange("p (h t d) -> p h t d", h=2, t=ST), ALU.add)
                            if n == 0:
                                steps.done(ins)
                        ins.then_inc(acc_taken.sem, 1)
                        dve.wait_ge(acc_taken.sem, l * 4 + kv + 2)
                        assert steps.n == done_before + PASS_STEPS
                steps.base, steps.n = l * DVE_STEPS + before, done_before + 4 * PASS_STEPS

                dve.wait_ge(o_sq_done.sem, o_sq_done.at(l, 1))
                steps.done(nc.vector.tensor_reduce(h_ss[:], o_sq[:], AX_X, ALU.add))
                ts(h_ms[:], h_ss[:], 1.0 / HD, EPS, ALU.mult, ALU.add).then_inc(o_ms_done.sem, 1)
                dve.wait_ge(o_root.sem, o_root.at(l, 1))
                steps.done(nc.vector.reciprocal(h_rs[:], h_ms[:]))
                o3 = o_all[:].rearrange("p t h d -> p (t h) d")
                tt(o3, o3, wide(h_rs[:], HD), ALU.mult).then_inc(o_normed.sem, 1)
                for c in range(2):
                    dve.wait_ge(lru_hi_done.sem, lru_hi_done.at(l, c + 1))
                    tt(h_lo[:, 4 + c, :], U[:, U_GR + c, :], h_hi[:, 4 + c, :].bitcast(F32), ALU.subtract)\
                        .then_inc(lru_lo_done.sem, 1)
                for n in range(6):
                    k = n if n < 4 else n + 2
                    dve.wait_ge(h_hi_done.sem, h_hi_done.at(l, n + 1))
                    stt(h_lo[:, k, :], bank[n % 4][:], head_gain[:, l, k:k + 1], h_hi[:, k, :].bitcast(F32),
                        ALU.mult, ALU.subtract).then_inc(h_lo_done.sem, 1)
                steps.done(nc.vector.memset(sumsq[:], 0.0)).then_inc(waits_met.sem, 1)
                with dve.Fori(0, DT // 2) as j:
                    project(N_OUT, DT, 3 * l + 2, j, 1, 1.0, (UP_W, UP_W))
                ffn(1, N_UP2, N_DN2, 2 * DT, 3 * l + 3, 0)
                assert steps.n == DVE_STEPS, steps.n
            norm_finish(LAYERS, 0)
            for m in range(DT):
                stt(resid[:, m, :], resid[:, m, :], gains[:, 3 * LAYERS, m:m + 1], rstd[:], ALU.mult, ALU.mult)\
                    .then_inc(out_ready.sem, 1)


MIX_BYTES, SMALL_BYTES = 98368, 5120
DVE_STEPS = 144
CONST_LOADS = 6


def wide(ap, n):
    return ap.unsqueeze(len(ap.shape)).to_broadcast([*ap.shape, n])


def block_halves(src, par):
    v = src.rearrange("p (n c two) -> p two c n", two=2, c=8)[:, par, :, :]
    return (slice(0, 8), v[:, :, 0:NCMP]), (slice(8, 16), v[:, :, 1:NCMP + 1])


def kernel(**inputs):
    import numpy as np
    import concourse.bacc as bacc
    from concourse.bass_utils import run_bass_kernel_spmd

    a = {k: np.asarray(v) for k, v in inputs.items()}
    L = LAYERS

    def tiles(w, kt, mt):
        return w.reshape(L, kt, P, mt, P).transpose(0, 3, 2, 1, 4).reshape(L, mt, P, kt * P)

    def down(w):
        w = w.reshape(L, 2, FH, P, DT, P).transpose(0, 4, 1, 3, 2, 5)
        return w.reshape(L, DT, 2, P, FH * P)

    def up(w1, w3):
        return np.stack([tiles(w1, DT, FT), tiles(w3, DT, FT)], axis=2)

    w = a["w_in"]
    fm = np.concatenate([w[:, :, 1304:1816], w[:, :, 0:768], w[:, :, 768:896], w[:, :, 1024:1152], w[:, :, 1816:2328]],
                        axis=2)
    tm = np.concatenate([w[:, :, 896:1024], w[:, :, 1152:1280], w[:, :, 1280:1304], w[:, :, 2584:2592],
                         w[:, :, 2328:2584], w[:, :, 2592:2848]], axis=2)

    def cols(v, n):
        return v.reshape(*v.shape[:-1], n, P)

    gains = np.stack([a["ffn1_norm"], a["mix_norm"], a["ffn2_norm"]], axis=1).reshape(3 * L, 1024)
    gains = cols(np.concatenate([gains, a["final_norm"][None]], axis=0), DT).transpose(2, 0, 1)
    lru = [cols(a["lru_conv_w"], 2)[:, t] for t in range(4)] +           [cols(a[k].reshape(L, 256), 2) for k in ("lru_conv_b", "lru_b_a", "lru_b_x", "lru_lambda")]
    gate = np.stack([a["lru_w_a"], a["lru_w_x"]], axis=1).reshape(L, 2, 2, 2, HD, HD)
    arrays = {
        "x": a["x"][0].T.reshape(DT, P, S).transpose(1, 0, 2),
        "up1": up(a["ffn1_w1"], a["ffn1_w3"]), "down1": down(a["ffn1_w2"]),
        "up2": up(a["ffn2_w1"], a["ffn2_w3"]), "down2": down(a["ffn2_w2"]),
        "w_in": tiles(fm, DT, WIN_TILES), "w_tm": tm.reshape(L, DT, P, TM_W),
        "w_out": tiles(a["w_out"], DT, DT),
        "cmp_w1": np.stack([a["nsa_cmp_w1_k"], a["nsa_cmp_w1_v"]], axis=1).reshape(L, 2, CP, P, 256)
                    .transpose(0, 1, 3, 2, 4),
        "gains": gains,
        "head_gain": cols(a["head_norm"].reshape(L, 1024), DT).transpose(2, 0, 1),
        "lru_par": np.stack(lru, axis=-1).transpose(2, 0, 1, 3),
        "gate_w": gate.transpose(3, 4, 0, 1, 2, 5).reshape(P, L, 4, HD),
        "cmp_pos": np.tile(np.stack([a["nsa_cmp_pos_k"], a["nsa_cmp_pos_v"]], axis=1).reshape(L, 2, CP, 2, HD)
                           .transpose(4, 0, 1, 3, 2), (2, 1, 1, 1, 1)),
        "cmp_w2": np.stack([a["nsa_cmp_w2_k"], a["nsa_cmp_w2_v"]], axis=1).reshape(L, 2, 2, P, HD)
                    .transpose(3, 0, 1, 2, 4),
        "ml_bias": np.stack([a["ml_b_i"], a["ml_b_f"]], axis=-1).transpose(1, 0, 2),
    }
    arrays = {k: np.ascontiguousarray(v) for k, v in arrays.items()}
    nc = bacc.Bacc("TRN2", target_bir_lowering=False, num_devices=1)
    d = {k: nc.dram_tensor(f"{k}_dram", v.shape, F32, kind="ExternalInput").ap() for k, v in arrays.items()}
    out = nc.dram_tensor("out_dram", (P, DT, S), F32, kind="ExternalOutput").ap()
    build(nc, d, out)
    got = run_bass_kernel_spmd(nc, [{f"{k}_dram": v for k, v in arrays.items()}], core_ids=[0]).results[0]["out_dram"]
    return np.ascontiguousarray(got.transpose(2, 1, 0)).reshape(1, S, 1024)
```

```python
from contextlib import ExitStack

import concourse.bass as bass
from concourse import mybir

F32 = mybir.dt.float32
F32R = mybir.dt.float32r
ALU = mybir.AluOpType
ACT = mybir.ActivationFunctionType
AX_X = mybir.AxisListType.X

P = 128
LAYERS = 2
S = 512
ST = S // P
DT = 1024 // P
FT = 2816 // P
FH = FT // 2
HD = 64
EPS = 1e-6
HEADS = 8
HPG = 4
NCMP = (S - 32) // 16 + 1
CP = 16
MASKED = 1e33
WIN_TILES = 16
U_XR, U_GR, U_Q, U_KC, U_VC, U_KS, U_QM, U_KM = 0, 2, 4, 8, 9, 10, 12, 14
TM_A, TM_B = 288, 512
UP_W, DOWN_W, TM_W = DT * P, FH * P, TM_A + TM_B
N_UP1, N_DN1, N_WIN, N_TM, N_OUT, N_UP2, N_DN2, N_CHUNKS = 0, 44, 60, 76, 84, 92, 136, 152


class Signal:

    def __init__(self, sem, before, per_layer):
        self.sem, self.before, self.per_layer = sem, before, per_layer

    def at(self, layer, count):
        return layer * self.per_layer + self.before + count


class Steps:

    def __init__(self, eng, sem):
        self.eng, self.sem, self.base, self.n = eng, sem, 0, 0

    def mark(self, ins):
        ins.then_inc(self.sem, 1)
        self.n += 1
        return self.base + self.n

    def done(self, ins):
        return self.eng.wait_ge(self.sem, self.mark(ins))


def build(nc, d, out):
    ctx = ExitStack()
    with ctx:
        enter = ctx.enter_context

        def sb(name, shape, dt=F32):
            return enter(nc.sbuf_tensor(name, shape, dt))

        resid = sb("resid", [P, DT, S])
        raw = [sb(f"raw{s}", [P, DOWN_W]) for s in range(2)]
        w_hi = [sb(f"w_hi{s}", [P, DOWN_W], F32R) for s in range(2)]
        w_lo = [sb(f"w_lo{s}", [P, DOWN_W], F32R) for s in range(2)]
        rstd = sb("rstd", [P, S])
        sumsq = sb("sumsq", [P, S])
        mean_sq = sumsq
        ones = sb("ones", [P, P])
        ident = sb("ident", [P, P])
        halves = sb("halves", [P, P])
        causal = sb("causal", [P, P])
        dist = sb("dist", [P, S])
        cmp_bias = sb("cmp_bias", [P, 2, ST, 4, 32])
        cmp_mask = sb("cmp_mask", [P, ST, 32])
        neg_slope = sb("neg_slope", [P, HEADS])
        pick = sb("pick", [4, 4, P])
        gains = sb("gains", [P, 7, DT])
        head_gain = sb("head_gain", [P, LAYERS, DT])
        lru_par = sb("lru_par", [P, LAYERS, 2, 8])
        gate_w = sb("gate_w", [P, LAYERS, 4, HD])
        gate_bd = sb("gate_bd", [P, 4, P])
        cmp_pos = sb("cmp_pos", [P, LAYERS, 2, 2, CP])
        cmp_w2 = sb("cmp_w2", [P, LAYERS, 2, 2, HD])
        w2cur = sb("w2cur", [P, 2, 2, HD])
        ml_bias = sb("ml_bias", [4, LAYERS, 2])
        kcT = sb("kcT", [P, 2, 32])
        vc_bd = sb("vc_bd", [P, 256])

        top = [nc.sbuf_base]

        def region(size):
            at = (top[0] + 63) // 64 * 64
            top[0] = at + size
            return at

        def at(name, offset, shape, dt=F32):
            return nc.alloc_sbuf_tensor_at(name, shape, dt, offset=offset)

        x_area = region(2 * DT * S * 4)
        x_hi = at("x_hi", x_area, [P, DT, S], F32R)
        x_lo = at("x_lo", x_area + DT * S * 4, [P, DT, S], F32R)
        rows = [at(f"row{i}", x_area + i * 2048, [4, S]) for i in range(6)]
        k_hi = at("k_hi", x_area + 12288, [P, 4, S], F32R)
        k_lo = at("k_lo", x_area + 20480, [P, 4, S], F32R)

        mix = region(MIX_BYTES)
        hid_hi = at("hid_hi", mix, [P, FT, S], F32R)
        hid_lo = at("hid_lo", mix + FT * S * 4, [P, FT, S], F32R)
        tmp0 = mix + 2 * FT * S * 4
        g_scaled = at("g_scaled", tmp0, [P, S])
        g_silu = at("g_silu", tmp0 + 2048, [P, S])
        u_scaled = at("u_scaled", tmp0 + 4096, [P, S])
        sq = at("sq", tmp0 + 2048, [P, 2, S])
        hidden = at("hidden", tmp0 + 6144, [P, S])

        U = at("U", mix, [P, WIN_TILES, S])
        h_hi = at("h_hi", mix, [P, DT, S], F32R)
        h_lo = at("h_lo", mix + 16384, [P, DT, S], F32R)
        m1 = mix + 32768
        r1 = m1
        lru = [at(f"lru{i}", r1 + i * 4096, [P, 2, S]) for i in range(5)]
        cmp_w1 = [at(f"cmp_w1_{i}", r1 + i * 16384, [P, CP, 256]) for i in range(2)]
        T = at("T", r1, [P, 2, S])
        PR = at("PR", r1 + 4096, [P, 2, S])
        PT = at("PT", r1 + 8192, [P, 2, S])
        q_head = [at(f"q_head{i}", r1 + 12288 + i * 2048, [P, S], F32R) for i in range(4)]
        ml_e = at("ml_e", r1 + 20480, [P, 2, S])
        ml_w = at("ml_w", r1 + 24576, [P, 2, S])
        att_o = at("att_o", r1 + 28672, [P, 2, S])
        cmp_act = at("cmp_act", r1 + 28672, [2 * NCMP, 2, 256])
        o_sq = at("o_sq", r1, [P, ST * 12, HD])
        m2 = m1 + 32768
        q_hi = at("q_hi", m2, [P, HEADS // 2, S], F32R)
        q_lo = at("q_lo", mix + U_Q * S * 4, [P, HEADS // 2, S], F32R)
        v_all = at("v_all", m2 + 8192, [P, 4, ST, HD])
        v_aug = at("v_aug", m2 + 12288, [P, ST, 4, HD + 1])
        o_sig = at("o_sig", m2 + 16448, [P, ST, 256])
        o_all = at("o_all", m2 + 20544, [P, ST, 12, HD])
        zc = [at(f"zc{i}", m2 + 20544 + i * 4096, [P, CP, 2 * NCMP]) for i in range(2)]
        assert m2 + 20544 + 12288 <= mix + MIX_BYTES
        assert tmp0 + 8192 <= mix + MIX_BYTES
        small = region(SMALL_BYTES)

        def sm(name, shape, state=[0]):
            n = 4
            for k in shape[1:]:
                n *= k
            t = at(name, small + state[0], shape)
            state[0] += (n + 31) // 32 * 32
            assert state[0] <= SMALL_BYTES
            return t

        rcol = sm("rcol", [P, ST])
        gates = sm("gates", [P, ST, 24])
        ifcol = sm("ifcol", [P, ST, 8])
        cmp_hid = sm("cmp_hid", [P, 2, 2, 62])
        cmp_max = sm("cmp_max", [P, 32])
        cmp_sum = sm("cmp_sum", [P, 32])
        n_max = sm("n_max", [P, 16])
        sums = sm("sums", [P, 4, 16])
        rec = sm("rec", [P, 16])
        coef = sm("coef", [P, 16])
        sp4 = sm("sp4", [P, 2])
        sp8 = sm("sp8", [P, 2])
        spt = sm("spt", [P, 6, 2])
        bcol = sm("bcol", [P, ST, 8])
        em = sm("em", [P, ST, 4])
        den = sm("den", [P, ST, 4])
        h_ss = sm("h_ss", [P, ST * 12])
        h_ms = sm("h_ms", [P, ST * 12])
        h_rs = sm("h_rs", [P, ST * 12])

        bank = [enter(nc.psum_tensor(f"bank{i}", [P, 512], F32)) for i in range(8)]

        def signal(name, per_layer, before=0):
            return Signal(enter(nc.semaphore(name)), before, per_layer)

        consts_loaded = signal("consts_loaded", 0)
        gains_loaded = signal("gains_loaded", 0)
        x_loaded = [signal(f"x_loaded{i}", 0) for i in range(2)]
        pool_consts = signal("pool_consts", 0)
        pool_zero = signal("pool_zero", 0)
        dve_consts = signal("dve_consts", 0)
        w_loaded = [signal(f"w_loaded{s}", 16 * N_CHUNKS // 2) for s in range(2)]
        w_hi_done = signal("w_hi_done", N_CHUNKS)
        w_lo_done = signal("w_lo_done", N_CHUNKS, 2)
        chunk_done = signal("chunk_done", N_CHUNKS, 2)
        resid_ready = signal("resid_ready", 24, 2)
        x_hi_done = signal("x_hi_done", 24, 8)
        x_lo_done = signal("x_lo_done", 24, 8)
        sq_ready = signal("sq_ready", 24, 8)
        sq_added = signal("sq_added", 24, 8 + 2)
        norm_sum = signal("norm_sum", 3)
        mean_ready = signal("mean_ready", 3)
        root_ready = signal("root_ready", 3)
        rstd_ready = signal("rstd_ready", 3)
        g_scaled_done = signal("g_scaled_done", 2 * FT, 1)
        silu_done = signal("silu_done", 2 * FT)
        u_scaled_done = signal("u_scaled_done", 2 * FT, 1)
        hidden_ready = signal("hidden_ready", 2 * FT)
        hidden_hi = signal("hidden_hi", 2 * FT)
        hidden_lo = signal("hidden_lo", 2 * FT)
        u_done = signal("u_done", WIN_TILES)
        rcol_ready = signal("rcol_ready", 1)
        rcol_done = signal("rcol_done", 1)
        tm_taken = signal("tm_taken", 1)
        tm_values_taken = signal("tm_values_taken", 1)
        o_sig_done = signal("o_sig_done", 1)
        cmp_w_loaded = [signal(f"cmp_w_loaded{i}", 4 * 16) for i in range(2)]
        layer_w_ready = signal("layer_w_ready", 1)
        k_hi_done = signal("k_hi_done", 4)
        k_lo_done = signal("k_lo_done", 4)
        q_hi_done = signal("q_hi_done", 1)
        q_lo_done = signal("q_lo_done", 1)
        zc_ready = [signal(f"zc_ready{i}", 1) for i in range(2)]
        cmp_h_ready = signal("cmp_h_ready", 1)
        cmp_act_done = signal("cmp_act_done", 1)
        cmp_t_ready = signal("cmp_t_ready", 1)
        cmp_hid_done = signal("cmp_hid_done", 1)
        cmp_kv_ready = signal("cmp_kv_ready", 1)
        cmp_kv_done = signal("cmp_kv_done", 1)
        cmp_s_ready = signal("cmp_s_ready", 2)
        cmp_t_done = signal("cmp_t_done", 1)
        cmp_p_done = signal("cmp_p_done", 1)
        cmp_pm_done = signal("cmp_pm_done", 1)
        cmp_tr_ready = signal("cmp_tr_ready", 1)
        cmp_pt_done = signal("cmp_pt_done", 1)
        cmp_o_ready = signal("cmp_o_ready", 1)
        cmp_o_done = signal("cmp_o_done", 1)
        conv_done = signal("conv_done", 2)
        lru_g_ready = signal("lru_g_ready", 2)
        lru_gates_done = signal("lru_gates_done", 2)
        sp_exp = signal("sp_exp", 1)
        sp_arg = signal("sp_arg", 2)
        sp_ln = signal("sp_ln", 1)
        sp_done = signal("sp_done", 1)
        lru_decay = signal("lru_decay", 1)
        lru_tanh = signal("lru_tanh", 1)
        lru_sqrt = signal("lru_sqrt", 1)
        lru_gelu = signal("lru_gelu", 1)
        lru_out = signal("lru_out", 1)
        lru_sq_done = signal("lru_sq_done", 1)
        lru_ms_ready = signal("lru_ms_ready", 1)
        lru_ms_done = signal("lru_ms_done", 1)
        lru_root = signal("lru_root", 1)
        lru_normed = signal("lru_normed", 2)
        lru_hi_done = signal("lru_hi_done", 2)
        lru_lo_done = signal("lru_lo_done", 2)
        q_loaded = [signal(f"q_loaded{i}", 4 * 32) for i in range(4)]
        att_s_ready = signal("att_s_ready", 64, 16)
        att_scored = signal("att_scored", 64, 4)
        att_exp_done = signal("att_exp_done", 64, 2)
        att_tr_ready = signal("att_tr_ready", 64, 2)
        att_copied = signal("att_copied", 64, 2)
        att_pv_ready = signal("att_pv_ready", 64, 2)
        acc_taken = signal("acc_taken", 8, 2)
        if_t_ready = signal("if_t_ready", 1)
        ml_abs = signal("ml_abs", 1)
        ml_exp = signal("ml_exp", 1)
        ml_arg = signal("ml_arg", 1)
        ml_ln = signal("ml_ln", 1)
        ml_rows = signal("ml_rows", 1)
        ml_cols_ready = signal("ml_cols_ready", 1)
        ml_cols_done = signal("ml_cols_done", 1)
        ml_em = signal("ml_em", 1)
        ml_m_ready = signal("ml_m_ready", 4)
        ml_d_done = signal("ml_d_done", 16, 0)
        ml_e_done = signal("ml_e_done", 16, 0)
        ml_s_ready = signal("ml_s_ready", 16)
        ml_w_done = signal("ml_w_done", 16, 2)
        ml_pv = signal("ml_pv", 16, 2)
        ml_o_done = signal("ml_o_done", 1)
        o_sq_done = signal("o_sq_done", ST)
        o_ms_done = signal("o_ms_done", 1)
        o_root = signal("o_root", 1)
        o_normed = signal("o_normed", ST)
        h_t_ready = signal("h_t_ready", 6)
        h_hi_done = signal("h_hi_done", 6)
        h_lo_done = signal("h_lo_done", 6, 0)
        dve_step = signal("dve_step", 0)
        waits_met = signal("waits_met", 0)
        out_ready = signal("out_ready", 0)
        out_stored = signal("out_stored", 0)

        def wait_alone(eng, sem, value):
            eng.wait_ge(sem, value).then_inc(waits_met.sem, 1)

        block = enter(nc.Block())

        @block.sync
        def _(sp):
            for i in range(2):
                half = slice(DT // 2 * i, DT // 2 * (i + 1))
                sp.dma_start(resid[:, half, :], d["x"][:, half, :]).then_inc(x_loaded[i].sem, 16)

            def stream(l, n, slot, src):
                sp.wait_ge(w_lo_done.sem, l * N_CHUNKS + n + 1)
                sp.dma_start(raw[slot][:, 0:src.shape[1]], src).then_inc(w_loaded[slot].sem, 16)

            with sp.Fori(0, LAYERS) as l:
                def ffn(up, down, n_up, n_down):
                    with sp.Fori(0, FT) as m:
                        for s in range(2):
                            stream(l, n_up + 2 * m + s, s, up[l, m, s])
                    with sp.Fori(0, DT) as m:
                        for s in range(2):
                            stream(l, n_down + 2 * m + s, s, down[l, m, s])

                ffn(d["up1"], d["down1"], N_UP1, N_DN1)
                with sp.Fori(0, WIN_TILES // 2) as j:
                    for s in range(2):
                        stream(l, N_WIN + 2 * j + s, s, d["w_in"][l, 2 * j + s])
                def piece(n):
                    part = slice(n % 4 * 4, n % 4 * 4 + 4)
                    sp.dma_start(cmp_w1[n // 4][:, part, :], d["cmp_w1"][l, n // 4, :, part, :])\
                        .then_inc(cmp_w_loaded[n // 4].sem, 16)

                for k in range(DT):
                    stream(l, N_TM + k, k % 2, d["w_tm"][l, k])
                    if k == 2:
                        sp.wait_ge(lru_normed.sem, lru_normed.at(l, 2))
                    if k >= 2:
                        piece(k - 2)
                piece(DT - 2)
                piece(DT - 1)
                for s in range(2):
                    stream(l, N_OUT + s, s, d["w_out"][l, s])
                with sp.Fori(1, DT // 2) as j:
                    for s in range(2):
                        stream(l, N_OUT + 2 * j + s, s, d["w_out"][l, 2 * j + s])
                ffn(d["up2"], d["down2"], N_UP2, N_DN2)
            for m in range(DT):
                sp.wait_ge(out_ready.sem, m + 1)
                sp.dma_start(out[:, m, :], resid[:, m, :]).then_inc(out_stored.sem, 16)
            sp.wait_ge(out_stored.sem, 16 * DT)

        @block.gpsimd
        def _(pool):
            pool.dma_start(gains[:], d["gains"]).then_inc(gains_loaded.sem, 16)
            loads = [(head_gain, "head_gain"), (lru_par, "lru_par"), (gate_w, "gate_w"),
                     (cmp_pos, "cmp_pos"), (cmp_w2, "cmp_w2"), (ml_bias, "ml_bias")]
            for t, name in loads:
                pool.dma_start(t[:], d[name]).then_inc(consts_loaded.sem, 16)
            zero = 0
            for t, v in [(ones, 1.0), (ident, 0.0), (halves, 0.0), (causal, 1.0), (cmp_mask, 1.0),
                         (pick, 1.0), (gate_bd, 0.0), (kcT, 0.0), (vc_bd, 0.0)]:
                nc.gpsimd.memset(t[:], v).then_inc(pool_zero.sem, 1)
                zero += 1
            nc.gpsimd.iota(dist[:], pattern=[[-1, S]], base=S - P, channel_multiplier=1,
                           allow_small_or_imprecise_dtypes=True).then_inc(pool_zero.sem, 1)
            nc.gpsimd.iota(cmp_bias[:], pattern=[[0, 2], [P, ST], [0, 4], [-16, 32]], base=-31, channel_multiplier=1,
                           allow_small_or_imprecise_dtypes=True).then_inc(pool_zero.sem, 1)
            for h in range(HEADS):
                nc.gpsimd.memset(neg_slope[:, h:h + 1], -(2.0 ** -(h + 1))).then_inc(pool_zero.sem, 1)
            zero += 2 + HEADS
            pool.wait_ge(pool_zero.sem, zero)
            sel = nc.gpsimd.affine_select
            sel(out=ident[:], in_=ident[:], compare_op=ALU.not_equal, fill=1.0, base=0, pattern=[[-1, P]],
                channel_multiplier=1).then_inc(pool_consts.sem, 1)
            sel(out=causal[:], in_=causal[:], compare_op=ALU.is_ge, fill=0.0, base=0, pattern=[[1, P]],
                channel_multiplier=-1).then_inc(pool_consts.sem, 1)
            sel(out=dist[:], in_=dist[:], compare_op=ALU.is_ge, fill=MASKED, base=S - P, pattern=[[-1, S]],
                channel_multiplier=1).then_inc(pool_consts.sem, 1)
            sel(out=cmp_bias[:], in_=cmp_bias[:], compare_op=ALU.is_ge, fill=MASKED, base=-31,
                pattern=[[0, 2], [P, ST], [0, 4], [-16, 32]], channel_multiplier=1).then_inc(pool_consts.sem, 1)
            sel(out=cmp_mask[:], in_=cmp_mask[:], compare_op=ALU.is_ge, fill=0.0, base=-31,
                pattern=[[P, ST], [-16, 32]], channel_multiplier=1).then_inc(pool_consts.sem, 1)
            sel(out=pick[:], in_=pick[:], compare_op=ALU.is_equal, fill=0.0, base=0, pattern=[[-1, 4], [0, P]],
                channel_multiplier=1).then_inc(pool_consts.sem, 1)

            with pool.Fori(0, LAYERS) as l:
                pool.wait_ge(q_hi_done.sem, q_hi_done.at(l, 1))
                wait_alone(pool, q_lo_done.sem, q_lo_done.at(l, 1))
                with pool.Fori(0, 2) as b:
                    with pool.Fori(0, 2) as g:
                        for h in range(HPG):
                            pool.wait_ge(att_s_ready.sem, l * 64 + (b * 2 + g) * 16 + 4 * h + 4)
                            for part, q in enumerate((q_hi, q_lo)):
                                pool.dma_start(q_head[h][HD * part:HD * part + HD, :],
                                             q[HD * (h % 2):HD * (h % 2) + HD, g * 2 + h // 2, :])\
                                  .then_inc(q_loaded[h].sem, 16)

        POOL_CONSTS = 6

        @block.tensor
        def _(pe):
            mm = nc.tensor.matmul
            pe.sem_inc(chunk_done.sem, 2)
            pe.sem_inc(att_s_ready.sem, 16)
            pe.sem_inc(att_tr_ready.sem, 2)
            pe.sem_inc(att_pv_ready.sem, 2)
            pe.sem_inc(ml_pv.sem, 2)
            pe.wait_ge(pool_consts.sem, POOL_CONSTS)
            pe.wait_ge(dve_consts.sem, 1)

            def product(slot, tiles, a_hi, a_lo, k0, dst, first, last, tile_wait=None):
                for k in range(tiles):
                    if tile_wait is not None:
                        tile_wait(k)
                    wh = w_hi[slot][:, k * P:(k + 1) * P]
                    wl = w_lo[slot][:, k * P:(k + 1) * P]
                    mm(dst, wh, a_hi[:, k0 + k, :], start=first and k == 0, stop=False)
                    mm(dst, wh, a_lo[:, k0 + k, :], start=False, stop=False)
                    ins = mm(dst, wl, a_hi[:, k0 + k, :], start=False, stop=last and k == tiles - 1)
                return ins

            with pe.Fori(0, LAYERS) as l:
                def chunk_split(n):
                    pe.wait_ge(w_lo_done.sem, w_lo_done.at(l, n + 1))

                def norm(q):
                    pe.wait_ge(sq_added.sem, sq_added.at(l, 8 * q))
                    mm(bank[6][:, :], ones[:], sumsq[:], start=True, stop=True).then_inc(norm_sum.sem, 1)

                def up(f, n_up, m, first):
                    n = n_up + 2 * m
                    chunk_split(n)
                    pe.wait_ge(g_scaled_done.sem, g_scaled_done.at(l, f * FT + m))
                    wait = (lambda k: pe.wait_ge(x_lo_done.sem, x_lo_done.at(l, (16 * f - 8) + k + 1))) if first else None
                    product(0, DT, x_hi, x_lo, 0, bank[0][:], True, True, wait).then_inc(chunk_done.sem, 1)
                    if first:
                        norm(2 * f)
                    chunk_split(n + 1)
                    pe.wait_ge(u_scaled_done.sem, u_scaled_done.at(l, f * FT + m))
                    product(1, DT, x_hi, x_lo, 0, bank[1][:], True, True).then_inc(chunk_done.sem, 1)

                def down(f, n_down, j):
                    for i in range(2):
                        m = 2 * j + i
                        n = n_down + 2 * m
                        pe.wait_ge(resid_ready.sem, resid_ready.at(l, 16 * f + m - 1))
                        for s in range(2):
                            chunk_split(n + s)
                            pe.wait_ge(hidden_lo.sem, hidden_lo.at(l, f * FT + FH * (s + 1)))
                            product(s, FH, hid_hi, hid_lo, FH * s, bank[4 + i][:], s == 0, s == 1)\
                                .then_inc(chunk_done.sem, 1)

                up(0, N_UP1, 0, True)
                with pe.Fori(1, FT) as m:
                    up(0, N_UP1, m, False)
                with pe.Fori(0, DT // 2) as j:
                    down(0, N_DN1, j)

                def w_in(j, first):
                    for i in range(2):
                        chunk_split(N_WIN + 2 * j + i)
                        if not first:
                            pe.wait_ge(u_done.sem, u_done.at(l, 2 * j + i - 1))
                        wait = (lambda k: pe.wait_ge(x_lo_done.sem, x_lo_done.at(l, k + 1))) if first and i == 0 else None
                        product(i, DT, x_hi, x_lo, 0, bank[2 + i][:], True, True, wait).then_inc(chunk_done.sem, 1)
                        if first and i == 0:
                            norm(1)

                w_in(0, True)
                with pe.Fori(1, 5) as j:
                    w_in(j, False)
                pe.wait_ge(layer_w_ready.sem, layer_w_ready.at(l, 1))
                for c in range(2):
                    pe.wait_ge(conv_done.sem, conv_done.at(l, c + 1))
                    mm(bank[4 * c][:], gate_bd[:, c, :], lru[0][:, c, :], start=True, stop=True)
                    mm(bank[4 * c + 1][:], gate_bd[:, 2 + c, :], lru[0][:, c, :], start=True, stop=True)\
                        .then_inc(lru_g_ready.sem, 1)
                with pe.Fori(5, 7) as j:
                    w_in(j, False)
                pe.wait_ge(lru_sq_done.sem, lru_sq_done.at(l, 1))
                for c in range(2):
                    ins = mm(bank[c][:], halves[:], lru[1][:, c, :], start=True, stop=True)
                ins.then_inc(lru_ms_ready.sem, 1)
                w_in(WIN_TILES // 2 - 1, False)
                pe.wait_ge(rstd_ready.sem, rstd_ready.at(l, 2))
                for t in range(ST):
                    ins = mm(bank[6][:, t:t + 1], rstd[0:1, t * P:(t + 1) * P], ones[0:1, 0:1], start=True, stop=True)
                ins.then_inc(rcol_ready.sem, 1)
                pe.wait_ge(u_done.sem, u_done.at(l, WIN_TILES))
                pe.wait_ge(rcol_done.sem, rcol_done.at(l, 1))
                for k in range(DT):
                    chunk_split(N_TM + k)
                    wh, wl = w_hi[k % 2], w_lo[k % 2]
                    for t in range(ST):
                        xh, xl = (a[:, k, t * P:(t + 1) * P] for a in (x_hi, x_lo))
                        for x, w, part in ((xh, wh, 0), (xh, wl, 1), (xl, wh, 2)):
                            for half, (c0, c1) in enumerate(((0, TM_A), (TM_A, TM_W))):
                                ins = mm(bank[2 * t + half][:, 0:c1 - c0], x, w[:, c0:c1],
                                         start=k == 0 and part == 0, stop=k == DT - 1 and part == 2)
                    ins.then_inc(chunk_done.sem, 1)
                pe.wait_ge(tm_taken.sem, tm_taken.at(l, 1))

                pe.wait_ge(tm_values_taken.sem, tm_values_taken.at(l, 1))
                for t in range(ST):
                    nc.tensor.transpose(bank[6][0:4, t * P:(t + 1) * P], ifcol[:, t, 0:4], ident[:])
                for t in range(ST):
                    ins = nc.tensor.transpose(bank[7][0:4, t * P:(t + 1) * P], ifcol[:, t, 4:8], ident[:])
                ins.then_inc(if_t_ready.sem, 1)
                for kv in range(2):
                    pe.wait_ge(cmp_w_loaded[kv].sem, cmp_w_loaded[kv].at(l, 4 * 16))
                    pe.wait_ge(zc_ready[kv].sem, zc_ready[kv].at(l, 1))
                    for c in range(CP):
                        ins = mm(bank[2 + kv][0:2 * NCMP, 0:256], zc[kv][:, c, :], cmp_w1[kv][:, c, :],
                                 start=c == 0, stop=c == CP - 1)
                ins.then_inc(cmp_h_ready.sem, 1)
                wait_alone(pe, cmp_act_done.sem, cmp_act_done.at(l, 1))
                for n in range(4):
                    ins = nc.tensor.transpose(bank[4][:, n * 64:n * 64 + 2 * NCMP],
                                              cmp_act[:, n // 2, (n % 2) * P:(n % 2 + 1) * P],
                                              ident[0:2 * NCMP, 0:2 * NCMP])
                ins.then_inc(cmp_t_ready.sem, 1)
                wait_alone(pe, ml_rows.sem, ml_rows.at(l, 1))
                for t in range(ST):
                    nc.tensor.transpose(bank[6][:, t * 8:t * 8 + 4], rows[3][:, t * P:(t + 1) * P], ident[0:4, 0:4])
                    ins = nc.tensor.transpose(bank[6][:, t * 8 + 4:t * 8 + 8], rows[5][:, t * P:(t + 1) * P],
                                              ident[0:4, 0:4])
                ins.then_inc(ml_cols_ready.sem, 1)
                pe.wait_ge(cmp_hid_done.sem, cmp_hid_done.at(l, 1))
                for par in range(2):
                    for g in range(2):
                        for m in range(2):
                            mm(bank[3][HD * par:HD * par + HD, g * 32:g * 32 + NCMP], w2cur[:, 0, m, :],
                               cmp_hid[:, 0, m, g * NCMP:(g + 1) * NCMP], start=m == 0, stop=m == 1)
                for j in range(4):
                    g = j // 2
                    for m in range(2):
                        ins = mm(bank[5][32 * j:32 * j + NCMP, HD * j:HD * (j + 1)],
                                 cmp_hid[:, 1, m, g * NCMP:(g + 1) * NCMP], w2cur[:, 1, m, :],
                                 start=m == 0, stop=m == 1)
                ins.then_inc(cmp_kv_ready.sem, 1)
                pe.wait_ge(cmp_kv_done.sem, cmp_kv_done.at(l, 1))
                for t in range(ST):
                    for h in range(HEADS):
                        par = h % 2
                        hp = HD * par
                        o = (t * 4 + h // 2) * 32
                        ins = mm(bank[2 + par][:, o:o + 32], U[hp:hp + HD, U_Q + h // 2, t * P:(t + 1) * P],
                                 kcT[hp:hp + HD, h // HPG, :], start=True, stop=True)
                        if t == ST - 1 and h >= HEADS - 2:
                            ins.then_inc(cmp_s_ready.sem, 1)
                pe.wait_ge(cmp_pm_done.sem, cmp_pm_done.at(l, 1))
                for n in range(8):
                    ins = nc.tensor.transpose(bank[4 + n // 4][:, (n % 4) * P:(n % 4 + 1) * P],
                                              PR[:, n // 4, (n % 4) * P:(n % 4 + 1) * P], ident[:])
                ins.then_inc(cmp_tr_ready.sem, 1)
                pe.wait_ge(cmp_pt_done.sem, cmp_pt_done.at(l, 1))
                for t in range(ST):
                    for par in range(2):
                        ins = mm(bank[2 + t][:, par * 256:(par + 1) * 256], PT[:, par, t * P:(t + 1) * P], vc_bd[:],
                                 start=True, stop=True)
                ins.then_inc(cmp_o_ready.sem, 1)
                pe.wait_ge(cmp_o_done.sem, cmp_o_done.at(l, 1))
                pe.wait_ge(ml_cols_done.sem, ml_cols_done.at(l, 1))

                def ml_maxima(h):
                    if h >= 2:
                        pe.wait_ge(ml_d_done.sem, ml_d_done.at(l, ST * (h - 1)))
                    mm(bank[6 + h % 2][:], pick[:, h, :], rows[4][:], start=True, stop=True).then_inc(ml_m_ready.sem, 1)

                def ml_scores(n):
                    h, j = n // ST, n % ST
                    hp = HD * (h % 2)
                    pe.wait_ge(ml_w_done.sem, ml_w_done.at(l, n - 1))
                    mm(bank[n % 2][:, 0:S - j * P], U[hp:hp + HD, U_KM + h // 2, j * P:(j + 1) * P],
                       U[hp:hp + HD, U_QM + h // 2, j * P:S], start=True, stop=True).then_inc(ml_s_ready.sem, 1)

                ml_maxima(0)
                ml_scores(0)
                for n in range(16):
                    if n + 1 < 16:
                        ml_scores(n + 1)
                    if n % ST == 1 and n // ST + 1 < 4:
                        ml_maxima(n // ST + 1)
                    h, j = n // ST, n % ST
                    pe.wait_ge(ml_w_done.sem, ml_w_done.at(l, n + 1))
                    for i in range(j, ST):
                        ins = mm(bank[(2, 3, 4, 5)[i]][:, h * (HD + 1):(h + 1) * (HD + 1)],
                                 ml_w[:, n % 2, (i - j) * P:(i - j + 1) * P], v_aug[:, j, h, :],
                                 start=j == 0, stop=j == i)
                    ins.then_inc(ml_pv.sem, 1)

                pe.wait_ge(ml_o_done.sem, ml_o_done.at(l, 1))
                wait_alone(pe, k_lo_done.sem, k_lo_done.at(l, 4))

                def scores(kv, u):
                    h, i = u // ST, u % ST
                    if i == 0:
                        pe.wait_ge(q_loaded[h].sem, l * 128 + kv * 32 + 32)
                    wait_alone(pe, att_scored.sem, l * 64 + kv * 16 + u + 1)
                    w = (i + 1) * P
                    q = q_head[h][:, i * P:(i + 1) * P]
                    mm(bank[u % 4][:, 0:w], q, k_hi[:, kv, 0:w], start=True, stop=False)
                    mm(bank[u % 4][:, 0:w], q, k_lo[:, kv, 0:w], start=False, stop=True)\
                        .then_inc(att_s_ready.sem, 1)

                def flip(kv, u):
                    pe.wait_ge(att_exp_done.sem, l * 64 + kv * 16 + u + 3)
                    pe.wait_ge(att_copied.sem, l * 64 + kv * 16 + u + 1)
                    for j in range(u % ST + 1):
                        ins = nc.tensor.transpose(bank[4 + u % 2][:, j * P:(j + 1) * P],
                                                  PR[:, u % 2, j * P:(j + 1) * P], ident[:])
                    ins.then_inc(att_tr_ready.sem, 1)

                def values(kv, u):
                    pe.wait_ge(att_copied.sem, l * 64 + kv * 16 + u + 3)
                    i = u % ST
                    if u % 8 == 0:
                        pe.wait_ge(acc_taken.sem, l * 8 + kv * 2 + u // 8 + 1)
                    for j in range(i + 1):
                        ins = mm(bank[6 + u // 8][:, (u % 8) * HD:(u % 8 + 1) * HD],
                                 PT[:, u % 2, j * P:(j + 1) * P], v_all[:, kv, j, :],
                                 start=j == 0, stop=j == i)
                    ins.then_inc(att_pv_ready.sem, 1)

                def attention(kv, last):
                    for u in range(16):
                        if u + 3 < 16:
                            scores(kv, u + 3)
                        elif not last:
                            scores(kv + 1, u + 3 - 16)
                        flip(kv, u)
                        if u:
                            values(kv, u - 1)
                    values(kv, 15)

                for u in range(3):
                    scores(0, u)
                with pe.Fori(0, 3) as kv:
                    attention(kv, False)
                attention(3, True)

                def head_pair(n, t):
                    return nc.tensor.transpose(bank[n % 4][:, t * P:(t + 1) * P], o_all[:, t, 2 * n:2 * n + 2, :], ident[:])

                for t in range(ST):
                    pe.wait_ge(o_normed.sem, o_normed.at(l, t + 1))
                    for n in range(4):
                        ins = head_pair(n, t)
                        if t == ST - 1:
                            ins.then_inc(h_t_ready.sem, 1)
                for n in range(4, 6):
                    pe.wait_ge(h_lo_done.sem, h_lo_done.at(l, n - 3))
                    for t in range(ST):
                        ins = head_pair(n, t)
                    ins.then_inc(h_t_ready.sem, 1)

                wait_alone(pe, h_lo_done.sem, h_lo_done.at(l, 6))
                wait_alone(pe, lru_lo_done.sem, lru_lo_done.at(l, 2))

                def w_out(j):
                    for i in range(2):
                        chunk_split(N_OUT + 2 * j + i)
                        pe.wait_ge(resid_ready.sem, resid_ready.at(l, DT + 2 * j + i - 1))
                        product(i, DT, h_hi, h_lo, 0, bank[4 + i][:], True, True).then_inc(chunk_done.sem, 1)

                with pe.Fori(0, DT // 2) as j:
                    w_out(j)

                up(1, N_UP2, 0, True)
                with pe.Fori(1, FT) as m:
                    up(1, N_UP2, m, False)
                with pe.Fori(0, DT // 2) as j:
                    down(1, N_DN2, j)
            pe.wait_ge(sq_added.sem, sq_added.at(LAYERS, 0))
            mm(bank[6][:, :], ones[:], sumsq[:], start=True, stop=True).then_inc(norm_sum.sem, 1)

        @block.scalar
        def _(act):
            fn = nc.scalar.activation
            act.sem_inc(att_exp_done.sem, 2)
            act.sem_inc(att_copied.sem, 2)
            act.wait_ge(gains_loaded.sem, 16)

            def split_hi(l, n, half, slot, width):
                act.wait_ge(w_loaded[slot].sem, w_loaded[slot].at(l, 16 * half + 16))
                act.wait_ge(chunk_done.sem, chunk_done.at(l, n - 1))
                fn(w_hi[slot][:, 0:width], raw[slot][:, 0:width], ACT.Copy).then_inc(w_hi_done.sem, 1)

            def next_hi(l, n, half, s, width):
                split_hi(l, n + 2 + s, half + 1, s, width)

            def norm_input(l, r, m, q):
                g = gains[:, q, bass.ds(m, 1)]
                tile = resid[:, bass.ds(m, 1), :].rearrange("p a s -> p (a s)")
                fn(x_hi[:, bass.ds(m, 1), :].rearrange("p a s -> p (a s)"), tile, ACT.Copy, scale=g)\
                    .then_inc(x_hi_done.sem, 1)

            def square(l, r, m, slot):
                wait_alone(act, sq_added.sem, sq_added.at(l, r + m - 1))
                fn(sq[:, slot, :], resid[:, bass.ds(m, 1), :].rearrange("p a s -> p (a s)"), ACT.Square)\
                    .then_inc(sq_ready.sem, 1)

            def root(l, q):
                nc.scalar.preload_act_table(ACT.Sqrt)
                act.wait_ge(mean_ready.sem, mean_ready.at(l, q + 1))
                fn(mean_sq[:], mean_sq[:], ACT.Sqrt).then_inc(root_ready.sem, 1)

            for m in range(DT):
                if m % (DT // 2) == 0:
                    act.wait_ge(x_loaded[m // (DT // 2)].sem, 16)
                norm_input(0, -DT, m, 0)
                square(0, -DT, m, m % 2)
            act.wait_ge(consts_loaded.sem, 16 * CONST_LOADS)

            with act.Fori(0, LAYERS) as l:
                def up(f, n_up, m, width, first=False):
                    n, half = n_up + 2 * m, n_up // 2 + m
                    next_hi(l, n, half, 0, width)
                    if first:
                        root(l, 2 * f)
                    act.wait_ge(g_scaled_done.sem, g_scaled_done.at(l, f * FT + m + 1))
                    fn(g_silu[:], g_scaled[:], ACT.Silu).then_inc(silu_done.sem, 1)
                    next_hi(l, n, half, 1, width)
                    act.wait_ge(hidden_ready.sem, hidden_ready.at(l, f * FT + m + 1))
                    fn(hid_hi[:, bass.ds(m, 1), :].rearrange("p a s -> p (a s)"), hidden[:], ACT.Copy)\
                        .then_inc(hidden_hi.sem, 1)

                def project(n0, r, q, j, chunks, width):
                    for i in range(2):
                        m = 2 * j + i
                        for c in range(chunks):
                            s = (i * chunks + c) % 2
                            half = n0 // 2 + (chunks * j + (i * chunks + c) // 2)
                            if width[i]:
                                next_hi(l, n0 + 2 * chunks * j + (i * chunks + c) - s, half, s, width[i])
                        act.wait_ge(resid_ready.sem, resid_ready.at(l, r + m + 1))
                        norm_input(l, r, m, q)
                        square(l, r, m, i)

                def ffn(f, n_up, n_down, r, q, next_width):
                    up(f, n_up, 0, UP_W, True)
                    nc.scalar.preload_act_table(ACT.Silu)
                    with act.Fori(1, FT - 1) as m:
                        up(f, n_up, m, UP_W)
                    up(f, n_up, FT - 1, DOWN_W)
                    with act.Fori(0, DT // 2 - 1) as j:
                        project(n_down, r, q, j, 2, (DOWN_W, DOWN_W))
                    project(n_down, r, q, DT // 2 - 1, 2, (DOWN_W, next_width))

                for s in range(2):
                    split_hi(l, s, 0, s, UP_W)
                ffn(0, N_UP1, N_DN1, 0, 3 * l + 1, UP_W)

                next_hi(l, N_WIN, N_WIN // 2, 0, UP_W)
                root(l, 1)
                next_hi(l, N_WIN, N_WIN // 2, 1, UP_W)

                def next_tile(m):
                    next_hi(l, N_WIN + m - m % 2, (N_WIN + m) // 2, m % 2, UP_W)

                next_tile(2)
                act.wait_ge(sp_arg.sem, sp_arg.at(l, 1))
                fn(spt[:, 1, :], spt[:, 0, :], ACT.Exp, scale=-1.0).then_inc(sp_exp.sem, 1)
                next_tile(3)
                act.wait_ge(sp_arg.sem, sp_arg.at(l, 2))
                fn(spt[:, 3, :], spt[:, 2, :], ACT.Ln).then_inc(sp_ln.sem, 1)
                next_tile(4)
                next_tile(5)
                next_tile(6)
                next_tile(7)
                next_tile(8)
                next_tile(9)
                for c in range(2):
                    act.wait_ge(lru_g_ready.sem, lru_g_ready.at(l, c + 1))
                    fn(lru[1][:, c, :], bank[4 * c][:], ACT.Sigmoid, bias=lru_par[:, l, c, 5:6])
                    fn(lru[2][:, c, :], bank[4 * c + 1][:], ACT.Sigmoid, bias=lru_par[:, l, c, 6:7])\
                        .then_inc(lru_gates_done.sem, 1)
                act.wait_ge(sp_done.sem, sp_done.at(l, 1))
                act.wait_ge(lru_gates_done.sem, lru_gates_done.at(l, 2))
                for c in range(2):
                    ins = fn(lru[4][:, c, :], lru[1][:, c, :], ACT.Exp, scale=sp8[:, c:c + 1])
                ins.then_inc(lru_decay.sem, 1)
                for c in range(2):
                    ins = fn(lru[1][:, c, :], lru[1][:, c, :], ACT.Tanh, scale=sp4[:, c:c + 1])
                ins.then_inc(lru_tanh.sem, 1)
                next_tile(10)
                act.wait_ge(u_done.sem, u_done.at(l, U_GR + 2))
                fn(U[:, U_GR:U_GR + 2, :], U[:, U_GR:U_GR + 2, :], ACT.Gelu_apprx_tanh).then_inc(lru_gelu.sem, 1)
                act.wait_ge(lru_tanh.sem, lru_tanh.at(l, 1))
                fn(lru[1][:], lru[1][:], ACT.Sqrt).then_inc(lru_sqrt.sem, 1)
                next_tile(11)
                next_tile(12)
                act.wait_ge(lru_out.sem, lru_out.at(l, 1))
                fn(lru[1][:], lru[0][:], ACT.Square).then_inc(lru_sq_done.sem, 1)
                next_tile(13)
                act.wait_ge(lru_ms_done.sem, lru_ms_done.at(l, 1))
                fn(lru[3][:], lru[3][:], ACT.Sqrt).then_inc(lru_root.sem, 1)
                next_hi(l, N_TM - 2, N_TM // 2 - 1, 0, TM_W)
                next_hi(l, N_TM - 2, N_TM // 2 - 1, 1, TM_W)
                act.wait_ge(rcol_ready.sem, rcol_ready.at(l, 1))
                fn(rcol[:], bank[6][:, 0:ST], ACT.Copy).then_inc(rcol_done.sem, 1)
                for j in range(DT // 2):
                    for s in range(2):
                        next_hi(l, N_TM + 2 * j, N_TM // 2 + j, s, TM_W if j < DT // 2 - 1 else UP_W)
                act.wait_ge(chunk_done.sem, chunk_done.at(l, N_OUT))
                act.wait_ge(rcol_done.sem, rcol_done.at(l, 1))
                for t in range(ST):
                    fn(ifcol[:, t, :], bank[2 * t][:, 280:288], ACT.Copy, scale=rcol[:, t:t + 1])
                    fn(v_all[:, :, t, :], bank[2 * t][:, 0:256].rearrange("p (k d) -> p k d", k=4), ACT.Copy,
                       scale=rcol[:, t:t + 1])
                for t in range(ST):
                    ins = fn(gates[:, t, :], bank[2 * t][:, 256:280], ACT.Sigmoid, scale=rcol[:, t:t + 1])
                ins.then_inc(tm_taken.sem, 1)
                act.wait_ge(tm_values_taken.sem, tm_values_taken.at(l, 1))
                fn(o_sig[:], o_sig[:], ACT.Sigmoid).then_inc(o_sig_done.sem, 1)
                act.wait_ge(ml_abs.sem, ml_abs.at(l, 1))
                fn(rows[2][:], rows[2][:], ACT.Exp, scale=-1.0).then_inc(ml_exp.sem, 1)
                act.wait_ge(ml_arg.sem, ml_arg.at(l, 1))
                fn(rows[4][:], rows[3][:], ACT.Ln).then_inc(ml_ln.sem, 1)
                act.wait_ge(cmp_h_ready.sem, cmp_h_ready.at(l, 1))
                for kv in range(2):
                    ins = fn(cmp_act[:, kv, :], bank[2 + kv][0:2 * NCMP, 0:256], ACT.Silu)
                ins.then_inc(cmp_act_done.sem, 1)
                act.wait_ge(cmp_t_ready.sem, cmp_t_ready.at(l, 1))
                fn(cmp_hid[:].rearrange("p a b n -> p (a b) n"),
                   bank[4][:, 0:256].rearrange("p (a n) -> p a n", n=64)[:, :, 0:2 * NCMP], ACT.Copy)\
                    .then_inc(cmp_hid_done.sem, 1)
                for kv in range(4):
                    src = slice(HD * (kv % 2), HD * (kv % 2) + HD)
                    for half in range(2):
                        ins = fn(k_hi[HD * half:HD * half + HD, kv, :], U[src, U_KS + kv // 2, :], ACT.Copy,
                                 scale=HD ** -0.5)
                    ins.then_inc(k_hi_done.sem, 1)
                fn(q_hi[:], U[:, U_Q:U_Q + HEADS // 2, :], ACT.Copy).then_inc(q_hi_done.sem, 1)
                act.wait_ge(cmp_t_done.sem, cmp_t_done.at(l, 1))
                fn(PR[:], T[:], ACT.Exp).then_inc(cmp_p_done.sem, 1)
                act.wait_ge(cmp_tr_ready.sem, cmp_tr_ready.at(l, 1))
                for n in range(2):
                    ins = fn(PT[:, n, :], bank[4 + n][:], ACT.Copy)
                ins.then_inc(cmp_pt_done.sem, 1)
                act.wait_ge(ml_cols_done.sem, ml_cols_done.at(l, 1))
                fn(em[:], bcol[:, :, 4:8], ACT.Exp, scale=-1.0).then_inc(ml_em.sem, 1)
                for n in range(16):
                    act.wait_ge(ml_d_done.sem, ml_d_done.at(l, n + 1))
                    e = ml_e[:, n % 2, 0:S - (n % ST) * P]
                    fn(e, e, ACT.Exp).then_inc(ml_e_done.sem, 1)


                def exps(kv, u):
                    act.wait_ge(att_scored.sem, l * 64 + kv * 16 + u + 5)
                    act.wait_ge(att_tr_ready.sem, l * 64 + kv * 16 + u + 1)
                    w = (u % ST + 1) * P
                    fn(PR[:, u % 2, 0:w], T[:, u % 2, 0:w], ACT.Exp, bias=n_max[:, u:u + 1],
                       accum_out=sums[:, kv, u:u + 1]).then_inc(att_exp_done.sem, 1)

                def attention(kv, last):
                    for u in range(16):
                        if u + 1 < 16:
                            exps(kv, u + 1)
                        elif not last:
                            exps(kv + 1, 0)
                        act.wait_ge(att_tr_ready.sem, l * 64 + kv * 16 + u + 3)
                        act.wait_ge(att_pv_ready.sem, l * 64 + kv * 16 + u + 1)
                        w = (u % ST + 1) * P
                        fn(PT[:, u % 2, 0:w], bank[4 + u % 2][:, 0:w], ACT.Copy).then_inc(att_copied.sem, 1)

                exps(0, 0)
                with act.Fori(0, 3) as kv:
                    attention(kv, False)
                attention(3, True)

                act.wait_ge(acc_taken.sem, acc_taken.at(l, 8))
                for t in range(ST):
                    fn(o_sq[:, 12 * t:12 * t + 12, :], o_all[:, t, :, :], ACT.Square).then_inc(o_sq_done.sem, 1)
                nc.scalar.preload_act_table(ACT.Sqrt)
                act.wait_ge(o_ms_done.sem, o_ms_done.at(l, 1))
                fn(h_ms[:], h_ms[:], ACT.Sqrt).then_inc(o_root.sem, 1)
                act.wait_ge(lru_normed.sem, lru_normed.at(l, 2))
                for c in range(2):
                    fn(h_hi[:, 4 + c, :], U[:, U_GR + c, :], ACT.Copy).then_inc(lru_hi_done.sem, 1)
                for n in range(6):
                    k = n if n < 4 else n + 2
                    act.wait_ge(h_t_ready.sem, h_t_ready.at(l, n + 1))
                    if k == U_GR:
                        act.wait_ge(lru_lo_done.sem, lru_lo_done.at(l, 2))
                    fn(h_hi[:, k, :], bank[n % 4][:], ACT.Copy, scale=head_gain[:, l, k:k + 1])\
                        .then_inc(h_hi_done.sem, 1)

                with act.Fori(0, DT // 2) as j:
                    project(N_OUT, DT, 3 * l + 2, j, 1, (UP_W, UP_W))
                ffn(1, N_UP2, N_DN2, 2 * DT, 3 * l + 3, 0)
            root(LAYERS, 0)

        @block.vector
        def _(dve):
            tt, ts, stt = nc.vector.tensor_tensor, nc.vector.tensor_scalar, nc.vector.scalar_tensor_tensor
            steps = Steps(dve, dve_step.sem)
            dve.sem_inc(w_lo_done.sem, 2)
            dve.sem_inc(sq_added.sem, 2)
            dve.sem_inc(resid_ready.sem, 2)
            dve.sem_inc(att_scored.sem, 4)
            dve.sem_inc(ml_w_done.sem, 2)
            dve.sem_inc(g_scaled_done.sem, 1)
            dve.sem_inc(u_scaled_done.sem, 1)
            dve.sem_inc(acc_taken.sem, 2)
            dve.wait_ge(gains_loaded.sem, 16)

            def flat(t, m):
                return t[:, bass.ds(m, 1), :].rearrange("p a s -> p (a s)")

            def split_lo(l, n, slot, width):
                dve.wait_ge(w_hi_done.sem, w_hi_done.at(l, n + 1))
                tt(w_lo[slot][:, 0:width], raw[slot][:, 0:width], w_hi[slot][:, 0:width].bitcast(F32), ALU.subtract)\
                    .then_inc(w_lo_done.sem, 1)

            def norm_low(l, r, m, q):
                dve.wait_ge(x_hi_done.sem, x_hi_done.at(l, r + m + 1))
                stt(flat(x_lo, m), flat(resid, m), gains[:, q, bass.ds(m, 1)], flat(x_hi, m).bitcast(F32),
                    ALU.mult, ALU.subtract).then_inc(x_lo_done.sem, 1)

            def norm_add(l, r, m, slot):
                dve.wait_ge(sq_ready.sem, sq_ready.at(l, r + m + 1))
                dve.wait_ge(sq_added.sem, sq_added.at(l, r + m))
                tt(sumsq[:], sumsq[:], sq[:, slot, :], ALU.add).then_inc(sq_added.sem, 1)

            def norm_finish(l, q):
                dve.wait_ge(norm_sum.sem, norm_sum.at(l, q + 1))
                ts(mean_sq[:], bank[6][:], 1.0 / (DT * P), EPS, ALU.mult, ALU.add).then_inc(mean_ready.sem, 1)
                dve.wait_ge(root_ready.sem, root_ready.at(l, q + 1))
                nc.vector.reciprocal(rstd[:], mean_sq[:]).then_inc(rstd_ready.sem, 1)
                dve.wait_ge(rstd_ready.sem, rstd_ready.at(l, q + 1))

            steps.done(nc.vector.memset(sumsq[:], 0.0)).then_inc(waits_met.sem, 1)
            for m in range(DT):
                if m % (DT // 2) == 0:
                    dve.wait_ge(x_loaded[m // (DT // 2)].sem, 16)
                norm_low(0, -DT, m, 0)
                norm_add(0, -DT, m, m % 2)
            dve.wait_ge(consts_loaded.sem, 16 * CONST_LOADS)
            dve.wait_ge(pool_consts.sem, POOL_CONSTS)
            nc.vector.memset(halves[0:HD, 0:HD], 1.0)
            nc.vector.memset(halves[HD:P, HD:P], 1.0).then_inc(dve_consts.sem, 1)
            for h in range(HEADS):
                ts(cmp_bias[:, h % 2, :, h // 2, :], cmp_bias[:, h % 2, :, h // 2, :], neg_slope[:, h:h + 1], None, ALU.mult)
            before = steps.n

            with dve.Fori(0, LAYERS) as l:
                steps.base, steps.n = l * DVE_STEPS + before, 0

                def up(f, n_up, m, width, first=False):
                    n = n_up + 2 * m
                    if first:
                        split_lo(l, n + 2, 0, width)
                        norm_finish(l, 2 * f)
                    dve.wait_ge(chunk_done.sem, chunk_done.at(l, n + 1))
                    tt(g_scaled[:], bank[0][:], rstd[:], ALU.mult).then_inc(g_scaled_done.sem, 1)
                    if not first:
                        split_lo(l, n + 2, 0, width)
                    dve.wait_ge(chunk_done.sem, chunk_done.at(l, n + 2))
                    tt(u_scaled[:], bank[1][:], rstd[:], ALU.mult).then_inc(u_scaled_done.sem, 1)
                    split_lo(l, n + 3, 1, width)
                    dve.wait_ge(silu_done.sem, silu_done.at(l, f * FT + m + 1))
                    dve.wait_ge(u_scaled_done.sem, u_scaled_done.at(l, f * FT + m + 1))
                    tt(hidden[:], g_silu[:], u_scaled[:], ALU.mult).then_inc(hidden_ready.sem, 1)
                    dve.wait_ge(hidden_hi.sem, hidden_hi.at(l, f * FT + m + 1))
                    tt(flat(hid_lo, m), hidden[:], flat(hid_hi, m).bitcast(F32), ALU.subtract)\
                        .then_inc(hidden_lo.sem, 1)

                def project(n0, r, q, j, chunks, factor, width):
                    for i in range(2):
                        m = 2 * j + i
                        first_n = n0 + 2 * chunks * j + i * chunks
                        if chunks == 2 and width[i]:
                            split_lo(l, first_n + 2, 0, width[i])
                        dve.wait_ge(chunk_done.sem, chunk_done.at(l, first_n + chunks))
                        stt(flat(resid, m), bank[4 + i][:], factor, flat(resid, m), ALU.mult, ALU.add)\
                            .then_inc(resid_ready.sem, 1)
                        if chunks == 1:
                            split_lo(l, first_n + 2, i, width[i])
                        elif width[i]:
                            split_lo(l, first_n + 3, 1, width[i])
                        norm_low(l, r, m, q)
                        norm_add(l, r, m, i)

                def ffn(f, n_up, n_down, r, q, next_width):
                    up(f, n_up, 0, UP_W, True)
                    with dve.Fori(1, FT - 1) as m:
                        up(f, n_up, m, UP_W)
                    up(f, n_up, FT - 1, DOWN_W)
                    steps.done(nc.vector.memset(sumsq[:], 0.0)).then_inc(waits_met.sem, 1)
                    with dve.Fori(0, DT // 2 - 1) as j:
                        project(n_down, r, q, j, 2, 0.5, (DOWN_W, DOWN_W))
                    project(n_down, r, q, DT // 2 - 1, 2, 0.5, (DOWN_W, next_width))

                for s in range(2):
                    split_lo(l, s, s, UP_W)
                ffn(0, N_UP1, N_DN1, 0, 3 * l + 1, UP_W)

                def take_u(m, i, n):
                    dve.wait_ge(chunk_done.sem, chunk_done.at(l, n + 1))
                    tt(flat(U, m), bank[2 + i][:], rstd[:], ALU.mult).then_inc(u_done.sem, 1)

                split_lo(l, N_WIN + 2, 0, UP_W)
                norm_finish(l, 1)
                def log1p(e, u, ln, a, b, arg_sem, arg_count, ln_sem, ln_count):
                    dve.wait_ge(arg_sem, arg_count)
                    steps.done(ts(a, u, -1.0, None, ALU.add))
                    steps.done(tt(a, e, a, ALU.subtract))
                    steps.done(nc.vector.reciprocal(b, u))
                    steps.done(tt(a, a, b, ALU.mult))
                    dve.wait_ge(ln_sem, ln_count)
                    steps.done(tt(ln, ln, a, ALU.add))


                def tile(m):
                    take_u(m, m % 2, N_WIN + m)
                    split_lo(l, N_WIN + m + 2, m % 2, UP_W)

                take_u(0, 0, N_WIN)
                take_u(1, 1, N_WIN + 1)
                split_lo(l, N_WIN + 3, 1, UP_W)
                for par in range(2):
                    h = slice(HD * par, HD * par + HD)
                    nc.vector.tensor_copy(gate_bd[h, :, h], gate_w[h, l, :, :])
                nc.vector.tensor_copy(w2cur[:], cmp_w2[:, l, :, :, :]).then_inc(layer_w_ready.sem, 1)
                stt(spt[:, 0, :], lru_par[:, l, :, 7], -1.0, lru_par[:, l, :, 7], ALU.mult, ALU.max).then_inc(sp_arg.sem, 1)
                tile(2)
                dve.wait_ge(sp_exp.sem, sp_exp.at(l, 1))
                ts(spt[:, 2, :], spt[:, 1, :], 1.0, None, ALU.add).then_inc(sp_arg.sem, 1)
                tile(3)
                tile(4)

                def conv(c):
                    dve.wait_ge(u_done.sem, u_done.at(l, U_XR + c + 1))
                    par = lru_par[:, l, c, :]
                    steps.done(ts(lru[0][:, c, :], U[:, U_XR + c, :], par[:, 3:4], par[:, 4:5], ALU.mult, ALU.add))
                    for tap in (2, 1, 0):
                        lag = 3 - tap
                        ins = stt(lru[0][:, c, lag:S], U[:, U_XR + c, 0:S - lag], par[:, tap:tap + 1],
                                  lru[0][:, c, lag:S], ALU.mult, ALU.add)
                        if tap:
                            steps.done(ins)
                    ins.then_inc(conv_done.sem, 1)
                    dve.wait_ge(conv_done.sem, conv_done.at(l, c + 1))

                conv(0)
                tile(5)
                conv(1)
                tile(6)
                log1p(spt[:, 1, :], spt[:, 2, :], spt[:, 3, :], spt[:, 4, :], spt[:, 5, :],
                      sp_arg.sem, sp_arg.at(l, 2), sp_ln.sem, sp_ln.at(l, 1))
                steps.done(ts(spt[:, 4, :], lru_par[:, l, :, 7], -1.0, 0.0, ALU.mult, ALU.max))
                steps.done(tt(spt[:, 4, :], spt[:, 4, :], spt[:, 3, :], ALU.add))
                ts(sp8[:], spt[:, 4, :], -8.0, None, ALU.mult)
                ts(sp4[:], spt[:, 4, :], 4.0, None, ALU.mult).then_inc(sp_done.sem, 1)
                tile(7)
                tile(8)
                tile(9)
                dve.wait_ge(lru_gates_done.sem, lru_gates_done.at(l, 2))
                steps.done(tt(lru[2][:], lru[2][:], lru[0][:], ALU.mult))
                tile(10)
                tile(11)
                dve.wait_ge(lru_decay.sem, lru_decay.at(l, 1))
                dve.wait_ge(lru_sqrt.sem, lru_sqrt.at(l, 1))
                for c in range(2):
                    ins = stt(lru[3][:, c, :], lru[4][:, c, :], 1.0, lru[1][:, c, :], ALU.add, ALU.mult)
                steps.done(ins)
                steps.done(tt(lru[1][:], lru[3][:], lru[2][:], ALU.mult))
                tile(12)
                for c in range(2):
                    ins = nc.vector.tensor_tensor_scan(lru[3][:, c, :], lru[4][:, c, :], lru[1][:, c, :], 0.0,
                                                       ALU.mult, ALU.add)
                steps.done(ins)
                dve.wait_ge(lru_gelu.sem, lru_gelu.at(l, 1))
                tt(lru[0][:], lru[3][:], U[:, U_GR:U_GR + 2, :], ALU.mult).then_inc(lru_out.sem, 1)
                tile(13)
                dve.wait_ge(lru_ms_ready.sem, lru_ms_ready.at(l, 1))
                for c in range(2):
                    ins = ts(lru[3][:, c, :], bank[c][:], 1.0 / HD, EPS, ALU.mult, ALU.add)
                ins.then_inc(lru_ms_done.sem, 1)

                def lru_norm(c):
                    dve.wait_ge(lru_root.sem, lru_root.at(l, 1))
                    steps.done(nc.vector.reciprocal(lru[3][:, c, :], lru[3][:, c, :]))
                    stt(U[:, U_GR + c, :], lru[0][:, c, :], head_gain[:, l, 4 + c:5 + c], lru[3][:, c, :],
                        ALU.mult, ALU.mult).then_inc(lru_normed.sem, 1)

                take_u(WIN_TILES - 2, 0, N_TM - 2)
                split_lo(l, N_TM, 0, TM_W)
                lru_norm(0)
                take_u(WIN_TILES - 1, 1, N_TM - 1)
                split_lo(l, N_TM + 1, 1, TM_W)
                lru_norm(1)
                nc.vector.memset(v_aug[:, :, :, HD:HD + 1], 1.0)
                for k in range(DT):
                    split_lo(l, N_TM + k + 2, k % 2, TM_W if k < DT - 2 else UP_W)
                    if k < 4:
                        kv, par = k // 2, k % 2
                        if k == 0:
                            dve.wait_ge(u_done.sem, u_done.at(l, WIN_TILES))
                        for g in range(2):
                            src = slice(HD * g, HD * g + HD)
                            for pairs, view in block_halves(U[src, U_KC + kv, :], par):
                                ins = tt(zc[kv][HD * par:HD * par + HD, pairs, g * NCMP:(g + 1) * NCMP], view,
                                         wide(cmp_pos[src, l, kv, par, pairs], NCMP), ALU.add)
                        if par:
                            ins.then_inc(zc_ready[kv].sem, 1)
                dve.wait_ge(rcol_done.sem, rcol_done.at(l, 1))
                dve.wait_ge(chunk_done.sem, chunk_done.at(l, N_OUT))
                for t in range(ST):
                    ts(o_sig[:, t, :], bank[2 * t + 1][:, 256:512], rcol[:, t:t + 1], None, ALU.mult)
                    ins = ts(v_aug[:, t, :, 0:HD], bank[2 * t + 1][:, 0:256].rearrange("p (h d) -> p h d", h=4),
                             rcol[:, t:t + 1], None, ALU.mult)
                ins.then_inc(tm_values_taken.sem, 1)
                dve.wait_ge(if_t_ready.sem, if_t_ready.at(l, 1))
                ts(rows[0][:], bank[6][0:4, :], ml_bias[:, l, 0:1], None, ALU.add)
                steps.done(ts(rows[1][:], bank[7][0:4, :], ml_bias[:, l, 1:2], None, ALU.add))
                stt(rows[2][:], rows[1][:], -1.0, rows[1][:], ALU.mult, ALU.max).then_inc(ml_abs.sem, 1)
                dve.wait_ge(ml_exp.sem, ml_exp.at(l, 1))
                ts(rows[3][:], rows[2][:], 1.0, None, ALU.add).then_inc(ml_arg.sem, 1)
                log1p(rows[2][:], rows[3][:], rows[4][:], rows[5][:], rows[2][:],
                      ml_arg.sem, ml_arg.at(l, 1), ml_ln.sem, ml_ln.at(l, 1))
                steps.done(ts(rows[1][:], rows[1][:], 0.0, None, ALU.min))
                steps.done(tt(rows[1][:], rows[1][:], rows[4][:], ALU.subtract))
                steps.done(nc.vector.memset(rows[5][:], 1.0))
                steps.done(nc.vector.tensor_tensor_scan(rows[2][:], rows[5][:], rows[1][:], 0.0, ALU.mult, ALU.add))
                steps.done(tt(rows[3][:], rows[0][:], rows[2][:], ALU.subtract))
                steps.done(nc.vector.tensor_tensor_scan(rows[4][:], rows[3][:], rows[3][:], 0.0, ALU.max, ALU.max))
                steps.done(tt(rows[5][:], rows[2][:], rows[4][:], ALU.add))
                ts(rows[4][:], rows[4][:], -1.0, None, ALU.mult).then_inc(ml_rows.sem, 1)

                dve.wait_ge(ml_cols_ready.sem, ml_cols_ready.at(l, 1))
                nc.vector.tensor_copy(bcol[:], bank[6][:, 0:32].rearrange("p (t c) -> p t c", t=ST))\
                    .then_inc(ml_cols_done.sem, 1)
                dve.wait_ge(ml_cols_done.sem, ml_cols_done.at(l, 1))


                dve.wait_ge(cmp_kv_ready.sem, cmp_kv_ready.at(l, 1))
                nc.vector.tensor_copy(kcT[:, :, 0:NCMP], bank[3][:, 0:64].rearrange("p (g n) -> p g n", g=2)[:, :, 0:NCMP])
                for j in range(4):
                    h = slice(32 * j, 32 * j + NCMP)
                    ins = nc.vector.tensor_copy(vc_bd[h, HD * j:HD * (j + 1)], bank[5][h, HD * j:HD * (j + 1)])
                ins.then_inc(cmp_kv_done.sem, 1)
                for kv in range(4):
                    dve.wait_ge(k_hi_done.sem, k_hi_done.at(l, kv + 1))
                    src = slice(HD * (kv % 2), HD * (kv % 2) + HD)
                    for half in range(2):
                        ins = stt(k_lo[HD * half:HD * half + HD, kv, :], U[src, U_KS + kv // 2, :], HD ** -0.5,
                                  k_hi[src, kv, :].bitcast(F32), ALU.mult, ALU.subtract)
                    ins.then_inc(k_lo_done.sem, 1)
                for half in range(2):
                    dve.wait_ge(cmp_s_ready.sem, cmp_s_ready.at(l, half + 1))
                    ins = stt(T[:, half, :], bank[2 + half][:], HD ** -0.5,
                              cmp_bias[:, half, :, :, :].rearrange("p t h n -> p (t h n)"),
                              ALU.mult, ALU.add)
                steps.done(ins)
                t4 = T[:].rearrange("p a (b n) -> p (a b) n", n=32)
                steps.done(nc.vector.tensor_reduce(cmp_max[:], t4, AX_X, ALU.max))
                tt(t4, t4, wide(cmp_max[:], 32), ALU.subtract).then_inc(cmp_t_done.sem, 1)
                dve.wait_ge(cmp_p_done.sem, cmp_p_done.at(l, 1))
                p4 = PR[:].rearrange("p a (b n) -> p (a b) n", n=32)
                steps.done(nc.vector.tensor_reduce(cmp_sum[:], p4, AX_X, ALU.add))
                for par in range(2):
                    pt4 = PR[:, par, :].rearrange("p (t h n) -> p t h n", t=ST, n=32)
                    ins = tt(pt4, pt4, cmp_mask[:].unsqueeze(2).to_broadcast([P, ST, 4, 32]), ALU.mult)
                ins.then_inc(cmp_pm_done.sem, 1)
                dve.wait_ge(q_hi_done.sem, q_hi_done.at(l, 1))
                tt(q_lo[:], U[:, U_Q:U_Q + HEADS // 2, :], q_hi[:].bitcast(F32), ALU.subtract).then_inc(q_lo_done.sem, 1)

                steps.done(nc.vector.reciprocal(cmp_sum[:], cmp_sum[:]))
                c3 = cmp_sum[:].rearrange("p (a t h) -> p a t h", a=2, t=ST)
                g4 = gates[:].rearrange("p t (h a c) -> p a t h c", a=2, c=3)
                dve.wait_ge(tm_taken.sem, tm_taken.at(l, 1))
                steps.done(tt(c3, c3, g4[:, :, :, :, 0], ALU.mult))
                dve.wait_ge(cmp_o_ready.sem, cmp_o_ready.at(l, 1))
                for t in range(ST):
                    ins = tt(o_all[:, t, 0:HEADS, :].rearrange("p (h a) d -> p a h d", a=2),
                             bank[2 + t][:].rearrange("p (a h d) -> p a h d", a=2, h=4), wide(c3[:, :, t, :], HD),
                             ALU.mult)
                ins.then_inc(cmp_o_done.sem, 1)

                def exponent(n):
                    h, j = n // ST, n % ST
                    if j == 0:
                        dve.wait_ge(ml_m_ready.sem, ml_m_ready.at(l, h + 1))
                    ts(ml_e[:, n % 2, 0:S - j * P], bank[6 + h % 2][:, j * P:S], bcol[:, j, h:h + 1], 0.0, ALU.add, ALU.min)\
                        .then_inc(ml_d_done.sem, 1)

                exponent(0)
                for n in range(16):
                    if n + 1 < 16:
                        exponent(n + 1)
                    w = S - (n % ST) * P
                    dve.wait_ge(ml_e_done.sem, ml_e_done.at(l, n + 1))
                    dve.wait_ge(ml_s_ready.sem, ml_s_ready.at(l, n + 1))
                    dve.wait_ge(ml_pv.sem, ml_pv.at(l, n - 1))
                    steps.done(stt(ml_w[:, n % 2, 0:w], ml_e[:, n % 2, 0:w], HD ** -0.5, bank[n % 2][:, 0:w],
                                   ALU.mult, ALU.mult))
                    tt(ml_w[:, n % 2, 0:P], ml_w[:, n % 2, 0:P], causal[:], ALU.mult).then_inc(ml_w_done.sem, 1)
                dve.wait_ge(ml_pv.sem, ml_pv.at(l, 16))
                dve.wait_ge(ml_em.sem, ml_em.at(l, 1))
                acc = [bank[2 + t][:, 0:4 * (HD + 1)].rearrange("p (h d) -> p h d", h=4) for t in range(ST)]
                for t in range(ST):
                    ins = nc.vector.tensor_copy(den[:, t, :], acc[t][:, :, HD])
                steps.done(ins)
                steps.done(stt(den[:], den[:], -1.0, den[:], ALU.mult, ALU.max))
                steps.done(tt(den[:], den[:], em[:], ALU.max))
                steps.done(nc.vector.reciprocal(den[:], den[:]))
                for t in range(ST):
                    ins = tt(o_all[:, t, HEADS:12, :], acc[t][:, :, 0:HD], wide(den[:, t, :], HD), ALU.mult)
                ins.then_inc(ml_o_done.sem, 1)
                dve.wait_ge(ml_o_done.sem, ml_o_done.at(l, 1))
                dve.wait_ge(o_sig_done.sem, o_sig_done.at(l, 1))
                steps.done(tt(o_all[:, :, HEADS:12, :], o_all[:, :, HEADS:12, :],
                              o_sig[:].rearrange("p t (h d) -> p t h d", h=4), ALU.mult)).then_inc(waits_met.sem, 1)

                def take_outputs(kv, half):
                    b, g = kv // 2, kv % 2
                    u0, h0 = 8 * half, g * HPG + 2 * half
                    dve.wait_ge(att_exp_done.sem, att_exp_done.at(l, 16 * kv + u0 + 8))
                    steps.done(nc.vector.reciprocal(rec[:, u0:u0 + 8], sums[:, kv, u0:u0 + 8]))
                    gate = gates[:].rearrange("p t (h c) -> p c h t", c=3)[:, b + 1, h0:h0 + 2, :]
                    steps.done(tt(coef[:, u0:u0 + 8].rearrange("p (h t) -> p h t", h=2),
                                  rec[:, u0:u0 + 8].rearrange("p (h t) -> p h t", h=2), gate, ALU.mult))
                    dve.wait_ge(att_pv_ready.sem, att_pv_ready.at(l, 16 * kv + u0 + 8))
                    steps.done(tt(att_o[:, half, :].rearrange("p (u d) -> p u d", u=8),
                                  bank[6 + half][:].rearrange("p (u d) -> p u d", u=8),
                                  wide(coef[:, u0:u0 + 8], HD), ALU.mult))
                    o = o_all[:].rearrange("p t h d -> p h t d")[:, h0:h0 + 2, :, :]
                    tt(o, o, att_o[:, half, :].rearrange("p (h t d) -> p h t d", h=2, t=ST), ALU.add)\
                        .then_inc(acc_taken.sem, 1)

                for kv in range(4):
                    g = kv % 2
                    for u in range(16):
                        h, i = u // ST, u % ST
                        w = (i + 1) * P
                        dve.wait_ge(att_s_ready.sem, att_s_ready.at(l, 16 * kv + u + 1))
                        dve.wait_ge(att_exp_done.sem, att_exp_done.at(l, 16 * kv + u - 1))
                        steps.done(stt(T[:, u % 2, 0:w], dist[:, S - w:S], neg_slope[:, g * HPG + h:g * HPG + h + 1],
                                       bank[u % 4][:, 0:w], ALU.mult, ALU.add))
                        nc.vector.tensor_reduce(n_max[:, u:u + 1], T[:, u % 2, 0:w], AX_X, ALU.max, negate=True)\
                            .then_inc(att_scored.sem, 1)
                        if u == 2 and kv:
                            take_outputs(kv - 1, 1)
                        if u == 11:
                            take_outputs(kv, 0)
                take_outputs(3, 1)
                dve.wait_ge(acc_taken.sem, acc_taken.at(l, 8))

                for t in range(ST):
                    dve.wait_ge(o_sq_done.sem, o_sq_done.at(l, t + 1))
                    heads = slice(12 * t, 12 * t + 12)
                    ins = nc.vector.tensor_reduce(h_ss[:, heads], o_sq[:, heads, :], AX_X, ALU.add)
                steps.done(ins)
                ts(h_ms[:], h_ss[:], 1.0 / HD, EPS, ALU.mult, ALU.add).then_inc(o_ms_done.sem, 1)
                dve.wait_ge(o_root.sem, o_root.at(l, 1))
                steps.done(nc.vector.reciprocal(h_rs[:], h_ms[:]))
                for t in range(ST):
                    tt(o_all[:, t, :, :], o_all[:, t, :, :], wide(h_rs[:, 12 * t:12 * t + 12], HD), ALU.mult)\
                        .then_inc(o_normed.sem, 1)
                for c in range(2):
                    dve.wait_ge(lru_hi_done.sem, lru_hi_done.at(l, c + 1))
                    tt(h_lo[:, 4 + c, :], U[:, U_GR + c, :], h_hi[:, 4 + c, :].bitcast(F32), ALU.subtract)\
                        .then_inc(lru_lo_done.sem, 1)
                for n in range(6):
                    k = n if n < 4 else n + 2
                    dve.wait_ge(h_hi_done.sem, h_hi_done.at(l, n + 1))
                    stt(h_lo[:, k, :], bank[n % 4][:], head_gain[:, l, k:k + 1], h_hi[:, k, :].bitcast(F32),
                        ALU.mult, ALU.subtract).then_inc(h_lo_done.sem, 1)
                steps.done(nc.vector.memset(sumsq[:], 0.0)).then_inc(waits_met.sem, 1)
                with dve.Fori(0, DT // 2) as j:
                    project(N_OUT, DT, 3 * l + 2, j, 1, 1.0, (UP_W, UP_W))
                ffn(1, N_UP2, N_DN2, 2 * DT, 3 * l + 3, 0)
                assert steps.n == DVE_STEPS, steps.n
            norm_finish(LAYERS, 0)
            for m in range(DT):
                stt(resid[:, m, :], resid[:, m, :], gains[:, 3 * LAYERS, m:m + 1], rstd[:], ALU.mult, ALU.mult)\
                    .then_inc(out_ready.sem, 1)


MIX_BYTES, SMALL_BYTES = 98368, 5120
DVE_STEPS = 151
CONST_LOADS = 6


def wide(ap, n):
    return ap.unsqueeze(len(ap.shape)).to_broadcast([*ap.shape, n])


def block_halves(src, par):
    v = src.rearrange("p (n c two) -> p two c n", two=2, c=8)[:, par, :, :]
    return (slice(0, 8), v[:, :, 0:NCMP]), (slice(8, 16), v[:, :, 1:NCMP + 1])


def kernel(**inputs):
    import numpy as np
    import concourse.bacc as bacc
    from concourse.bass_utils import run_bass_kernel_spmd

    a = {k: np.asarray(v) for k, v in inputs.items()}
    L = LAYERS

    def tiles(w, kt, mt):
        return w.reshape(L, kt, P, mt, P).transpose(0, 3, 2, 1, 4).reshape(L, mt, P, kt * P)

    def down(w):
        w = w.reshape(L, 2, FH, P, DT, P).transpose(0, 4, 1, 3, 2, 5)
        return w.reshape(L, DT, 2, P, FH * P)

    def up(w1, w3):
        return np.stack([tiles(w1, DT, FT), tiles(w3, DT, FT)], axis=2)

    w = a["w_in"]
    fm = np.concatenate([w[:, :, 1304:1816], w[:, :, 0:768], w[:, :, 768:896], w[:, :, 1024:1152], w[:, :, 1816:2328]],
                        axis=2)
    tm = np.concatenate([w[:, :, 896:1024], w[:, :, 1152:1280], w[:, :, 1280:1304], w[:, :, 2584:2592],
                         w[:, :, 2328:2584], w[:, :, 2592:2848]], axis=2)

    def cols(v, n):
        return v.reshape(*v.shape[:-1], n, P)

    gains = np.stack([a["ffn1_norm"], a["mix_norm"], a["ffn2_norm"]], axis=1).reshape(3 * L, 1024)
    gains = cols(np.concatenate([gains, a["final_norm"][None]], axis=0), DT).transpose(2, 0, 1)
    lru = [cols(a["lru_conv_w"], 2)[:, t] for t in range(4)]
    lru += [cols(a[k].reshape(L, 256), 2) for k in ("lru_conv_b", "lru_b_a", "lru_b_x", "lru_lambda")]
    gate = np.stack([a["lru_w_a"], a["lru_w_x"]], axis=1).reshape(L, 2, 2, 2, HD, HD)
    arrays = {
        "x": a["x"][0].T.reshape(DT, P, S).transpose(1, 0, 2),
        "up1": up(a["ffn1_w1"], a["ffn1_w3"]), "down1": down(a["ffn1_w2"]),
        "up2": up(a["ffn2_w1"], a["ffn2_w3"]), "down2": down(a["ffn2_w2"]),
        "w_in": tiles(fm, DT, WIN_TILES), "w_tm": tm.reshape(L, DT, P, TM_W),
        "w_out": tiles(a["w_out"], DT, DT),
        "cmp_w1": np.stack([a["nsa_cmp_w1_k"], a["nsa_cmp_w1_v"]], axis=1).reshape(L, 2, CP, P, 256)
                    .transpose(0, 1, 3, 2, 4),
        "gains": gains,
        "head_gain": cols(a["head_norm"].reshape(L, 1024), DT).transpose(2, 0, 1),
        "lru_par": np.stack(lru, axis=-1).transpose(2, 0, 1, 3),
        "gate_w": gate.transpose(3, 4, 0, 1, 2, 5).reshape(P, L, 4, HD),
        "cmp_pos": np.tile(np.stack([a["nsa_cmp_pos_k"], a["nsa_cmp_pos_v"]], axis=1).reshape(L, 2, CP, 2, HD)
                           .transpose(4, 0, 1, 3, 2), (2, 1, 1, 1, 1)),
        "cmp_w2": np.stack([a["nsa_cmp_w2_k"], a["nsa_cmp_w2_v"]], axis=1).reshape(L, 2, 2, P, HD)
                    .transpose(3, 0, 1, 2, 4),
        "ml_bias": np.stack([a["ml_b_i"], a["ml_b_f"]], axis=-1).transpose(1, 0, 2),
    }
    arrays = {k: np.ascontiguousarray(v) for k, v in arrays.items()}
    nc = bacc.Bacc("TRN2", target_bir_lowering=False, num_devices=1)
    d = {k: nc.dram_tensor(f"{k}_dram", v.shape, F32, kind="ExternalInput").ap() for k, v in arrays.items()}
    out = nc.dram_tensor("out_dram", (P, DT, S), F32, kind="ExternalOutput").ap()
    build(nc, d, out)
    got = run_bass_kernel_spmd(nc, [{f"{k}_dram": v for k, v in arrays.items()}], core_ids=[0]).results[0]["out_dram"]
    return np.ascontiguousarray(got.transpose(2, 1, 0)).reshape(1, S, 1024)
```
